# Optimizing a Trainium2 kernel written in Bass

```python
import jax, jax.numpy as jnp
from jax import lax
import numpy as np

D_MODEL = 1024
BATCH = 1
SEQ = 512
DEPTH = 1

CHUNK = 64
N_META = 16
N_PAD = CHUNK - N_META
WINDOW = 128
WINDOW_CHUNKS = WINDOW // CHUNK

ATT_HEAD_DIM = 64
ATT_Q_HEADS = D_MODEL // ATT_HEAD_DIM
ATT_KV_HEADS = ATT_Q_HEADS // 4
ATT_GROUP = ATT_Q_HEADS // ATT_KV_HEADS
ATT_Q = ATT_Q_HEADS * ATT_HEAD_DIM
ATT_KV = ATT_KV_HEADS * ATT_HEAD_DIM

RET_HEADS = 4
RET_HEAD_DIM = D_MODEL // RET_HEADS
RET_W = RET_HEADS * RET_HEAD_DIM
RET_ROPE_BASE = 10000.0

D_FF = 4 * D_MODEL
EPS = 1e-6
NEG = -1e30

SPLITS = (ATT_Q, ATT_KV, ATT_KV, RET_W, RET_W, RET_W, RET_W, D_MODEL, D_MODEL)
SPLIT_OFFSETS = tuple(int(o) for o in np.cumsum(SPLITS)[:-1])
D_IN_PROJ = int(sum(SPLITS))

kernel_name = 'hybrid_swa_sinks_retention_gated_block'

def _rmsnorm(x, w):
    xf = x.astype(jnp.float32)
    y = xf * lax.rsqrt(jnp.mean(xf * xf, axis=-1, keepdims=True) + EPS) * w.astype(jnp.float32)
    return y.astype(x.dtype)

def _shift_chunks(t, s):
    if s == 0:
        return t
    return jnp.concatenate([jnp.zeros_like(t[:, :s]), t[:, :-s]], axis=1)

def _window_attention_with_sinks(q, k, v, sinks):
    b, lp, _ = q.shape
    nc = lp // CHUNK
    qc = q.reshape(b, nc, CHUNK, ATT_KV_HEADS, ATT_GROUP, ATT_HEAD_DIM)
    kc = k.reshape(b, nc, CHUNK, ATT_KV_HEADS, ATT_HEAD_DIM)
    vc = v.reshape(b, nc, CHUNK, ATT_KV_HEADS, ATT_HEAD_DIM)
    kb = jnp.concatenate([_shift_chunks(kc, s) for s in range(WINDOW_CHUNKS - 1, -1, -1)], axis=2)
    vb = jnp.concatenate([_shift_chunks(vc, s) for s in range(WINDOW_CHUNKS - 1, -1, -1)], axis=2)
    k_meta = k[:, N_PAD:CHUNK].reshape(b, N_META, ATT_KV_HEADS, ATT_HEAD_DIM)
    v_meta = v[:, N_PAD:CHUNK].reshape(b, N_META, ATT_KV_HEADS, ATT_HEAD_DIM)
    scale = ATT_HEAD_DIM ** -0.5
    s_band = jnp.einsum('bnqhgd,bnkhd->bnhgqk', qc, kb).astype(jnp.float32) * scale
    s_meta = jnp.einsum('bnqhgd,bkhd->bnhgqk', qc, k_meta).astype(jnp.float32) * scale
    chunk_idx = jnp.arange(nc)
    key_pos = (chunk_idx[:, None] - (WINDOW_CHUNKS - 1)) * CHUNK + jnp.arange(WINDOW_CHUNKS * CHUNK)[None, :]
    band_ok = key_pos >= N_PAD
    meta_ok = chunk_idx >= WINDOW_CHUNKS
    s_band = jnp.where(band_ok[None, :, None, None, None, :], s_band, NEG)
    s_meta = jnp.where(meta_ok[None, :, None, None, None, None], s_meta, NEG)
    sink = sinks.astype(jnp.float32).reshape(ATT_KV_HEADS, ATT_GROUP)[None, None, :, :, None, None]
    m = jnp.maximum(jnp.maximum(s_band.max(-1, keepdims=True), s_meta.max(-1, keepdims=True)), sink)
    p_band = jnp.exp(s_band - m)
    p_meta = jnp.exp(s_meta - m)
    inv_denom = 1.0 / (p_band.sum(-1, keepdims=True) + p_meta.sum(-1, keepdims=True) + jnp.exp(sink - m))
    out = (jnp.einsum('bnhgqk,bnkhd->bnqhgd', (p_band * inv_denom).astype(v.dtype), vb)
           + jnp.einsum('bnhgqk,bkhd->bnqhgd', (p_meta * inv_denom).astype(v.dtype), v_meta))
    return out.reshape(b, lp, ATT_Q)

def _rotary(t, pos):
    half = RET_HEAD_DIM // 2
    inv_freq = RET_ROPE_BASE ** (-jnp.arange(half, dtype=jnp.float32) / half)
    ang = pos.astype(jnp.float32)[:, None] * inv_freq[None, :]
    cos = jnp.cos(ang)[None, :, None, :]
    sin = jnp.sin(ang)[None, :, None, :]
    t1, t2 = t[..., :half], t[..., half:]
    return jnp.concatenate([t1 * cos - t2 * sin, t1 * sin + t2 * cos], axis=-1)

def _retention(q, k, v, g):
    b, lp, _ = q.shape
    nc = lp // CHUNK
    f32 = jnp.float32
    pos = jnp.arange(lp)
    q = q.reshape(b, lp, RET_HEADS, RET_HEAD_DIM).astype(f32)
    k = k.reshape(b, lp, RET_HEADS, RET_HEAD_DIM).astype(f32)
    v = v.reshape(b, lp, RET_HEADS, RET_HEAD_DIM).astype(f32)
    q = _rotary(q, pos) * (RET_HEAD_DIM ** -0.5)
    k = _rotary(k, pos) * (pos >= N_PAD).astype(f32)[None, :, None, None]
    log_gamma = jnp.log(1.0 - 2.0 ** (-5.0 - jnp.arange(RET_HEADS, dtype=f32)))
    i = jnp.arange(CHUNK, dtype=f32)
    decay_intra = jnp.exp(log_gamma[:, None, None] * jnp.abs(i[:, None] - i[None, :]))
    decay_q = jnp.exp(log_gamma[:, None] * (i + 1.0))
    decay_k = jnp.exp(log_gamma[:, None] * (CHUNK - 1.0 - i))
    decay_chunk = jnp.exp(log_gamma * CHUNK)
    qc = q.reshape(b, nc, CHUNK, RET_HEADS, RET_HEAD_DIM)
    kc = k.reshape(b, nc, CHUNK, RET_HEADS, RET_HEAD_DIM)
    vc = v.reshape(b, nc, CHUNK, RET_HEADS, RET_HEAD_DIM)
    scores = jnp.einsum('bnqhd,bnkhd->bnhqk', qc, kc) * decay_intra[None, None]
    o_intra = jnp.einsum('bnhqk,bnkhe->bnqhe', scores, vc)
    kv = jnp.einsum('bnkhd,bnkhe,hk->nbhde', kc, vc, decay_k)

    def step(state, kv_n):
        return decay_chunk[None, :, None, None] * state + kv_n, state

    _, s_prev = lax.scan(step, jnp.zeros((b, RET_HEADS, RET_HEAD_DIM, RET_HEAD_DIM), f32), kv)
    o_cross = jnp.einsum('bnqhd,hq,nbhde->bnqhe', qc, decay_q, s_prev)
    o = (o_intra + o_cross).reshape(b, lp, RET_HEADS, RET_HEAD_DIM)
    o = o * lax.rsqrt(jnp.mean(o * o, axis=-1, keepdims=True) + EPS)
    return (jax.nn.silu(g.astype(f32)) * o.reshape(b, lp, RET_W)).astype(g.dtype)

def setup_inputs(seed: int = 0) -> dict:
    key = jax.random.key(seed)
    ks = jax.random.split(key, 12)
    f32 = jnp.float32
    x = jax.random.normal(ks[0], (BATCH, SEQ, D_MODEL), f32)
    meta_tokens = jax.random.normal(ks[1], (N_META, D_MODEL), f32)
    norm_mix_pre = 1.0 + 0.02 * jax.random.normal(ks[2], (DEPTH, D_MODEL), f32)
    w_in = jax.random.normal(ks[3], (DEPTH, D_MODEL, D_IN_PROJ), f32) * D_MODEL ** -0.5
    attn_sinks = 0.5 * jax.random.normal(ks[4], (DEPTH, ATT_Q_HEADS), f32)
    w_out = jax.random.normal(ks[5], (DEPTH, D_MODEL, D_MODEL), f32) * D_MODEL ** -0.5
    norm_mix_post = 1.0 + 0.02 * jax.random.normal(ks[6], (DEPTH, D_MODEL), f32)
    norm_ffn_pre = 1.0 + 0.02 * jax.random.normal(ks[7], (DEPTH, D_MODEL), f32)
    w_up = jax.random.normal(ks[8], (DEPTH, D_MODEL, D_FF), f32) * D_MODEL ** -0.5
    w_down = jax.random.normal(ks[9], (DEPTH, D_FF, D_MODEL), f32) * D_FF ** -0.5
    norm_ffn_post = 1.0 + 0.02 * jax.random.normal(ks[10], (DEPTH, D_MODEL), f32)
    return {'x': x, 'meta_tokens': meta_tokens, 'norm_mix_pre': norm_mix_pre, 'w_in': w_in,
            'attn_sinks': attn_sinks, 'w_out': w_out, 'norm_mix_post': norm_mix_post,
            'norm_ffn_pre': norm_ffn_pre, 'w_up': w_up, 'w_down': w_down,
            'norm_ffn_post': norm_ffn_post}

def reference(x, meta_tokens, norm_mix_pre, w_in, attn_sinks, w_out, norm_mix_post,
              norm_ffn_pre, w_up, w_down, norm_ffn_post):
    b = x.shape[0]
    pad = jnp.zeros((b, N_PAD, D_MODEL), x.dtype)
    meta = jnp.broadcast_to(meta_tokens.astype(x.dtype)[None], (b, N_META, D_MODEL))
    h = jnp.concatenate([pad, meta, x], axis=1)
    for layer in range(DEPTH):
        a = _rmsnorm(h, norm_mix_pre[layer])
        proj = a @ w_in[layer]
        q_a, k_a, v_a, q_r, k_r, v_r, g_r, gate_a, gate_r = jnp.split(proj, SPLIT_OFFSETS, axis=-1)
        o_a = _window_attention_with_sinks(q_a, k_a, v_a, attn_sinks[layer])
        o_r = _retention(q_r, k_r, v_r, g_r)
        mixed = jax.nn.sigmoid(gate_a) * o_a + jax.nn.sigmoid(gate_r) * o_r
        h = h + _rmsnorm(mixed @ w_out[layer], norm_mix_post[layer])
        f = _rmsnorm(h, norm_ffn_pre[layer])
        f = jnp.square(jax.nn.relu(f @ w_up[layer])) @ w_down[layer]
        h = h + _rmsnorm(f, norm_ffn_post[layer])
    return h[:, CHUNK:]


_drawn_inputs = setup_inputs


def setup_inputs(seed=0):
    import zlib

    import numpy as np

    out = dict(_drawn_inputs(seed))
    spreads = {}
    factors = {'attn_sinks': 8.0, 'norm_mix_post': 3.673, 'norm_ffn_pre': 13.259, 'norm_ffn_post': 18.349}
    for name, (base, spread) in spreads.items():
        noise = np.random.default_rng([zlib.crc32(name.encode()), seed]).standard_normal(out[name].shape)
        drawn = base * np.exp(spread * noise) if base else spread * noise
        out[name] = __import__('jax').numpy.asarray(drawn.astype(out[name].dtype))
    for name, factor in factors.items():
        out[name] = (out[name] * factor).astype(out[name].dtype)
    return out
```

```python
from contextlib import ExitStack

import concourse.bass as bass
from concourse import mybir

F32 = mybir.dt.float32
F32R = mybir.dt.float32r
BF16 = mybir.dt.bfloat16
ACT = mybir.ActivationFunctionType
ALU = mybir.AluOpType
AX_X = mybir.AxisListType.X
ds = bass.ds

P = 128
D = 1024
SEQ = 512
KT = D // P
NT = SEQ // P
CHUNK = 64
META = 16
TOK = SEQ + META
COLS = 512
DFF = 4096
HD = 64
KEYS = CHUNK + P + META
RH = 4
RD = 256
EPS = 1e-6
ATT_SCALE = HD ** -0.5
W_SLOTS = 4
QUADS = 33
H_BACK = 17


def hybrid_block(nc, x, meta_tokens, w_pre, sinks, w_post, w_ffn_pre, w_ffn_post, weights,
                 c_ident, c_cos, c_sin, c_decay, c_mask_q, c_mask_k, out):
    ctx = ExitStack()
    with ctx:
        def sem(name):
            return ctx.enter_context(nc.semaphore(name))

        def keep(name, shape, dt=F32):
            return ctx.enter_context(nc.sbuf_tensor(name, shape, dt))

        raw = keep("raw", [P, 4, 2, COLS])
        w_hi = keep("w_hi", [P, W_SLOTS, COLS], F32R)
        w_lo = keep("w_lo", [P, W_SLOTS, COLS], F32R)
        xt_hi = keep("xt_hi", [P, KT, TOK], F32R)
        xt_lo = keep("xt_lo", [P, KT, TOK], F32R)
        ident = keep("ident", [P, P])
        col_pre = keep("col_pre", [P, KT])
        col_ffn = keep("col_ffn", [P, KT])
        stat = keep("stat", [P, 64])
        neg_half = keep("neg_half", [P, 4])

        mixer = ExitStack()

        def a_buf(name, shape, dt=F32):
            return mixer.enter_context(nc.sbuf_tensor(name, shape, dt))

        o_a = a_buf("o_a", [P, NT, D])
        rq = a_buf("rq", [P, KT, SEQ])
        rk = a_buf("rk", [P, KT, TOK])
        g2 = a_buf("g2", [P, NT, D])
        v_r = a_buf("v_r", [P, NT, D])
        v_rm = a_buf("v_rm", [META, D])
        cos_sin = a_buf("cos_sin", [P, 2, TOK])
        cos, sin = cos_sin[:, 0, :], cos_sin[:, 1, :]
        th = cos_sin[:, :, 0:COLS]
        rope_a, rope_c, rope_b, rope_x = (v_r[:, n, :].rearrange("p (e c) -> p e c", e=2) for n in range(4))
        x_in, meta_in = g2, v_rm

        att = ExitStack()

        def t_buf(name, shape, dt=F32):
            return att.enter_context(nc.sbuf_tensor(name, shape, dt))

        kt_hi = t_buf("kt_hi", [P, 2, NT * KEYS], F32R)
        kt_lo = t_buf("kt_lo", [P, 2, NT * KEYS], F32R)
        qt = t_buf("qt", [P, 4, SEQ])
        v_first = t_buf("v_first", [P, NT, 256])
        v_second = t_buf("v_second", [P, NT, 256])
        qz_hi = [t_buf(f"qz_hi{u}", [P, 4, P], F32R) for u in range(2)]
        qz_lo = [t_buf(f"qz_lo{u}", [P, 4, P], F32R) for u in range(2)]
        prob = t_buf("prob", [P, 4, KEYS])
        pt_first = t_buf("pt_first", [P, 4, P])
        pt_second = t_buf("pt_second", [P, 4, P])
        rope_m = t_buf("rope_m", [P, 4, 2, META])
        mask_q = t_buf("mask_q", [P, P], BF16)
        mask_k = t_buf("mask_k", [P, NT * KEYS], BF16)
        sink = t_buf("sink", [P, 16])
        nsink = t_buf("nsink", [P, 16])
        att.close()

        ret = ExitStack()

        def r_buf(name, shape, dt=F32):
            return ret.enter_context(nc.sbuf_tensor(name, shape, dt))

        decay = r_buf("decay", [P, RH, TOK])
        hk_hi = r_buf("hk_hi", [P, 2, TOK], F32R)
        hk_lo = r_buf("hk_lo", [P, 2, TOK], F32R)
        hq_hi = r_buf("hq_hi", [P, 2, SEQ], F32R)
        hq_lo = r_buf("hq_lo", [P, 2, SEQ], F32R)
        hv_hi = r_buf("hv_hi", [P, NT + 1, RD], F32R)
        hv_lo = r_buf("hv_lo", [P, NT + 1, RD], F32R)
        sc = r_buf("sc", [P, 2, SEQ])
        sc_hi = r_buf("sc_hi", [P, 2, SEQ], F32R)
        sc_lo = r_buf("sc_lo", [P, 2, SEQ], F32R)
        ret_junk = r_buf("ret_junk", [P, RD])
        ret.close()
        mixer.close()

        u_hi = keep("u_hi", [P, 16, SEQ], F32R)
        u_lo = keep("u_lo", [P, 16, SEQ], F32R)
        y = keep("y", [P, NT, D])
        h = keep("h", [P, NT, D])
        row_post = keep("row_post", [P, D])
        row_ffn = keep("row_ffn", [P, D])
        relu = keep("relu", [P, 4, COLS])
        relu2 = keep("relu2", [P, 2, COLS])
        scaled = keep("scaled", [P, 2, D])
        junk = keep("junk", [P, D])

        ps = ctx.enter_context(nc.psum_tensor("ps", [P, 8, COLS], F32))
        M = [ps[:, b, :] for b in range(4)]
        A = [ps[:, 4 + b, :] for b in range(4)]
        S4 = ps[:, 4:6, 0:2 * KEYS].rearrange("p b (m k) -> p b m k", m=2)
        TB = A[2]
        MB = A[3]

        raw_landed = [sem(f"raw_landed{c}") for c in range(4)]
        hi_ready, lo_ready, mm_done = sem("hi_ready"), sem("lo_ready"), sem("mm_done")
        bank_free = [sem(f"bank_free{b}") for b in range(4)]
        x_landed = [sem(f"x_landed{t}") for t in range(NT)]
        meta_landed, const_landed, table_landed = sem("meta_landed"), sem("const_landed"), sem("table_landed")
        decay_landed = sem("decay_landed")
        ms_eps = sem("ms_eps")
        zeroed, masks_ready = sem("zeroed"), sem("masks_ready")
        sq_ready, rstd_ready, normed, turned = sem("sq_ready"), sem("rstd_ready"), sem("normed"), sem("turned")
        meta_scaled, xt_hi_ready, xt_lo_ready = sem("meta_scaled"), sem("xt_hi_ready"), sem("xt_lo_ready")
        kt_hi_done, v_done = sem("kt_hi_done"), sem("v_done")
        rope_parts, rope_slot_free, meta_free = sem("rope_parts"), sem("rope_slot_free"), sem("meta_free")
        qz_hi_ready, qk_done = sem("qz_hi_ready"), sem("qk_done")
        max_ready, bias_ready, sink_ready, exp_done = sem("max_ready"), sem("bias_ready"), sem("sink_ready"), sem("exp_done")
        den_ready, rden_ready = sem("den_ready"), sem("rden_ready")
        p_turned, pt_pair0_ready, pt_pair1_ready = sem("p_turned"), sem("pt_pair0_ready"), sem("pt_pair1_ready")
        pv_done, att_out = sem("pv_done"), sem("att_out")
        hk_hi_ready, hq_hi_ready, hv_hi_ready = sem("hk_hi_ready"), sem("hq_hi_ready"), sem("hv_hi_ready")
        hq_lo_ready, hv_lo_ready = sem("hq_lo_ready"), sem("hv_lo_ready")
        r_gated, qz_lo_ready = sem("r_gated"), sem("qz_lo_ready")
        rs_done, sc_ready, sc_hi_ready, sc_lo_ready = sem("rs_done"), sem("sc_ready"), sem("sc_hi_ready"), sem("sc_lo_ready")
        ro_done, ro_sq, ro_rstd, ro_scaled = sem("ro_done"), sem("ro_sq"), sem("ro_rstd"), sem("ro_scaled")
        th_ready, gated, mixed_done = sem("th_ready"), sem("gated"), sem("mixed_done")
        mix_turned, mix_hi, mix_lo = sem("mix_turned"), sem("mix_hi"), sem("mix_lo")
        y_sq, y_sum, y_rstd, y_scaled, h_done = sem("y_sq"), sem("y_sum"), sem("y_rstd"), sem("y_scaled"), sem("h_done")
        h_sq, h_rstd, f_normed, f_turned = sem("h_sq"), sem("h_rstd"), sem("f_normed"), sem("f_turned")
        ft_hi, ft_lo = sem("ft_hi"), sem("ft_lo")
        relu_ready, sq_hi_ready, sq_full, u_done = sem("relu_ready"), sem("sq_hi_ready"), sem("sq_full"), sem("u_done")
        x_back, rows_landed = sem("x_back"), sem("rows_landed")
        y_done, o_sq, o_rstd, o_scaled, o_ready, stored = (sem(n) for n in (
            "y_done", "o_sq", "o_rstd", "o_scaled", "o_ready", "stored"))

        start_junk = [rq[:, 2 * t:2 * t + 2, :].rearrange("p a b -> p (a b)") for t in range(NT)]
        mask_f = o_a[0:2, 3, 0:P + NT * KEYS]
        m_scaled = o_a[:, 1, 0:KT * META].rearrange("p (k n) -> p k n", k=KT)

        def kt_views(kt, f):
            v = kt[:, f, :].rearrange("p (t k) -> p t k", k=KEYS)
            return v[:, :, CHUNK:CHUNK + P], v[:, 1:NT, 0:CHUNK], v[:, :, CHUNK + P:KEYS]

        def score_shape(n):
            return (META, SEQ) if n == 0 else (P, SEQ - P * (n - 1))

        def f32(ap):
            return ap.bitcast(F32)

        x_v = x[0].rearrange("(t p) d -> t p d", p=P)
        out_v = out[0].rearrange("(t p) d -> t p d", p=P)

        block = ctx.enter_context(nc.Block())

        @block.sync
        def _(sp):
            def load(q, c):
                sp.dma_start(raw[:, c], weights[q, c] if isinstance(q, int) else weights[ds(q, 1), c].squeeze(0)).then_inc(raw_landed[c], 16)

            def reload(q, c):
                sp.wait_ge(lo_ready, 8 * (q - 1) + 2 * c + 2)
                load(q, c)

            sp.dma_start(meta_in[:], meta_tokens).then_inc(meta_landed, 16)
            for t in range(NT):
                sp.dma_start(x_in[:, t, :], x_v[t]).then_inc(x_landed[t], 16)
            for c in range(4):
                load(0, c)
            with sp.Fori(1, H_BACK) as q:
                for c in range(4):
                    reload(q, c)
            sp.wait_ge(mix_lo, KT)
            sp.dma_start(h[:], x[0].rearrange("(t p) d -> p t d", p=P)).then_inc(x_back, 16)
            with sp.Fori(H_BACK, QUADS) as q:
                for c in range(4):
                    reload(q, c)
            for t in range(NT):
                sp.wait_ge(o_ready, t + 1)
                sp.dma_start(out_v[t], y[:, t, :]).then_inc(stored, 16)
            sp.wait_ge(stored, 16 * NT)

        @block.gpsimd
        def _(pool):
            pool.dma_start(ident[:], c_ident).then_inc(const_landed, 16)
            with nc.allow_non_contiguous_dma(reason="norm weights as columns"):
                pool.dma_start(col_pre[:], w_pre[0].rearrange("(k p) -> p k", p=P)).then_inc(const_landed, 16)
                pool.dma_start(col_ffn[:], w_ffn_pre[0].rearrange("(k p) -> p k", p=P)).then_inc(const_landed, 16)
            pool.dma_start(mask_f[:, 0:P], c_mask_q).then_inc(table_landed, 16)
            pool.dma_start(mask_f[:, P:P + NT * KEYS], c_mask_k).then_inc(table_landed, 16)
            pool.dma_start(sink[:], sinks[0].partition_broadcast(P)).then_inc(table_landed, 16)
            pool.dma_start(cos, c_cos).then_inc(table_landed, 16)
            pool.dma_start(sin, c_sin).then_inc(table_landed, 16)
            for kt in (kt_hi, kt_lo):
                for f in range(2):
                    nc.gpsimd.memset(f32(kt[:, f, 0:CHUNK]), 0.0)
            for qz in (*qz_hi, *qz_lo):
                nc.gpsimd.memset(f32(qz[:]), 0.0)
            nc.gpsimd.memset(mask_q[:], 0.0)
            nc.gpsimd.memset(mask_k[:], 0.0)
            nc.gpsimd.memset(v_first[:, 0, :], 0.0).then_inc(zeroed, 1)
            nc.gpsimd.memset(neg_half[:], -0.5).then_inc(rope_slot_free, 1)
            nc.gpsimd.memset(stat[:, 62:63], 0.0).then_inc(rope_slot_free, 1)
            nc.gpsimd.memset(stat[:, 63:64], 0.0).then_inc(meta_free, 1)

            def rsqrt(dst, src, eps, done):
                rows, cols = src.shape
                nc.gpsimd.tensor_scalar(dst, src, eps, None, ALU.add).then_inc(ms_eps, 1)
                pool.wait_ge(ms_eps, done + 1)
                return nc.gpsimd.tensor_tensor(dst, dst, neg_half[0:rows, 0:cols], ALU.pow)

            pool.wait_ge(sq_ready, 1)
            rsqrt(stat[0:META, 5:6], stat[0:META, 4:5], EPS, 0).then_inc(rstd_ready, 1)
            for t in range(NT):
                pool.wait_ge(sq_ready, t + 2)
                rsqrt(stat[:, 8 + t:9 + t], stat[:, t:t + 1], EPS, 1 + t).then_inc(rstd_ready, 1)

            def rotate(i, first_tile, dst, n0):
                for e in range(2):
                    pool.wait_ge(rope_parts, 2 * i + n0 + e + 1)
                    lo_t = dst[:, ds(4 * i + 2 * e, 1), 0:SEQ].squeeze(1)
                    hi_t = dst[:, ds(4 * i + 2 * e + 1, 1), 0:SEQ].squeeze(1)
                    nc.gpsimd.tensor_tensor(lo_t, rope_a[:, e], rope_b[:, e], ALU.subtract)
                    nc.gpsimd.tensor_tensor(hi_t, rope_c[:, e], rope_x[:, e], ALU.add).then_inc(rope_slot_free, 1)

            with pool.Fori(0, 2) as i:
                rotate(i, 0, rq, 0)
            with pool.Fori(0, 2) as i:
                rotate(i, 0, rk, 4)
            pool.wait_ge(qk_done, 16)
            pool.dma_start(decay[:], c_decay).then_inc(decay_landed, 16)
            for hd in range(RH):
                pool.wait_ge(ro_sq, 4 * hd + 4)
                rsqrt(stat[:, 36:40], stat[:, 32:36], 4 * EPS, hd + 5).then_inc(ro_rstd, 1)
            pool.wait_ge(mix_lo, KT)
            pool.dma_start(row_post[:], w_post[0].partition_broadcast(P)).then_inc(rows_landed, 16)
            pool.dma_start(row_ffn[:], w_ffn_post[0].partition_broadcast(P)).then_inc(rows_landed, 16)
            for t in range(NT + 1):
                if t < NT:
                    pool.wait_ge(y_sq, 4 + t + 1)
                    nc.gpsimd.tensor_tensor(stat[:, 8 + t:9 + t], stat[:, t:t + 1], stat[:, 4 + t:5 + t], ALU.add).then_inc(y_sum, 1)
                    pool.wait_ge(y_sum, t + 1)
                    rsqrt(stat[:, 12 + t:13 + t], stat[:, 8 + t:9 + t], EPS, 9 + max(0, 2 * t - 1)).then_inc(y_rstd, 1)
                if t > 0:
                    pool.wait_ge(h_sq, t)
                    rsqrt(stat[:, 19 + t:20 + t], stat[:, 15 + t:16 + t], EPS, 9 + min(2 * t, 7)).then_inc(h_rstd, 1)
            for t in range(NT):
                pool.wait_ge(o_sq, t + 1)
                rsqrt(stat[:, 12 + t:13 + t], stat[:, 8 + t:9 + t], EPS, 17 + t).then_inc(o_rstd, 1)

        @block.scalar
        def _(act):
            def split(q, k):
                if k >= KT:
                    q, k = q + 1, k - KT
                s = 8 * q + k
                if k % 2 == 0:
                    act.wait_ge(raw_landed[k // 2], 16 * q + 16)
                if not (isinstance(s, int) and s < W_SLOTS):
                    act.wait_ge(mm_done, 4 * (s - W_SLOTS + 1))
                nc.scalar.activation(w_hi[:, k % W_SLOTS, :], raw[:, k // 2, k % 2, :], ACT.Copy).then_inc(hi_ready, 1)

            def quad(q, aux=None, evac=None, after=None, last=False):
                for k in range(KT):
                    if not (last and k + 3 >= KT):
                        split(q, k + 3)
                    for do in (aux or {}).get(k, ()):
                        do()
                for b in range(4 if evac else 0):
                    act.wait_ge(mm_done, 4 * (8 * q + 7) + b + 1)
                    evac(b)
                for do in after or ():
                    do()

            def bank_copy(banks, dst):
                def evac(b):
                    if b in banks:
                        nc.scalar.activation(dst(b), M[b], ACT.Copy).then_inc(bank_free[b], 1)
                return evac

            act.wait_ge(meta_landed, 16)
            nc.scalar.activation(o_a[0:META, 2, :], meta_in[:], ACT.Square, scale=1 / 32, accum_out=stat[0:META, 4:5]).then_inc(sq_ready, 1)
            for t in range(NT):
                act.wait_ge(x_landed[t], 16)
                nc.scalar.activation(start_junk[t], x_in[:, t, :], ACT.Square, scale=1 / 32,
                                     accum_out=stat[:, t:t + 1]).then_inc(sq_ready, 1)
            for k in range(3):
                split(0, k)
            act.wait_ge(meta_scaled, 1)
            nc.scalar.activation(xt_hi[:, :, SEQ:TOK], m_scaled, ACT.Copy).then_inc(xt_hi_ready, 1)
            for f in range(KT):
                act.wait_ge(turned, 1 + 3 + f + 1)
                nc.scalar.activation(xt_hi[:, f, 0:SEQ], ps[:, f, :], ACT.Copy,
                                     scale=col_pre[:, f:f + 1]).then_inc(xt_hi_ready, 1)
            act.wait_ge(table_landed, 16 * 5)
            act.wait_ge(zeroed, 1)
            nc.scalar.activation(mask_q[0:2, :], mask_f[:, 0:P], ACT.Copy)
            nc.scalar.activation(mask_k[0:2, :], mask_f[:, P:P + NT * KEYS], ACT.Copy)
            nc.scalar.mul(nsink[:], sink[:], -1.0).then_inc(masks_ready, 1)

            def kv_evac(b):
                if b < 2:
                    own, prev, met = kt_views(kt_hi, b)
                    nc.scalar.activation(own, M[b].rearrange("p (t n) -> p t n", t=NT), ACT.Copy)
                    nc.scalar.activation(prev, M[b][:, CHUNK:CHUNK + 3 * P].rearrange("p (t n) -> p t n", t=3)[:, :, 0:CHUNK], ACT.Copy)
                    if b == 1:
                        act.wait_ge(mm_done, 4 * 8)
                        for f in range(2):
                            nc.scalar.activation(kt_views(kt_hi, f)[2], A[1][:, f * META:(f + 1) * META].unsqueeze(1)
                                                 .to_broadcast([P, NT, META]), ACT.Copy).then_inc(kt_hi_done, 1)
                if b == 2:
                    nc.scalar.activation(v_first[CHUNK:P, 0, :], M[2][0:CHUNK, 0:256], ACT.Copy)
                    nc.scalar.activation(v_first[:, 1, :], M[2][:, 256:512], ACT.Copy).then_inc(v_done, 1)
                if b == 3:
                    nc.scalar.activation(v_first[:, 2, :], M[3][:, 0:256], ACT.Copy)
                    nc.scalar.activation(v_first[:, 3, :], M[3][:, 256:512], ACT.Copy).then_inc(v_done, 1)

            quad(0, evac=kv_evac)

            def q_evac():
                return bank_copy((0, 1, 2, 3), lambda b: qt[:, b, :])

            quad(1, evac=q_evac())
            act.wait_ge(bank_free[3], 1 + 1)

            def stage_q(t, u):
                rows = slice(64 * u, 64 * u + 64)

                def do():
                    nc.scalar.activation(qz_hi[u][rows], qt[rows, :, ds(P * t, P)], ACT.Copy).then_inc(qz_hi_ready, 1)
                return do

            def exps(unit):
                def do():
                    act.wait_ge(bias_ready, unit + 1)
                    for m in range(4):
                        nc.scalar.activation(prob[:, m, :], S4[:, m // 2, m % 2, :], ACT.Exp, bias=stat[:, 12 + m:13 + m],
                                             scale=ATT_SCALE, accum_out=stat[:, 20 + m:21 + m])
                    act.wait_ge(sink_ready, unit + 1)
                    nc.scalar.activation(stat[:, 24:28], stat[:, 16:20], ACT.Exp).then_inc(exp_done, 1)
                return do

            def copy_pair(unit, pair, done):
                heads = slice(2 * pair, 2 * pair + 2)

                def do():
                    act.wait_ge(p_turned, 2 * unit + pair + 1)
                    nc.scalar.activation(pt_first[:, heads, :], TB[:, 0:256].rearrange("p (m q) -> p m q", m=2), ACT.Copy)
                    nc.scalar.activation(pt_second[0:KEYS - P, heads, :], TB[0:KEYS - P, 256:512].rearrange("p (m q) -> p m q", m=2),
                                         ACT.Copy).then_inc(done, 1)
                return do

            def attention(t, unit0):
                return {0: (stage_q(t, 0), stage_q(t, 1)), 2: (exps(unit0),), 4: (copy_pair(unit0, 0, pt_pair0_ready),),
                        5: (exps(unit0 + 1),),
                        7: (copy_pair(unit0 + 1, 0, pt_pair0_ready), copy_pair(unit0 + 1, 1, pt_pair1_ready))}

            def rope_evac(i, n0):
                def evac(b):
                    if b % 2:
                        act.wait_ge(rope_slot_free, 2 * i + n0 + b // 2 + 1)
                        nc.scalar.activation(rope_x[:, b // 2], M[b], ACT.Copy).then_inc(bank_free[b], 1)
                return evac

            with act.Fori(0, 2) as i:
                aux = attention(i, 2 * i)
                quad(i + 2, aux, rope_evac(i, 0))
            with act.Fori(0, 2) as i:
                aux = attention(i + 2, 2 * i + 4)
                quad(i + 4, aux, rope_evac(i, 4))
            quad(6, evac=q_evac())
            act.wait_ge(bank_free[3], 6 + 1)

            with act.Fori(0, 2) as i:
                aux = attention(i, 2 * i + 8)
                quad(i + 7, aux, bank_copy((1, 3), lambda b: v_r[:, b, ds(i * COLS, COLS)]))

            def tanh_evac(free, n0, i):
                def evac(b):
                    if b >= 2:
                        if free:
                            act.wait_ge(gated, 4 * i + n0 + b - 1)
                        else:
                            act.wait_ge(bank_free[b - 2], i + 9 + 1)
                    nc.scalar.activation(th[:, b % 2, :], M[b], ACT.Tanh, scale=0.5).then_inc(bank_free[b] if free else th_ready, 1)
                return evac

            with act.Fori(0, 2) as i:
                aux = attention(i + 2, 2 * i + 12)
                quad(i + 9, aux, tanh_evac(False, 0, i))

            act.wait_ge(rope_slot_free, 2 + 8)

            def stage_kq(hd):
                def do():
                    nc.scalar.activation(hk_hi[:], rk[:, ds(2 * hd, 2), :], ACT.Copy).then_inc(hk_hi_ready, 1)
                    nc.scalar.activation(hq_hi[:], rq[:, ds(2 * hd, 2), :], ACT.Copy).then_inc(hq_hi_ready, 1)
                return do

            def stage_v(hd):
                def do():
                    nc.scalar.activation(hv_hi[:, 0:NT, :], v_r[:, :, ds(RD * hd, RD)], ACT.Copy)
                    nc.scalar.activation(hv_hi[0:META, NT, :], v_rm[:, ds(RD * hd, RD)], ACT.Copy).then_inc(hv_hi_ready, 1)
                return do

            def score_hi(hd, n):
                rows, cols = score_shape(n)

                def do():
                    act.wait_ge(sc_ready, 5 * hd + n + 1)
                    nc.scalar.activation(sc_hi[0:rows, n % 2, 0:cols], sc[0:rows, n % 2, 0:cols], ACT.Copy).then_inc(sc_hi_ready, 1)
                return do

            def ret_squares(hd):
                def do():
                    act.wait_ge(ro_done, hd + 1)
                    for j in range(NT):
                        if j:
                            act.wait_ge(ro_sq, 4 * hd + j)
                        nc.scalar.activation(ret_junk[:], A[2 + j // 2][:, (j % 2) * RD:(j % 2 + 1) * RD], ACT.Square,
                                             scale=1 / 8, accum_out=stat[:, 32 + j:33 + j]).then_inc(ro_sq, 1)
                return do

            def retention(hd):
                return {0: (stage_kq(hd),), 1: (stage_v(hd),), 2: (score_hi(hd, 0), score_hi(hd, 1)), 4: (score_hi(hd, 2),),
                        5: (score_hi(hd, 3),), 6: (score_hi(hd, 4),), 7: (ret_squares(hd),)}

            with act.Fori(0, 2) as i:
                quad(i + 11, retention(i), tanh_evac(True, 0, i))
            quad(13, retention(2), tanh_evac(True, 8, 0))

            def mix_part(f):
                def do():
                    act.wait_ge(mix_turned, f + 1)
                    nc.scalar.activation(xt_hi[:, f, 0:SEQ], A[f % 4], ACT.Copy, scale=0.5).then_inc(mix_hi, 1)
                return do

            last_gate = tanh_evac(True, 12, 0)

            def gate_and_mix(b):
                last_gate(b)
                if b:
                    mix_part(b - 1)()

            quad(14, retention(3), gate_and_mix, (mix_part(3),))

            def y_evac(cg):
                def evac(b):
                    nc.scalar.activation(relu[:, b], M[b], ACT.Square, scale=1 / 32,
                                         accum_out=stat[:, 4 * cg + b:4 * cg + b + 1]).then_inc(y_sq, 1)
                return evac

            quad(15, {k: (mix_part(4 + k),) for k in range(4)}, y_evac(0))
            quad(16, None, y_evac(1))

            for t in range(NT):
                act.wait_ge(h_done, t + 1)
                if t:
                    act.wait_ge(h_sq, t)
                nc.scalar.activation(junk[:], h[:, t, :], ACT.Square, scale=1 / 32,
                                     accum_out=stat[:, 16 + t:17 + t]).then_inc(h_sq, 1)
            for f in range(KT):
                act.wait_ge(f_turned, NT - 1 + f + 1)
                nc.scalar.activation(xt_hi[:, f, 0:SEQ], ps[:, f, :], ACT.Copy, scale=col_ffn[:, f:f + 1]).then_inc(ft_hi, 1)

            def up_evac(i, half):
                def evac(b):
                    nc.scalar.activation(relu[:, b, :], M[b], ACT.Relu).then_inc(bank_free[b], 1)
                    if b == 3:
                        for n in range(4):
                            act.wait_ge(bank_free[n], i + (17 + 6 * half) + 1)
                            nc.scalar.activation(u_hi[:, ds(4 * i + n, 1), :].squeeze(1), relu[:, n, :],
                                                 ACT.Square).then_inc(sq_hi_ready, 1)
                return evac

            for half in range(2):
                q0 = 17 + 8 * half
                with act.Fori(0, 4) as i:
                    quad(i + q0, None, up_evac(i, half))
                for r in range(4):
                    quad(q0 + 4 + r, last=(half == 1 and r == 3))
            for t in range(NT):
                act.wait_ge(y_done, t + 1)
                if t:
                    act.wait_ge(o_sq, t)
                nc.scalar.activation(junk[:], y[:, t, :], ACT.Square, scale=1 / 32,
                                     accum_out=stat[:, 8 + t:9 + t]).then_inc(o_sq, 1)

        @block.vector
        def _(dve):
            def split(q, k):
                if k >= KT:
                    q, k = q + 1, k - KT
                dve.wait_ge(hi_ready, 8 * q + k + 1)
                nc.vector.tensor_tensor(w_lo[:, k % W_SLOTS, :], raw[:, k // 2, k % 2, :], f32(w_hi[:, k % W_SLOTS, :]),
                                        ALU.subtract).then_inc(lo_ready, 1)

            def quad(q, aux=None, evac=None, after=None, last=False):
                for k in range(KT):
                    if not (last and k + 3 >= KT):
                        split(q, k + 3)
                    for do in (aux or {}).get(k, ()):
                        do()
                for b in range(4 if evac else 0):
                    dve.wait_ge(mm_done, 4 * (8 * q + 7) + b + 1)
                    evac(b)
                for do in after or ():
                    do()

            def sub_hi(lo, hi, src, scale):
                return nc.vector.scalar_tensor_tensor(out=lo, in0=src, scalar=scale, in1=f32(hi), op0=ALU.mult, op1=ALU.subtract)

            dve.wait_ge(rstd_ready, 1)
            nc.vector.tensor_scalar(meta_in[:], meta_in[:], stat[0:META, 5:6], None, ALU.mult).then_inc(normed, 1)
            for t in range(NT):
                dve.wait_ge(rstd_ready, t + 2)
                nc.vector.tensor_scalar(x_in[:, t, :], x_in[:, t, :], stat[:, 8 + t:9 + t], None, ALU.mult).then_inc(normed, 1)
                if t == 0:
                    dve.wait_ge(turned, 1)
                    dve.wait_ge(const_landed, 16 * 3)
                    nc.vector.tensor_tensor(m_scaled, A[3][:, 0:KT * META].rearrange("p (k n) -> p k n", k=KT),
                                            col_pre[:].unsqueeze(2).to_broadcast([P, KT, META]), ALU.mult).then_inc(meta_scaled, 1)
            for k in range(3):
                split(0, k)
            dve.wait_ge(xt_hi_ready, 1)
            nc.vector.tensor_tensor(xt_lo[:, :, SEQ:TOK], m_scaled, f32(xt_hi[:, :, SEQ:TOK]), ALU.subtract)
            for f in range(KT):
                dve.wait_ge(xt_hi_ready, f + 2)
                sub_hi(xt_lo[:, f, 0:SEQ], xt_hi[:, f, 0:SEQ], ps[:, f, :], col_pre[:, f:f + 1]).then_inc(xt_lo_ready, 1)
            dve.wait_ge(masks_ready, 1)

            def kv_evac(b):
                if b < 2:
                    dve.wait_ge(kt_hi_done, 2)
                    own, prev, met = kt_views(kt_lo, b)
                    own_hi, prev_hi, met_hi = kt_views(kt_hi, b)
                    nc.vector.tensor_tensor(met, A[1][:, b * META:(b + 1) * META].unsqueeze(1).to_broadcast([P, NT, META]),
                                            f32(met_hi), ALU.subtract)
                    nc.vector.tensor_tensor(own, M[b].rearrange("p (t n) -> p t n", t=NT), f32(own_hi), ALU.subtract)
                    nc.vector.tensor_tensor(prev, M[b][:, CHUNK:CHUNK + 3 * P].rearrange("p (t n) -> p t n", t=3)[:, :, 0:CHUNK],
                                            f32(prev_hi), ALU.subtract).then_inc(bank_free[b], 1)
                if b >= 2:
                    dve.wait_ge(v_done, b - 1)
                if b == 2:
                    nc.vector.tensor_copy(v_second[0:CHUNK, 0, :], M[2][0:CHUNK, 256:512])
                if b == 3:
                    nc.vector.tensor_copy(v_second[0:CHUNK, 1, :], M[3][0:CHUNK, 0:256])
                    nc.vector.tensor_copy(v_second[0:CHUNK, 2, :], M[3][0:CHUNK, 256:512])
                    nc.vector.tensor_copy(v_second[0:CHUNK, 3, :], A[0][0:CHUNK, 0:256]).then_inc(bank_free[2], 1)
                    nc.vector.tensor_copy(v_second[CHUNK:CHUNK + META, :, :], A[0][CHUNK:CHUNK + META, 0:256].unsqueeze(1)
                                          .to_broadcast([META, NT, 256])).then_inc(bank_free[3], 1)

            quad(0, evac=kv_evac)
            quad(1)

            def stage_q(t, u, unit):
                rows = slice(64 * u, 64 * u + 64)

                def do():
                    dve.wait_ge(qz_hi_ready, unit + 1)
                    nc.vector.tensor_tensor(qz_lo[u][rows], qt[rows, :, ds(P * t, P)], f32(qz_hi[u][rows]), ALU.subtract).then_inc(qz_lo_ready, 1)
                return do

            def softmax_max(unit, g):
                def do():
                    dve.wait_ge(qk_done, unit + 1)
                    nc.vector.tensor_reduce(stat[:, 8:12].rearrange("p (b m) -> p b m", b=2), S4, AX_X, ALU.max).then_inc(max_ready, 1)
                    dve.wait_ge(max_ready, unit + 1)
                    nc.vector.scalar_tensor_tensor(out=stat[:, 12:16], in0=stat[:, 8:12], scalar=-ATT_SCALE,
                                                   in1=nsink[:, 4 * g:4 * g + 4], op0=ALU.mult, op1=ALU.min).then_inc(bias_ready, 1)
                    dve.wait_ge(bias_ready, unit + 1)
                    nc.vector.tensor_tensor(stat[:, 16:20], sink[:, 4 * g:4 * g + 4], stat[:, 12:16], ALU.add).then_inc(sink_ready, 1)
                return do

            def denominator(unit):
                def do():
                    dve.wait_ge(exp_done, unit + 1)
                    nc.vector.tensor_tensor(stat[:, 28:32], stat[:, 20:24], stat[:, 24:28], ALU.add).then_inc(den_ready, 1)
                    dve.wait_ge(den_ready, unit + 1)
                    nc.vector.reciprocal(stat[:, 52:56], stat[:, 28:32]).then_inc(rden_ready, 1)
                return do

            def copy_pair(unit):
                def do():
                    dve.wait_ge(p_turned, 2 * unit + 2)
                    nc.vector.tensor_copy(pt_first[:, 2:4, :], TB[:, 0:256].rearrange("p (m q) -> p m q", m=2))
                    nc.vector.tensor_copy(pt_second[0:KEYS - P, 2:4, :],
                                          TB[0:KEYS - P, 256:512].rearrange("p (m q) -> p m q", m=2)).then_inc(pt_pair1_ready, 1)
                return do

            def attention_out(t, unit, g):
                def do():
                    dve.wait_ge(pv_done, unit + 1)
                    dve.wait_ge(rden_ready, unit + 1)
                    nc.vector.tensor_tensor(o_a[:, ds(t, 1), 256 * g:256 * g + 256].squeeze(1).rearrange("p (m d) -> p m d", m=4),
                                            TB[:, 0:256].rearrange("p (m d) -> p m d", m=4),
                                            stat[:, 52:56].unsqueeze(2).to_broadcast([P, 4, HD]), ALU.mult).then_inc(att_out, 1)
                return do

            def attention(t, unit0, g0):
                a, b = unit0, unit0 + 1
                return ({0: (stage_q(t, 0, a), stage_q(t, 1, b)), 2: (softmax_max(a, g0),), 3: (denominator(a),),
                         5: (copy_pair(a), softmax_max(b, g0 + 1)), 6: (attention_out(t, a, g0),), 7: (denominator(b),)},
                        (attention_out(t, b, g0 + 1),))

            def rope_evac(i, n0, q0):
                def evac(b):
                    e = b // 2
                    if b % 2 == 0:
                        dve.wait_ge(rope_slot_free, 2 * i + n0 + e + 1)
                        nc.vector.tensor_tensor(rope_a[:, e], M[b], cos[:, 0:SEQ], ALU.mult)
                        nc.vector.tensor_tensor(rope_c[:, e], M[b], sin[:, 0:SEQ], ALU.mult).then_inc(bank_free[b], 1)
                    if b == 2 and n0 == 4:
                        dve.wait_ge(mm_done, 4 * (8 * (i + q0) + 8))
                        mt = MB[:, 0:4 * META].rearrange("p (e two n) -> p two e n", e=2, two=2)
                        cm, sm = (c[:, SEQ:TOK].unsqueeze(1).to_broadcast([P, 2, META]) for c in (cos, sin))
                        for n, (half, w) in enumerate(((0, cm), (0, sm), (1, sm), (1, cm))):
                            ins = nc.vector.tensor_tensor(rope_m[:, n], mt[:, half], w, ALU.mult)
                        ins.then_inc(meta_free, 1)
                    if b == 3:
                        for e in range(2):
                            dve.wait_ge(bank_free[2 * e + 1], i + q0 + 1)
                            nc.vector.tensor_tensor(rope_b[:, e], rope_x[:, e], sin[:, 0:SEQ], ALU.mult)
                            nc.vector.tensor_tensor(rope_x[:, e], rope_x[:, e], cos[:, 0:SEQ], ALU.mult).then_inc(rope_parts, 1)
                        if n0 == 4:
                            dve.wait_ge(meta_free, i + 1 + 1)
                            rk_m = rk[:, ds(4 * i, 4), SEQ:TOK].rearrange("p (e two) n -> p two e n", two=2)
                            nc.vector.tensor_tensor(rk_m[:, 0], rope_m[:, 0], rope_m[:, 2], ALU.subtract)
                            nc.vector.tensor_tensor(rk_m[:, 1], rope_m[:, 1], rope_m[:, 3], ALU.add)
                return evac

            with dve.Fori(0, 2) as i:
                aux, after = attention(i, 2 * i, 0)
                quad(i + 2, aux, rope_evac(i, 0, 2), after)
            with dve.Fori(0, 2) as i:
                aux, after = attention(i + 2, 2 * i + 4, 0)
                quad(i + 4, aux, rope_evac(i, 4, 4), after)
            quad(6)
            dve.wait_ge(rope_slot_free, 2 + 8)

            def v_evac(i):
                def evac(b):
                    if b % 2 == 0:
                        nc.vector.tensor_copy(v_r[:, b, ds(i * COLS, COLS)], M[b]).then_inc(bank_free[b], 1)
                    if b == 2:
                        dve.wait_ge(mm_done, 4 * (8 * (i + 7) + 8))
                        nc.vector.tensor_copy(v_rm[:, ds(i * COLS, COLS)], MB[0:META, :]).then_inc(meta_free, 1)
                return evac

            with dve.Fori(0, 2) as i:
                aux, after = attention(i, 2 * i + 8, 2)
                quad(i + 7, aux, v_evac(i), after)

            def silu_evac(i):
                def evac(b):
                    dve.wait_ge(th_ready, 4 * i + b + 1)
                    nc.vector.scalar_tensor_tensor(out=g2[:, b, ds(i * COLS, COLS)], in0=th[:, b % 2, :], scalar=1.0, in1=M[b],
                                                   op0=ALU.add, op1=ALU.mult).then_inc(bank_free[b], 1)
                return evac

            with dve.Fori(0, 2) as i:
                aux, after = attention(i + 2, 2 * i + 12, 2)
                quad(i + 9, aux, silu_evac(i), after)

            def stage_k(hd):
                def do():
                    dve.wait_ge(hk_hi_ready, hd + 1)
                    nc.vector.tensor_tensor(hk_lo[:], rk[:, ds(2 * hd, 2), :], f32(hk_hi[:]), ALU.subtract)
                    dve.wait_ge(hq_hi_ready, hd + 1)
                    nc.vector.tensor_tensor(hq_lo[:], rq[:, ds(2 * hd, 2), :], f32(hq_hi[:]), ALU.subtract).then_inc(hq_lo_ready, 1)
                return do

            def stage_v(hd):
                def do():
                    dve.wait_ge(hv_hi_ready, hd + 1)
                    nc.vector.tensor_tensor(hv_lo[:, 0:NT, :], v_r[:, :, ds(RD * hd, RD)], f32(hv_hi[:, 0:NT, :]), ALU.subtract)
                    nc.vector.tensor_tensor(hv_lo[0:META, NT, :], v_rm[:, ds(RD * hd, RD)], f32(hv_hi[0:META, NT, :]),
                                            ALU.subtract).then_inc(hv_lo_ready, 1)
                return do

            def decay_scores(hd, n):
                rows, cols = score_shape(n)
                first = META if n == 0 else 0

                def do():
                    dve.wait_ge(rs_done, 5 * hd + n + 1)
                    nc.vector.tensor_tensor(sc[0:rows, n % 2, 0:cols], A[n % 2][0:rows, 0:cols],
                                            decay[0:rows, ds(hd, 1), first:first + cols].squeeze(1), ALU.mult).then_inc(sc_ready, 1)
                return do

            def score_lo(hd, n):
                rows, cols = score_shape(n)

                def do():
                    dve.wait_ge(sc_hi_ready, 5 * hd + n + 1)
                    nc.vector.tensor_tensor(sc_lo[0:rows, n % 2, 0:cols], sc[0:rows, n % 2, 0:cols],
                                            f32(sc_hi[0:rows, n % 2, 0:cols]), ALU.subtract).then_inc(sc_lo_ready, 1)
                return do

            def retention_out(hd):
                def do():
                    dve.wait_ge(ro_rstd, hd + 1)
                    for j in range(NT):
                        part = g2[:, j, ds(RD * hd, RD)]
                        nc.vector.scalar_tensor_tensor(out=part, in0=A[2 + j // 2][:, (j % 2) * RD:(j % 2 + 1) * RD],
                                                       scalar=stat[:, 36 + j:37 + j], in1=part, op0=ALU.mult,
                                                       op1=ALU.mult).then_inc(ro_scaled, 1)
                return do

            def retention(hd):
                return {0: (stage_k(hd),), 1: (stage_v(hd),),
                        2: (decay_scores(hd, 0), decay_scores(hd, 1), score_lo(hd, 0), score_lo(hd, 1)),
                        4: (decay_scores(hd, 2), score_lo(hd, 2)), 5: (decay_scores(hd, 3), score_lo(hd, 3)),
                        6: (decay_scores(hd, 4), score_lo(hd, 4)), 7: (retention_out(hd),)}

            def gate_a_evac(i):
                def evac(b):
                    dve.wait_ge(bank_free[b], i + 11 + 1)
                    part = o_a[:, b, ds(i * COLS, COLS)]
                    nc.vector.scalar_tensor_tensor(out=part, in0=th[:, b % 2, :], scalar=1.0, in1=part, op0=ALU.add,
                                                   op1=ALU.mult).then_inc(gated, 1)
                return evac

            def gate_r_evac(i):
                def evac(b):
                    dve.wait_ge(bank_free[b], i + 13 + 1)
                    cols = slice(i * COLS, (i + 1) * COLS)
                    nc.vector.scalar_tensor_tensor(out=th[:, b % 2, :], in0=th[:, b % 2, :], scalar=1.0, in1=g2[:, b, cols],
                                                   op0=ALU.add, op1=ALU.mult).then_inc(r_gated, 1)
                    dve.wait_ge(r_gated, 4 * i + b + 1)
                    nc.vector.tensor_tensor(o_a[:, b, cols], o_a[:, b, cols], th[:, b % 2, :], ALU.add).then_inc(gated, 1)
                return evac

            dve.wait_ge(decay_landed, 16)
            with dve.Fori(0, 2) as i:
                quad(i + 11, retention(i), gate_a_evac(i))
            quad(13, retention(2), gate_r_evac(0))

            def mix_part(f):
                def do():
                    dve.wait_ge(mix_hi, f + 1)
                    sub_hi(xt_lo[:, f, 0:SEQ], xt_hi[:, f, 0:SEQ], A[f % 4], 0.5).then_inc(mix_lo, 1)
                return do

            last_gate = gate_r_evac(1)

            def gate_and_mix(b):
                if b == 0:
                    dve.wait_ge(ro_scaled, 4 * RH)
                last_gate(b)
                mix_part(b)()

            quad(14, retention(3), gate_and_mix)

            def y_evac(cg):
                def evac(b):
                    dve.wait_ge(y_sq, 4 * cg + b + 1)
                    nc.vector.tensor_copy(y[:, b, cg * COLS:(cg + 1) * COLS], M[b]).then_inc(bank_free[b], 1)
                return evac

            quad(15, {k: (mix_part(4 + k),) for k in range(4)}, y_evac(0))
            quad(16, None, y_evac(1))

            dve.wait_ge(bank_free[3], 16 + 1)
            dve.wait_ge(x_back, 16)
            dve.wait_ge(rows_landed, 32)
            for t in range(NT + 1):
                if t < NT:
                    dve.wait_ge(y_rstd, t + 1)
                    nc.vector.scalar_tensor_tensor(out=scaled[:, t % 2, :], in0=y[:, t, :], scalar=stat[:, 12 + t:13 + t],
                                                   in1=row_post[:], op0=ALU.mult, op1=ALU.mult).then_inc(y_scaled, 1)
                    dve.wait_ge(y_scaled, t + 1)
                    nc.vector.tensor_tensor(h[:, t, :], h[:, t, :], scaled[:, t % 2, :], ALU.add).then_inc(h_done, 1)
                if t > 0:
                    dve.wait_ge(h_rstd, t)
                    nc.vector.tensor_scalar(y[:, t - 1, :], h[:, t - 1, :], stat[:, 19 + t:20 + t], None, ALU.mult).then_inc(f_normed, 1)
            for f in range(KT):
                dve.wait_ge(ft_hi, f + 1)
                sub_hi(xt_lo[:, f, 0:SEQ], xt_hi[:, f, 0:SEQ], ps[:, f, :], col_ffn[:, f:f + 1]).then_inc(ft_lo, 1)

            def up_evac(i, half):
                def evac(b):
                    dve.wait_ge(bank_free[b], i + (17 + 6 * half) + 1)
                    nc.vector.tensor_tensor(relu2[:, b % 2, :], relu[:, b, :], relu[:, b, :], ALU.mult).then_inc(sq_full, 1)
                    dve.wait_ge(sq_full, 4 * i + 16 * half + b + 1)
                    dve.wait_ge(sq_hi_ready, 4 * i + 16 * half + b + 1)
                    nc.vector.tensor_tensor(u_lo[:, ds(4 * i + b, 1), :].squeeze(1), relu2[:, b % 2, :],
                                            f32(u_hi[:, ds(4 * i + b, 1), :].squeeze(1)), ALU.subtract).then_inc(u_done, 1)
                return evac

            def down_evac(half, cg):
                def evac(b):
                    part = y[:, b, cg * COLS:(cg + 1) * COLS]
                    if half == 0:
                        nc.vector.tensor_copy(part, M[b]).then_inc(bank_free[b], 1)
                    else:
                        nc.vector.tensor_tensor(part, M[b], part, ALU.add).then_inc(y_done if cg else bank_free[b], 1)
                return evac

            for half in range(2):
                q0 = 17 + 8 * half
                with dve.Fori(0, 4) as i:
                    quad(i + q0, None, up_evac(i, half))
                for r in range(4):
                    quad(q0 + 4 + r, None, down_evac(half, r // 2) if r % 2 else None, last=(half == 1 and r == 3))

            for t in range(NT):
                dve.wait_ge(o_rstd, t + 1)
                nc.vector.scalar_tensor_tensor(out=scaled[:, t % 2, :], in0=y[:, t, :], scalar=stat[:, 12 + t:13 + t],
                                               in1=row_ffn[:], op0=ALU.mult, op1=ALU.mult).then_inc(o_scaled, 1)
                dve.wait_ge(o_scaled, t + 1)
                nc.vector.tensor_tensor(y[:, t, :], h[:, t, :], scaled[:, t % 2, :], ALU.add).then_inc(o_ready, 1)

        @block.tensor
        def _(pe):
            def three(out_ap, l_hi, l_lo, r_hi, r_lo, start, stop, **kw):
                nc.tensor.matmul(out_ap, l_hi, r_hi, start=start, stop=False, **kw)
                nc.tensor.matmul(out_ap, l_hi, r_lo, start=False, stop=False, **kw)
                return nc.tensor.matmul(out_ap, l_lo, r_hi, start=False, stop=stop, **kw)

            def columns(k, b):
                return (w[:, k % W_SLOTS, b * P:(b + 1) * P] for w in (w_hi, w_lo))

            def tokens(k, first, n):
                return (t[:, k, first:first + n] for t in (xt_hi, xt_lo))

            def features_step(k, b):
                return three(M[b], *columns(k, b), *tokens(k, 0, SEQ), k == 0, k == KT - 1)

            def rows_step(k, b):
                return three(M[b], *tokens(k, b * P, P), w_hi[:, k % W_SLOTS, :], w_lo[:, k % W_SLOTS, :], k == 0, k == KT - 1)

            def quad(q, step, extra=None, aux=None, before=None, grp=None, first=True):
                for k in range(KT):
                    pe.wait_ge(lo_ready, 8 * q + k + 1)
                    for b in range(4):
                        if before:
                            before(k, b)
                        if k == 0 and first and not (isinstance(q, int) and q == 0):
                            pe.wait_ge(bank_free[b], q if grp is None else grp)
                        mm = step(k, b)
                        if b < 3 or not extra:
                            mm.then_inc(mm_done, 1)
                        for do in (aux or {}).get((k, b), ()):
                            do()
                    if extra:
                        extra(k).then_inc(mm_done, 1)
                    for do in (aux or {}).get(k, ()):
                        do()

            pe.wait_ge(const_landed, 16 * 3)
            pe.wait_ge(normed, 1)
            for f in range(KT):
                mm = nc.tensor.transpose(A[3][:, f * META:(f + 1) * META], meta_in[:, f * P:(f + 1) * P], ident[0:META, 0:META])
            mm.then_inc(turned, 1)
            for t in range(NT):
                pe.wait_ge(normed, t + 2)
                for f in range(KT):
                    if t == 0 and f == 7:
                        pe.wait_ge(meta_scaled, 1)
                    mm = nc.tensor.transpose(ps[:, f, t * P:(t + 1) * P], x_in[:, t, f * P:(f + 1) * P], ident[:])
                    if t == NT - 1 or f == KT - 1:
                        mm.then_inc(turned, 1)

            def kv_step(k, b):
                if b < 2:
                    return features_step(k, b)
                wv = [w[:, k % W_SLOTS, 256:512] for w in (w_hi, w_lo)]
                for n in range(2):
                    first, rows = ((0, P), (CHUNK, P), (CHUNK + P, P), (CHUNK + 2 * P, P))[2 * (b - 2) + n]
                    mm = three(M[b][0:rows, n * 256:(n + 1) * 256], *tokens(k, first, rows), *wv, k == 0 and n == 0,
                               k == KT - 1, skip_group_check=True)
                return mm

            def kv_extra(k):
                if k == 0:
                    pe.wait_ge(xt_lo_ready, 6)
                wv = [w[:, k % W_SLOTS, 256:512] for w in (w_hi, w_lo)]
                rows = CHUNK + META
                three(A[0][0:rows, 0:256], *tokens(k, TOK - rows, rows), *wv, k == 0, k == KT - 1)
                for f in range(2):
                    mm = three(A[1][:, f * META:(f + 1) * META], *columns(k, f), *tokens(k, SEQ, META), k == 0 and f == 0,
                               k == KT - 1, skip_group_check=True)
                return mm

            quad(0, kv_step, kv_extra, before=lambda k, b: pe.wait_ge(xt_lo_ready, max(k, b) + 1) if k == 0 or b == 0 else None)

            quad(1, features_step)

            def scores(t, unit, u, f):
                def do():
                    pe.wait_ge(qz_lo_ready, unit + 1)
                    if u == 1:
                        pe.wait_ge(exp_done, unit)
                    for m in range(4):
                        dst = S4[:, m // 2, m % 2, :]
                        nc.tensor.matmul(dst, mask_q[:], mask_k[:, ds(KEYS * t, KEYS)], start=True, stop=False)
                        mm = three(dst, qz_hi[u][:, m, :], qz_lo[u][:, m, :], kt_hi[:, f, ds(KEYS * t, KEYS)],
                                   kt_lo[:, f, ds(KEYS * t, KEYS)], False, True)
                    mm.then_inc(qk_done, 1)
                return do

            def turn_probs(unit, u, pair):
                def do():
                    if pair == 0:
                        pe.wait_ge(exp_done, unit + 1)
                        if u == 1:
                            pe.wait_ge(att_out, unit)
                    else:
                        pe.wait_ge(pt_pair0_ready, unit + 1)
                    for n in range(2):
                        m = 2 * pair + n
                        nc.tensor.transpose(TB[:, n * P:(n + 1) * P], prob[:, m, 0:P], ident[:])
                        mm = nc.tensor.transpose(TB[0:KEYS - P, 256 + n * P:256 + (n + 1) * P], prob[:, m, P:KEYS], ident[:])
                    mm.then_inc(p_turned, 1)
                return do

            def values(t, unit, g):
                def do():
                    pe.wait_ge(pt_pair1_ready, unit + 1)
                    for m in range(4):
                        dst = TB[:, m * HD:(m + 1) * HD]
                        nc.tensor.matmul(dst, pt_first[:, m, :], v_first[:, ds(t, 1), g * HD:(g + 1) * HD].squeeze(1), start=True, stop=False)
                        mm = nc.tensor.matmul(dst, pt_second[0:KEYS - P, m, :],
                                              v_second[0:KEYS - P, ds(t, 1), g * HD:(g + 1) * HD].squeeze(1), start=False, stop=True)
                    mm.then_inc(pv_done, 1)
                return do

            def attention(t, unit0, g0):
                a, b, f = unit0, unit0 + 1, g0 // 2
                return {1: (scores(t, a, 0, f),), 3: (turn_probs(a, 0, 0),), 4: (turn_probs(a, 0, 1), scores(t, b, 1, f)),
                        5: (values(t, a, g0),), 6: (turn_probs(b, 1, 0),), (7, 0): (turn_probs(b, 1, 1),),
                        7: (values(t, b, g0 + 1),)}

            def meta_keys(k, n):
                if k == 0:
                    pe.wait_ge(meta_free, n + 1)
                for b in range(4):
                    mm = three(MB[:, b * META:(b + 1) * META], *columns(k, b), *tokens(k, SEQ, META), k == 0 and b == 0,
                               k == KT - 1, skip_group_check=True)
                return mm

            def meta_rows(k, n):
                if k == 0:
                    pe.wait_ge(meta_free, n + 1)
                return three(MB[0:META, :], *tokens(k, SEQ, META), w_hi[:, k % W_SLOTS, :], w_lo[:, k % W_SLOTS, :], k == 0, k == KT - 1)

            with pe.Fori(0, 2) as i:
                quad(i + 2, features_step, None, attention(i, 2 * i, 0))
            with pe.Fori(0, 2) as i:
                quad(i + 4, features_step, lambda k: meta_keys(k, i), attention(i + 2, 2 * i + 4, 0))
            quad(6, features_step)
            with pe.Fori(0, 2) as i:
                quad(i + 7, rows_step, lambda k: meta_rows(k, i + 2), attention(i, 2 * i + 8, 2))
            with pe.Fori(0, 2) as i:
                quad(i + 9, rows_step, None, attention(i + 2, 2 * i + 12, 2))

            def ret_scores(hd, n):
                rows, cols = score_shape(n)
                k0, q0 = (SEQ, 0) if n == 0 else (P * (n - 1), P * (n - 1))

                def do():
                    if n == 0:
                        pe.wait_ge(hq_lo_ready, hd + 1)
                    for f in range(2):
                        mm = three(A[n % 2][0:rows, 0:cols], hk_hi[:, f, k0:k0 + rows], hk_lo[:, f, k0:k0 + rows],
                                   hq_hi[:, f, q0:SEQ], hq_lo[:, f, q0:SEQ], f == 0, f == 1)
                    mm.then_inc(rs_done, 1)
                return do

            def ret_values(hd, n):
                rows, cols = score_shape(n)
                tile, j0 = (NT, 0) if n == 0 else (n - 1, n - 1)

                def do():
                    if n == 0:
                        pe.wait_ge(hv_lo_ready, hd + 1)
                    pe.wait_ge(sc_lo_ready, 5 * hd + n + 1)
                    for j in range(j0, NT):
                        c0 = (j - j0) * P
                        mm = three(A[2 + j // 2][:, (j % 2) * RD:(j % 2 + 1) * RD], sc_hi[0:rows, n % 2, c0:c0 + P],
                                   sc_lo[0:rows, n % 2, c0:c0 + P], hv_hi[0:rows, tile, :], hv_lo[0:rows, tile, :],
                                   n == 0 and j % 2 == 0, n == j + 1, skip_group_check=True)
                    if n == NT:
                        mm.then_inc(ro_done, 1)
                return do

            def retention(hd):
                s, v = (lambda n: ret_scores(hd, n)), (lambda n: ret_values(hd, n))
                return {1: (s(0), s(1)), 3: (v(0), s(2)), 4: (v(1), s(3)), 5: (v(2), s(4)), 6: (v(3), v(4))}

            with pe.Fori(0, 2) as i:
                quad(i + 11, rows_step, None, retention(i))
            quad(13, rows_step, None, retention(2))
            quad(14, rows_step, None, retention(3))

            def turn_mixed(f):
                def do():
                    if f == 0:
                        pe.wait_ge(ro_scaled, 4 * RH)
                    if f >= 4:
                        pe.wait_ge(gated, 16)
                        pe.wait_ge(mix_lo, f - 3)
                    for t in range(NT):
                        mm = nc.tensor.transpose(A[f % 4][:, t * P:(t + 1) * P], o_a[:, t, f * P:(f + 1) * P], ident[:])
                    mm.then_inc(mix_turned, 1)
                return do

            for f in range(4):
                turn_mixed(f)()
            quad(15, rows_step, None, {k: (turn_mixed(4 + k),) for k in range(4)}, before=lambda k, b: pe.wait_ge(mix_lo, k + 1) if b == 0 else None)
            quad(16, rows_step)

            for t in range(NT):
                pe.wait_ge(f_normed, t + 1)
                for f in range(KT):
                    mm = nc.tensor.transpose(ps[:, f, t * P:(t + 1) * P], y[:, t, f * P:(f + 1) * P], ident[:])
                    if t == NT - 1 or f == KT - 1:
                        mm.then_inc(f_turned, 1)

            def down_step(r):
                def step(k, b):
                    kk = 8 * r + k
                    return three(M[b], u_hi[:, kk, b * P:(b + 1) * P], u_lo[:, kk, b * P:(b + 1) * P],
                                 w_hi[:, k % W_SLOTS, :], w_lo[:, k % W_SLOTS, :], kk == 0, kk == 15)
                return step

            for half in range(2):
                q0 = 17 + 8 * half
                g0 = 17 + 6 * half
                if half == 0:
                    quad(17, features_step, grp=17,
                         before=lambda k, b: pe.wait_ge(ft_lo, max(k, b) + 1) if k == 0 or b == 0 else None)
                with pe.Fori(1 if half == 0 else 0, 4) as i:
                    quad(i + q0, features_step, grp=i + g0)
                for r in range(4):
                    quad(q0 + 4 + r, down_step(r % 2), grp=g0 + 4 + r // 2, first=r % 2 == 0,
                         before=(lambda k, b: pe.wait_ge(u_done, 16 * half + 16) if k == b == 0 else None) if r % 2 else None)


def tables():
    import numpy as np

    f = np.float32
    half = RD // 2
    pos = np.concatenate([np.arange(CHUNK, CHUNK + SEQ), np.arange(CHUNK - META, CHUNK)]).astype(f)
    inv_freq = (f(10000.0) ** (-np.arange(half, dtype=f) / f(half))).astype(f)
    ang = (pos[None, :] * inv_freq[:, None]).astype(f)
    log_gamma = np.log(f(1.0) - f(2.0) ** (f(-5.0) - np.arange(RH, dtype=f))).astype(f)
    k, q = np.arange(P)[:, None], np.arange(TOK)[None, :]
    seen = (q // CHUNK >= k // CHUNK)
    decay = np.exp(log_gamma[None, :, None] * np.abs(q - k)[:, None, :].astype(f)) * seen[:, None, :] * f(RD ** -0.5)
    mask_q = np.zeros((2, P), f)
    mask_q[0, :CHUNK] = mask_q[1, CHUNK:] = 1
    mask_k = np.zeros((2, NT, KEYS), f)
    mask_k[0, :, P:P + CHUNK] = -1e30
    mask_k[1, :, 0:CHUNK] = -1e30
    mask_k[0, 0, 0:CHUNK] = -1e30
    return {"ident": np.eye(P, dtype=f), "cos": np.cos(ang), "sin": np.sin(ang), "decay": decay.astype(f),
            "mask_q": mask_q, "mask_k": mask_k.reshape(2, NT * KEYS)}


_INS = ["x", "meta_tokens", "norm_mix_pre", "attn_sinks", "norm_mix_post", "norm_ffn_pre", "norm_ffn_post"]
_TABLES = ["ident", "cos", "sin", "decay", "mask_q", "mask_k"]


def quads(w_in, w_out, w_up, w_down):
    import numpy as np

    def cut(w, row, col):
        return w[0, row:row + D, col:col + COLS].reshape(4, 2, P, COLS).transpose(0, 2, 1, 3)

    def q_a(half):
        q = cut(w_in, 0, COLS * half)
        return q.reshape(4, P, 2, 2, 4, HD).transpose(0, 1, 2, 4, 3, 5).reshape(q.shape)

    order = [cut(w_in, 0, 1024), q_a(0)]
    order += [cut(w_in, 0, 1536 + COLS * n) for n in range(4)] + [q_a(1)]
    order += [cut(w_in, 0, 3584 + COLS * n) for n in range(8)]
    order += [cut(w_out, 0, COLS * n) for n in range(2)]
    for half in range(2):
        order += [cut(w_up, 0, DFF // 2 * half + COLS * n) for n in range(4)]
        order += [cut(w_down, DFF // 2 * half + D * r, COLS * cg) for cg in range(2) for r in range(2)]
    return np.ascontiguousarray(np.stack(order))


def kernel(**inputs):
    import numpy as np
    import concourse.bacc as bacc
    from concourse.bass_utils import run_bass_kernel_spmd as run

    nc = bacc.Bacc("TRN2", target_bir_lowering=False, num_devices=1)
    given = {n: np.ascontiguousarray(inputs[n]) for n in _INS}
    given["weights"] = quads(*(np.asarray(inputs[n]) for n in ("w_in", "w_out", "w_up", "w_down")))
    given.update(tables())
    arrays, args = {}, []
    for name in _INS + ["weights"] + _TABLES:
        arrays[f"in_{name}"] = given[name]
        args.append(nc.dram_tensor(f"in_{name}", given[name].shape, mybir.dt.from_np(given[name].dtype), kind="ExternalInput").ap())
    args.append(nc.dram_tensor("out_0", (1, SEQ, D), F32, kind="ExternalOutput").ap())
    hybrid_block(nc, *args)
    r = run(nc, [arrays], core_ids=[0])
    return r.results[0]["out_0"]
```

```python
from contextlib import ExitStack

import concourse.bass as bass
from concourse import mybir

F32 = mybir.dt.float32
F32R = mybir.dt.float32r
BF16 = mybir.dt.bfloat16
ACT = mybir.ActivationFunctionType
ALU = mybir.AluOpType
AX_X = mybir.AxisListType.X
ds = bass.ds

P = 128
D = 1024
SEQ = 512
KT = D // P
NT = SEQ // P
CHUNK = 64
META = 16
TOK = SEQ + META
M_LO = 32
M_BOTH = M_LO + META
COLS = 512
DFF = 4096
HD = 64
KEYS = CHUNK + P + META
RH = 4
RD = 256
EPS = 1e-6
ATT_SCALE = HD ** -0.5
W_SLOTS = 4
QUADS = 33
MIX_AT = ((0, 2), (2, 4), (3, 6))
H_BACK = 17


def hybrid_block(nc, x, meta_tokens, w_pre, sinks, w_post, w_ffn_pre, w_ffn_post, weights,
                 c_ident, c_cos, c_sin, c_decay, c_mask_q, c_mask_k, out):
    ctx = ExitStack()
    with ctx:
        def sem(name):
            return ctx.enter_context(nc.semaphore(name))

        def keep(name, shape, dt=F32):
            return ctx.enter_context(nc.sbuf_tensor(name, shape, dt))

        raw = keep("raw", [P, 4, 2, COLS])
        w_hi = keep("w_hi", [P, W_SLOTS, COLS], F32R)
        w_lo = keep("w_lo", [P, W_SLOTS, COLS], F32R)
        xt_hi = keep("xt_hi", [P, KT, SEQ + M_BOTH], F32R)
        xt_lo = keep("xt_lo", [P, KT, TOK], F32R)
        ident = keep("ident", [P, P])
        col_pre = keep("col_pre", [P, KT])
        col_ffn = keep("col_ffn", [P, KT])
        stat = keep("stat", [P, 64])
        neg_half = keep("neg_half", [P, 4])

        mixer = ExitStack()

        def a_buf(name, shape, dt=F32):
            return mixer.enter_context(nc.sbuf_tensor(name, shape, dt))

        o_a = a_buf("o_a", [P, NT, D])
        rq = a_buf("rq", [P, KT, SEQ])
        rk = a_buf("rk", [P, KT, TOK])
        g2 = a_buf("g2", [P, NT, D])
        v_r = a_buf("v_r", [P, NT, D])
        v_rm = a_buf("v_rm", [META, D])
        cos_sin = a_buf("cos_sin", [P, 2, TOK])
        cos, sin = cos_sin[:, 0, :], cos_sin[:, 1, :]
        th = cos_sin[:, :, 0:COLS]
        rope_a, rope_c, rope_b, rope_x = (v_r[:, n, :].rearrange("p (e c) -> p e c", e=2) for n in range(4))
        x_in, meta_in = g2, v_rm

        att = ExitStack()

        def t_buf(name, shape, dt=F32):
            return att.enter_context(nc.sbuf_tensor(name, shape, dt))

        kt_hi = t_buf("kt_hi", [P, 2, NT * KEYS], F32R)
        kt_lo = t_buf("kt_lo", [P, 2, NT * KEYS], F32R)
        qt = t_buf("qt", [P, 4, SEQ])
        v_first = t_buf("v_first", [P, NT, 256])
        v_second = t_buf("v_second", [P, NT, 256])
        qz_hi = [t_buf(f"qz_hi{u}", [P, 4, P], F32R) for u in range(2)]
        qz_lo = [t_buf(f"qz_lo{u}", [P, 4, P], F32R) for u in range(2)]
        prob = t_buf("prob", [P, 4, KEYS])
        pt_first = t_buf("pt_first", [P, 4, P])
        pt_second = t_buf("pt_second", [P, 4, P])
        rope_m = t_buf("rope_m", [P, 4, 2, META])
        m_rows = t_buf("m_rows", [P, COLS])
        fold = t_buf("fold", [P, META])
        mask_q = t_buf("mask_q", [P, P], BF16)
        mask_k = t_buf("mask_k", [P, NT * KEYS], BF16)
        sink = t_buf("sink", [P, 16])
        nsink = t_buf("nsink", [P, 16])
        att.close()

        ret = ExitStack()

        def r_buf(name, shape, dt=F32):
            return ret.enter_context(nc.sbuf_tensor(name, shape, dt))

        decay = r_buf("decay", [P, RH, TOK])
        hk_hi = r_buf("hk_hi", [P, 2, TOK], F32R)
        hk_lo = r_buf("hk_lo", [P, 2, TOK], F32R)
        hq_hi = r_buf("hq_hi", [P, 2, SEQ], F32R)
        hq_lo = r_buf("hq_lo", [P, 2, SEQ], F32R)
        hv_hi = r_buf("hv_hi", [P, NT + 1, RD], F32R)
        hv_lo = r_buf("hv_lo", [P, NT + 1, RD], F32R)
        sc = r_buf("sc", [P, 2, SEQ])
        sc_hi = r_buf("sc_hi", [P, 2, SEQ], F32R)
        sc_lo = r_buf("sc_lo", [P, 2, SEQ], F32R)
        ret_junk = r_buf("ret_junk", [P, RD])
        th_more = r_buf("th_more", [P, 2, COLS])
        th_gate = [th[:, 0, :], th[:, 1, :], th_more[:, 0, :], th_more[:, 1, :]]
        ret.close()
        mixer.close()

        u_hi = keep("u_hi", [P, 16, SEQ], F32R)
        u_lo = keep("u_lo", [P, 16, SEQ], F32R)
        y = keep("y", [P, NT, D])
        h = keep("h", [P, NT, D])
        row_post = keep("row_post", [P, D])
        row_ffn = keep("row_ffn", [P, D])
        relu = keep("relu", [P, 4, COLS])
        relu2 = keep("relu2", [P, 2, COLS])
        scaled = keep("scaled", [P, 2, COLS])
        junk = keep("junk", [P, D])

        ps = ctx.enter_context(nc.psum_tensor("ps", [P, 8, COLS], F32))
        M = [ps[:, b, :] for b in range(4)]
        A = [ps[:, 4 + b, :] for b in range(4)]
        S4 = ps[:, 4:6, 0:2 * KEYS].rearrange("p b (m k) -> p b m k", m=2)
        TB = A[2]
        MB = A[3]

        raw_landed = [sem(f"raw_landed{c}") for c in range(4)]
        hi_ready, lo_ready, mm_done = sem("hi_ready"), sem("lo_ready"), sem("mm_done")
        bank_free = [sem(f"bank_free{b}") for b in range(4)]
        x_landed = [sem(f"x_landed{t}") for t in range(NT)]
        meta_landed, const_landed, table_landed = sem("meta_landed"), sem("const_landed"), sem("table_landed")
        decay_landed = sem("decay_landed")
        ms_eps = sem("ms_eps")
        zeroed, masks_ready = sem("zeroed"), sem("masks_ready")
        sq_ready, rstd_ready, normed, turned = sem("sq_ready"), sem("rstd_ready"), sem("normed"), sem("turned")
        meta_scaled, xt_hi_ready, xt_lo_ready = sem("meta_scaled"), sem("xt_hi_ready"), sem("xt_lo_ready")
        kt_hi_done, v_done = sem("kt_hi_done"), sem("v_done")
        rope_parts, rope_slot_free, meta_free = sem("rope_parts"), sem("rope_slot_free"), sem("meta_free")
        meta_done, meta_staged, meta_folded = sem("meta_done"), sem("meta_staged"), sem("meta_folded")
        qz_hi_ready, qk_done = sem("qz_hi_ready"), sem("qk_done")
        max_ready, bias_ready, sink_ready, exp_done = sem("max_ready"), sem("bias_ready"), sem("sink_ready"), sem("exp_done")
        den_ready, rden_ready = sem("den_ready"), sem("rden_ready")
        p_turned, pt_pair0_ready, pt_pair1_ready = sem("p_turned"), sem("pt_pair0_ready"), sem("pt_pair1_ready")
        pv_done, att_out = sem("pv_done"), sem("att_out")
        hk_hi_ready, hq_hi_ready, hv_hi_ready = sem("hk_hi_ready"), sem("hq_hi_ready"), sem("hv_hi_ready")
        hq_lo_ready, hv_lo_ready = sem("hq_lo_ready"), sem("hv_lo_ready")
        r_gated, qz_lo_ready = sem("r_gated"), sem("qz_lo_ready")
        rs_done, sc_ready, sc_hi_ready, sc_lo_ready = sem("rs_done"), sem("sc_ready"), sem("sc_hi_ready"), sem("sc_lo_ready")
        ro_done, ro_sq, ro_rstd, ro_scaled = sem("ro_done"), sem("ro_sq"), sem("ro_rstd"), sem("ro_scaled")
        th_ready, gated, mixed_done = sem("th_ready"), sem("gated"), sem("mixed_done")
        mix_turned, mix_hi, mix_lo = sem("mix_turned"), sem("mix_hi"), sem("mix_lo")
        y_sq, y_sum, y_rstd, y_scaled, h_done = sem("y_sq"), sem("y_sum"), sem("y_rstd"), sem("y_scaled"), sem("h_done")
        h_sq, h_rstd, f_normed, f_turned = sem("h_sq"), sem("h_rstd"), sem("f_normed"), sem("f_turned")
        ft_hi, ft_lo = sem("ft_hi"), sem("ft_lo")
        relu_ready, sq_hi_ready, sq_full, u_done = sem("relu_ready"), sem("sq_hi_ready"), sem("sq_full"), sem("u_done")
        x_back, row_post_landed, row_ffn_landed = sem("x_back"), sem("row_post_landed"), sem("row_ffn_landed")
        y_done, o_sq, o_rstd, o_scaled, o_ready, stored = (sem(n) for n in (
            "y_done", "o_sq", "o_rstd", "o_scaled", "o_ready", "stored"))

        start_junk = [rq[:, 2 * t:2 * t + 2, :].rearrange("p a b -> p (a b)") for t in range(NT)]
        mask_f = o_a[0:2, 3, 0:P + NT * KEYS]
        m_scaled = o_a[:, 1, 0:KT * META].rearrange("p (k n) -> p k n", k=KT)

        def kt_views(kt, f):
            v = kt[:, f, :].rearrange("p (t k) -> p t k", k=KEYS)
            return v[:, :, CHUNK:CHUNK + P], v[:, 1:NT, 0:CHUNK], v[:, :, CHUNK + P:KEYS]

        def score_shape(n):
            return (META, SEQ) if n == 0 else (P, SEQ - P * (n - 1))

        def f32(ap):
            return ap.bitcast(F32)

        x_v = x[0].rearrange("(t p) d -> t p d", p=P)
        out_v = out[0].rearrange("(t p) d -> t p d", p=P)

        block = ctx.enter_context(nc.Block())

        @block.sync
        def _(sp):
            def load(q, c):
                sp.dma_start(raw[:, c], weights[q, c] if isinstance(q, int) else weights[ds(q, 1), c].squeeze(0)).then_inc(raw_landed[c], 16)

            def reload(q, c):
                sp.wait_ge(lo_ready, 8 * (q - 1) + 2 * c + 2)
                load(q, c)

            sp.dma_start(meta_in[:], meta_tokens).then_inc(meta_landed, 16)
            for t in range(NT):
                sp.dma_start(x_in[:, t, :], x_v[t]).then_inc(x_landed[t], 16)
                if t == 0:
                    sp.dma_start(ident[:], c_ident).then_inc(const_landed, 16)
                    sp.dma_start(col_pre[:], w_pre).then_inc(const_landed, 16)
            for c in range(4):
                load(0, c)
            with sp.Fori(1, H_BACK) as q:
                for c in range(4):
                    reload(q, c)
            sp.wait_ge(mix_lo, KT)
            sp.dma_start(row_post[:], w_post[0].partition_broadcast(P)).then_inc(row_post_landed, 16)
            sp.dma_start(h[:], x[0].rearrange("(t p) d -> p t d", p=P)).then_inc(x_back, 16)
            with sp.Fori(H_BACK, QUADS) as q:
                for c in range(4):
                    reload(q, c)
            for t in range(NT):
                for c in range(2):
                    sp.wait_ge(o_ready, 2 * t + c + 1)
                    cols = slice(c * COLS, (c + 1) * COLS)
                    sp.dma_start(out_v[t][:, cols], h[:, t, cols]).then_inc(stored, 16)
            sp.wait_ge(stored, 16 * 2 * NT)

        @block.gpsimd
        def _(pool):
            nc.gpsimd.memset(neg_half[:], -0.5).then_inc(rope_slot_free, 1)
            nc.gpsimd.memset(stat[:, 62:63], 0.0).then_inc(rope_slot_free, 1)
            nc.gpsimd.memset(stat[:, 63:64], 0.0).then_inc(meta_free, 1)

            def rsqrt(dst, src, eps, done):
                rows, cols = src.shape
                nc.gpsimd.tensor_scalar(dst, src, eps, None, ALU.add).then_inc(ms_eps, 1)
                pool.wait_ge(ms_eps, done + 1)
                return nc.gpsimd.tensor_tensor(dst, dst, neg_half[0:rows, 0:cols], ALU.pow)

            pool.wait_ge(sq_ready, 1)
            rsqrt(stat[0:META, 5:6], stat[0:META, 4:5], EPS, 0).then_inc(rstd_ready, 1)
            for t in range(NT):
                pool.wait_ge(sq_ready, t + 2)
                rsqrt(stat[:, 8 + t:9 + t], stat[:, t:t + 1], EPS, 1 + t).then_inc(rstd_ready, 1)

            pool.dma_start(mask_f[:, 0:P], c_mask_q).then_inc(table_landed, 16)
            pool.dma_start(mask_f[:, P:P + NT * KEYS], c_mask_k).then_inc(table_landed, 16)
            pool.dma_start(sink[:], sinks[0].partition_broadcast(P)).then_inc(table_landed, 16)
            pool.dma_start(col_ffn[:], w_ffn_pre).then_inc(table_landed, 16)
            pool.dma_start(cos, c_cos).then_inc(table_landed, 16)
            pool.dma_start(sin, c_sin).then_inc(table_landed, 16)
            for kt in (kt_hi, kt_lo):
                for f in range(2):
                    nc.gpsimd.memset(f32(kt[:, f, 0:CHUNK]), 0.0)
            for qz in (*qz_hi, *qz_lo):
                nc.gpsimd.memset(f32(qz[:]), 0.0)
            nc.gpsimd.memset(f32(xt_hi[:, :, TOK:SEQ + M_LO]), 0.0)
            nc.gpsimd.memset(m_rows[:], 0.0)
            nc.gpsimd.memset(fold[:], 0.0)
            nc.gpsimd.memset(mask_q[:], 0.0)
            nc.gpsimd.memset(mask_k[:], 0.0)
            nc.gpsimd.memset(v_first[:, 0, :], 0.0).then_inc(zeroed, 1)

            def rotate(i, first_tile, dst, n0):
                for e in range(2):
                    pool.wait_ge(rope_parts, 2 * i + n0 + e + 1)
                    lo_t = dst[:, ds(4 * i + 2 * e, 1), 0:SEQ].squeeze(1)
                    hi_t = dst[:, ds(4 * i + 2 * e + 1, 1), 0:SEQ].squeeze(1)
                    nc.gpsimd.tensor_tensor(lo_t, rope_a[:, e], rope_b[:, e], ALU.subtract)
                    nc.gpsimd.tensor_tensor(hi_t, rope_c[:, e], rope_x[:, e], ALU.add).then_inc(rope_slot_free, 1)

            with pool.Fori(0, 2) as i:
                rotate(i, 0, rq, 0)
            with pool.Fori(0, 2) as i:
                rotate(i, 0, rk, 4)
            pool.wait_ge(qk_done, 16)
            pool.dma_start(decay[:], c_decay).then_inc(decay_landed, 16)
            for hd in range(RH):
                pool.wait_ge(ro_sq, 4 * hd + 4)
                rsqrt(stat[:, 36:40], stat[:, 32:36], 4 * EPS, hd + 5).then_inc(ro_rstd, 1)
            pool.wait_ge(x_back, 16)
            pool.dma_start(row_ffn[:], w_ffn_post[0].partition_broadcast(P)).then_inc(row_ffn_landed, 16)
            for t in range(NT + 1):
                if t < NT:
                    pool.wait_ge(y_sq, 4 + t + 1)
                    nc.gpsimd.tensor_tensor(stat[:, 8 + t:9 + t], stat[:, t:t + 1], stat[:, 4 + t:5 + t], ALU.add).then_inc(y_sum, 1)
                    pool.wait_ge(y_sum, t + 1)
                    rsqrt(stat[:, 12 + t:13 + t], stat[:, 8 + t:9 + t], EPS, 9 + max(0, 2 * t - 1)).then_inc(y_rstd, 1)
                if t > 0:
                    pool.wait_ge(h_sq, t)
                    rsqrt(stat[:, 19 + t:20 + t], stat[:, 15 + t:16 + t], EPS, 9 + min(2 * t, 7)).then_inc(h_rstd, 1)
            for t in range(NT):
                pool.wait_ge(o_sq, 4 + t + 1)
                nc.gpsimd.tensor_tensor(stat[:, 8 + t:9 + t], stat[:, t:t + 1], stat[:, 4 + t:5 + t], ALU.add).then_inc(y_sum, 1)
                pool.wait_ge(y_sum, NT + t + 1)
                rsqrt(stat[:, 12 + t:13 + t], stat[:, 8 + t:9 + t], EPS, 17 + t).then_inc(o_rstd, 1)

        @block.scalar
        def _(act):
            def split(q, k, staggered=False):
                if k >= KT:
                    q, k = q + 1, k - KT
                s = 8 * q + k
                if k % 2 == 0:
                    act.wait_ge(raw_landed[k // 2], 16 * q + 16)
                if staggered:
                    act.wait_ge(mm_done, 4 * (s - k - 1) + k + 1)
                elif not (isinstance(s, int) and s < W_SLOTS):
                    act.wait_ge(mm_done, 4 * (s - W_SLOTS + 1))
                nc.scalar.activation(w_hi[:, k % W_SLOTS, :], raw[:, k // 2, k % 2, :], ACT.Copy).then_inc(hi_ready, 1)

            def quad(q, aux=None, evac=None, after=None, staggered=False):
                for k in range(KT):
                    if not (staggered and k + 3 >= KT):
                        split(q, k + 3)
                    for do in (aux or {}).get(k, ()):
                        do()
                for b in range(4 if evac else 0):
                    if staggered and b == 3 and q + 1 < QUADS:
                        for k in range(3):
                            split(q + 1, k, staggered=True)
                    act.wait_ge(mm_done, 4 * (8 * q + 4 + b + 1) if staggered else 4 * (8 * q + 7) + b + 1)
                    evac(b)
                for do in after or ():
                    do()

            def bank_copy(banks, dst):
                def evac(b):
                    if b in banks:
                        nc.scalar.activation(dst(b), M[b], ACT.Copy).then_inc(bank_free[b], 1)
                return evac

            act.wait_ge(meta_landed, 16)
            nc.scalar.activation(o_a[0:META, 2, :], meta_in[:], ACT.Square, scale=1 / 32, accum_out=stat[0:META, 4:5]).then_inc(sq_ready, 1)
            for t in range(NT):
                act.wait_ge(x_landed[t], 16)
                nc.scalar.activation(start_junk[t], x_in[:, t, :], ACT.Square, scale=1 / 32,
                                     accum_out=stat[:, t:t + 1]).then_inc(sq_ready, 1)
            split(0, 0)
            act.wait_ge(meta_scaled, 1)
            nc.scalar.activation(xt_hi[:, :, SEQ:TOK], m_scaled, ACT.Copy).then_inc(xt_hi_ready, 1)
            for f in range(KT):
                act.wait_ge(turned, 1 + 3 + f + 1)
                nc.scalar.activation(xt_hi[:, f, 0:SEQ], ps[:, f, :], ACT.Copy,
                                     scale=col_pre[:, f:f + 1]).then_inc(xt_hi_ready, 1)
                if f in (4, 6):
                    split(0, f // 2 - 1)

            def masks():
                act.wait_ge(table_landed, 16 * 6)
                act.wait_ge(zeroed, 1)
                nc.scalar.activation(mask_q[0:2, :], mask_f[:, 0:P], ACT.Copy)
                nc.scalar.activation(mask_k[0:2, :], mask_f[:, P:P + NT * KEYS], ACT.Copy)
                nc.scalar.mul(nsink[:], sink[:], -1.0).then_inc(masks_ready, 1)

            def kv_evac(b):
                if b < 2:
                    own, prev, met = kt_views(kt_hi, b)
                    nc.scalar.activation(own, M[b].rearrange("p (t n) -> p t n", t=NT), ACT.Copy)
                    nc.scalar.activation(prev, M[b][:, CHUNK:CHUNK + 3 * P].rearrange("p (t n) -> p t n", t=3)[:, :, 0:CHUNK],
                                         ACT.Copy).then_inc(kt_hi_done, 1)
                if b == 2:
                    nc.scalar.activation(v_first[CHUNK:P, 0, :], M[2][0:CHUNK, 0:256], ACT.Copy)
                    nc.scalar.activation(v_first[:, 1, :], M[2][:, 256:512], ACT.Copy).then_inc(v_done, 1)
                if b == 3:
                    nc.scalar.activation(v_first[:, 2, :], M[3][:, 0:256], ACT.Copy)
                    nc.scalar.activation(v_first[:, 3, :], M[3][:, 256:512], ACT.Copy).then_inc(v_done, 1)

            def meta_keys():
                act.wait_ge(meta_done, 1)
                for f in range(2):
                    nc.scalar.activation(kt_views(kt_hi, f)[2], A[1][:, f * META:(f + 1) * META].unsqueeze(1)
                                         .to_broadcast([P, NT, META]), ACT.Copy).then_inc(kt_hi_done, 1)

            quad(0, {6: (masks,), 7: (meta_keys,)}, kv_evac)

            def q_evac():
                return bank_copy((0, 1, 2, 3), lambda b: qt[:, b, :])

            quad(1, evac=q_evac())
            act.wait_ge(bank_free[3], 1 + 1)

            def stage_q(t, u):
                rows = slice(64 * u, 64 * u + 64)

                def do():
                    nc.scalar.activation(qz_hi[u][rows], qt[rows, :, ds(P * t, P)], ACT.Copy).then_inc(qz_hi_ready, 1)
                return do

            def exps(unit):
                def do():
                    act.wait_ge(bias_ready, unit + 1)
                    for m in range(4):
                        nc.scalar.activation(prob[:, m, :], S4[:, m // 2, m % 2, :], ACT.Exp, bias=stat[:, 12 + m:13 + m],
                                             scale=ATT_SCALE, accum_out=stat[:, 20 + m:21 + m])
                    act.wait_ge(sink_ready, unit + 1)
                    nc.scalar.activation(stat[:, 24:28], stat[:, 16:20], ACT.Exp).then_inc(exp_done, 1)
                return do

            def copy_pair(unit, pair, done):
                heads = slice(2 * pair, 2 * pair + 2)

                def do():
                    act.wait_ge(p_turned, 2 * unit + pair + 1)
                    nc.scalar.activation(pt_first[:, heads, :], TB[:, 0:256].rearrange("p (m q) -> p m q", m=2), ACT.Copy)
                    nc.scalar.activation(pt_second[0:KEYS - P, heads, :], TB[0:KEYS - P, 256:512].rearrange("p (m q) -> p m q", m=2),
                                         ACT.Copy).then_inc(done, 1)
                return do

            def attention(t, unit0):
                return {0: (stage_q(t, 0), stage_q(t, 1)), 2: (exps(unit0),), 4: (copy_pair(unit0, 0, pt_pair0_ready),),
                        5: (exps(unit0 + 1),),
                        7: (copy_pair(unit0 + 1, 0, pt_pair0_ready), copy_pair(unit0 + 1, 1, pt_pair1_ready))}

            def rope_evac(i, n0):
                def evac(b):
                    if b % 2:
                        act.wait_ge(rope_slot_free, 2 * i + n0 + b // 2 + 1)
                        nc.scalar.activation(rope_x[:, b // 2], M[b], ACT.Copy).then_inc(bank_free[b], 1)
                return evac

            with act.Fori(0, 2) as i:
                aux = attention(i, 2 * i)
                quad(i + 2, aux, rope_evac(i, 0))
            def stage_meta(i, rows, n):
                def do():
                    act.wait_ge(meta_done, i + 1 + 1)
                    nc.scalar.activation(m_rows[0:n, :], MB[rows, :], ACT.Copy).then_inc(meta_staged, 1)
                return do

            with act.Fori(0, 2) as i:
                aux = attention(i + 2, 2 * i + 4)
                aux[7] += (stage_meta(i, slice(0, M_BOTH), M_BOTH),)
                quad(i + 4, aux, rope_evac(i, 4))
            quad(6, evac=q_evac())
            act.wait_ge(bank_free[3], 6 + 1)

            with act.Fori(0, 2) as i:
                aux = attention(i, 2 * i + 8)
                aux[7] += (stage_meta(i + 2, slice(M_LO, M_BOTH), META),)
                quad(i + 7, aux, bank_copy((1, 3), lambda b: v_r[:, b, ds(i * COLS, COLS)]))

            def tanh_evac(i):
                def evac(b):
                    if b >= 2:
                        act.wait_ge(bank_free[b - 2], i + 9 + 1)
                    nc.scalar.activation(th[:, b % 2, :], M[b], ACT.Tanh, scale=0.5).then_inc(th_ready, 1)
                return evac

            def gate_evac(b):
                nc.scalar.activation(th_gate[b], M[b], ACT.Tanh, scale=0.5).then_inc(bank_free[b], 1)

            with act.Fori(0, 2) as i:
                aux = attention(i + 2, 2 * i + 12)
                quad(i + 9, aux, tanh_evac(i))

            act.wait_ge(rope_slot_free, 2 + 8)

            def stage_kq(hd):
                def do():
                    nc.scalar.activation(hk_hi[:], rk[:, ds(2 * hd, 2), :], ACT.Copy).then_inc(hk_hi_ready, 1)
                    nc.scalar.activation(hq_hi[:], rq[:, ds(2 * hd, 2), :], ACT.Copy).then_inc(hq_hi_ready, 1)
                return do

            def stage_v(hd):
                def do():
                    nc.scalar.activation(hv_hi[:, 0:NT, :], v_r[:, :, ds(RD * hd, RD)], ACT.Copy)
                    nc.scalar.activation(hv_hi[0:META, NT, :], v_rm[:, ds(RD * hd, RD)], ACT.Copy).then_inc(hv_hi_ready, 1)
                return do

            def score_hi(hd, n):
                rows, cols = score_shape(n)

                def do():
                    act.wait_ge(sc_ready, 5 * hd + n + 1)
                    nc.scalar.activation(sc_hi[0:rows, n % 2, 0:cols], sc[0:rows, n % 2, 0:cols], ACT.Copy).then_inc(sc_hi_ready, 1)
                return do

            def ret_squares(hd):
                def do():
                    act.wait_ge(ro_done, hd + 1)
                    for j in range(NT):
                        if j:
                            act.wait_ge(ro_sq, 4 * hd + j)
                        nc.scalar.activation(ret_junk[:], A[2 + j // 2][:, (j % 2) * RD:(j % 2 + 1) * RD], ACT.Square,
                                             scale=1 / 8, accum_out=stat[:, 32 + j:33 + j]).then_inc(ro_sq, 1)
                return do

            def retention(hd, more=True):
                return {1: (stage_v(hd),), 2: (score_hi(hd, 0), score_hi(hd, 1)), 4: (score_hi(hd, 2),), 5: (score_hi(hd, 3),),
                        6: (score_hi(hd, 4), *((stage_kq(hd + 1),) if more else ())), 7: (ret_squares(hd),)}

            stage_kq(0)()
            with act.Fori(0, 2) as i:
                quad(i + 11, retention(i), gate_evac)
            quad(13, retention(2), gate_evac)

            def mix_part(f):
                def do():
                    act.wait_ge(mix_turned, f + 1)
                    nc.scalar.activation(xt_hi[:, f, 0:SEQ], A[f % 4], ACT.Copy, scale=0.5).then_inc(mix_hi, 1)
                return do

            aux = retention(3, more=False)
            aux[7] += (mix_part(0), mix_part(1))
            quad(14, aux, gate_evac, (mix_part(2), mix_part(3)))

            def y_evac(cg):
                def evac(b):
                    nc.scalar.activation(relu[:, b], M[b], ACT.Square, scale=1 / 32,
                                         accum_out=stat[:, 4 * cg + b:4 * cg + b + 1]).then_inc(y_sq, 1)
                return evac

            quad(15, {k: (mix_part(f), mix_part(f + 1)) for k, f in MIX_AT[1:]}, y_evac(0))

            def h_squares(t):
                act.wait_ge(h_done, t + 1)
                if t:
                    act.wait_ge(h_sq, t)
                nc.scalar.activation(junk[:], h[:, t, :], ACT.Square, scale=1 / 32,
                                     accum_out=stat[:, 16 + t:17 + t]).then_inc(h_sq, 1)

            def y_and_h(b):
                y_evac(1)(b)
                if 0 < b < 3:
                    h_squares(b - 1)

            def turned_hi(n, f, first, cols):
                act.wait_ge(f_turned, n + 1)
                nc.scalar.activation(xt_hi[:, f, first:first + cols], A[f % 4][:, 0:cols], ACT.Copy,
                                     scale=col_ffn[:, f:f + 1]).then_inc(ft_hi, 1)

            quad(16, None, y_and_h, staggered=True)
            for f in range(4):
                turned_hi(f, f, 0, 2 * P)

            def turned_half():
                h_squares(2)
                h_squares(3)
                for f in range(4):
                    turned_hi(4 + f, f, 2 * P, 2 * P)

            def up_evac(i, half):
                def evac(b):
                    nc.scalar.activation(relu[:, b, :], M[b], ACT.Relu).then_inc(bank_free[b], 1)
                    if b == 3:
                        for n in range(4):
                            act.wait_ge(bank_free[n], i + (17 + 6 * half) + 1)
                            nc.scalar.activation(u_hi[:, ds(4 * i + n, 1), :].squeeze(1), relu[:, n, :],
                                                 ACT.Square).then_inc(sq_hi_ready, 1)
                return evac

            def out_squares(cg):
                def evac(b):
                    if cg:
                        act.wait_ge(y_done, b + 1)
                    else:
                        act.wait_ge(bank_free[b], 17 + 6 + 5)
                    nc.scalar.activation(relu[:, b], y[:, b, cg * COLS:(cg + 1) * COLS], ACT.Square, scale=1 / 32,
                                         accum_out=stat[:, 4 * cg + b:4 * cg + b + 1]).then_inc(o_sq, 1)
                return evac

            for half in range(2):
                q0 = 17 + 8 * half
                if half == 0:
                    quad(17, {0: (turned_half,), **{k: (lambda f=k + 3: turned_hi(4 + f, f, 0, SEQ),) for k in range(1, 5)}},
                         up_evac(0, 0))
                with act.Fori(1 - half, 4) as i:
                    quad(i + q0, None, up_evac(i, half))
                for r in range(4):
                    quad(q0 + 4 + r, None, out_squares(r // 2) if half == 1 and r % 2 else None, staggered=q0 + 5 + r == QUADS)
        @block.vector
        def _(dve):
            def split(q, k):
                if k >= KT:
                    q, k = q + 1, k - KT
                dve.wait_ge(hi_ready, 8 * q + k + 1)
                nc.vector.tensor_tensor(w_lo[:, k % W_SLOTS, :], raw[:, k // 2, k % 2, :], f32(w_hi[:, k % W_SLOTS, :]),
                                        ALU.subtract).then_inc(lo_ready, 1)

            def quad(q, aux=None, evac=None, after=None, staggered=False):
                for k in range(KT):
                    if not (staggered and k + 3 >= KT):
                        split(q, k + 3)
                    for do in (aux or {}).get(k, ()):
                        do()
                for b in range(4 if evac else 0):
                    dve.wait_ge(mm_done, 4 * (8 * q + 4 + b + 1) if staggered else 4 * (8 * q + 7) + b + 1)
                    evac(b)
                for do in after or ():
                    do()

            def sub_hi(lo, hi, src, scale):
                return nc.vector.scalar_tensor_tensor(out=lo, in0=src, scalar=scale, in1=f32(hi), op0=ALU.mult, op1=ALU.subtract)

            dve.wait_ge(rstd_ready, 1)
            nc.vector.tensor_scalar(meta_in[:], meta_in[:], stat[0:META, 5:6], None, ALU.mult).then_inc(normed, 1)
            for t in range(NT):
                dve.wait_ge(rstd_ready, t + 2)
                nc.vector.tensor_scalar(x_in[:, t, :], x_in[:, t, :], stat[:, 8 + t:9 + t], None, ALU.mult).then_inc(normed, 1)
                if t == 0:
                    dve.wait_ge(turned, 1)
                    dve.wait_ge(const_landed, 16 * 2)
                    nc.vector.tensor_tensor(m_scaled, A[3][:, 0:KT * META].rearrange("p (k n) -> p k n", k=KT),
                                            col_pre[:].unsqueeze(2).to_broadcast([P, KT, META]), ALU.mult).then_inc(meta_scaled, 1)
            def meta_lo(lo):
                nc.vector.tensor_tensor(lo, m_scaled, f32(xt_hi[:, :, SEQ:TOK]), ALU.subtract)

            split(0, 0)
            dve.wait_ge(xt_hi_ready, 1)
            meta_lo(xt_lo[:, :, SEQ:TOK])
            for f in range(KT):
                dve.wait_ge(xt_hi_ready, f + 2)
                sub_hi(xt_lo[:, f, 0:SEQ], xt_hi[:, f, 0:SEQ], ps[:, f, :], col_pre[:, f:f + 1]).then_inc(xt_lo_ready, 1)
                if f in (4, 6):
                    split(0, f // 2 - 1)
            meta_lo(xt_hi[:, :, SEQ + M_LO:SEQ + M_BOTH])

            def make_fold():
                dve.wait_ge(masks_ready, 1)
                nc.vector.tensor_tensor(fold[0:M_BOTH, :], ident[0:M_BOTH, 0:META], ident[0:M_BOTH, M_LO:M_BOTH], ALU.add)

            def kv_evac(b):
                if b < 2:
                    dve.wait_ge(kt_hi_done, 2 + b + 1)
                    own, prev, _ = kt_views(kt_lo, b)
                    own_hi, prev_hi, _ = kt_views(kt_hi, b)
                    nc.vector.tensor_tensor(own, M[b].rearrange("p (t n) -> p t n", t=NT), f32(own_hi), ALU.subtract)
                    nc.vector.tensor_tensor(prev, M[b][:, CHUNK:CHUNK + 3 * P].rearrange("p (t n) -> p t n", t=3)[:, :, 0:CHUNK],
                                            f32(prev_hi), ALU.subtract).then_inc(bank_free[b], 1)
                if b >= 2:
                    dve.wait_ge(v_done, b - 1)
                if b == 2:
                    nc.vector.tensor_copy(v_second[0:CHUNK, 0, :], M[2][0:CHUNK, 256:512])
                if b == 3:
                    nc.vector.tensor_copy(v_second[0:CHUNK, 1, :], M[3][0:CHUNK, 0:256])
                    nc.vector.tensor_copy(v_second[0:CHUNK, 2, :], M[3][0:CHUNK, 256:512])
                    nc.vector.tensor_copy(v_second[0:CHUNK, 3, :], A[0][0:CHUNK, 0:256]).then_inc(bank_free[2], 1)
                    nc.vector.tensor_copy(v_second[CHUNK:CHUNK + META, :, :], A[0][CHUNK:CHUNK + META, 0:256].unsqueeze(1)
                                          .to_broadcast([META, NT, 256])).then_inc(bank_free[3], 1)

            def meta_keys():
                dve.wait_ge(kt_hi_done, 2)
                for f in range(2):
                    nc.vector.tensor_tensor(kt_views(kt_lo, f)[2], A[1][:, f * META:(f + 1) * META].unsqueeze(1)
                                            .to_broadcast([P, NT, META]), f32(kt_views(kt_hi, f)[2]), ALU.subtract)

            quad(0, {6: (make_fold,), 7: (meta_keys,)}, kv_evac)
            quad(1)

            def stage_q(t, u, unit):
                rows = slice(64 * u, 64 * u + 64)

                def do():
                    dve.wait_ge(qz_hi_ready, unit + 1)
                    nc.vector.tensor_tensor(qz_lo[u][rows], qt[rows, :, ds(P * t, P)], f32(qz_hi[u][rows]), ALU.subtract).then_inc(qz_lo_ready, 1)
                return do

            def softmax_max(unit, g):
                def do():
                    dve.wait_ge(qk_done, unit + 1)
                    nc.vector.tensor_reduce(stat[:, 8:12].rearrange("p (b m) -> p b m", b=2), S4, AX_X, ALU.max).then_inc(max_ready, 1)
                    dve.wait_ge(max_ready, unit + 1)
                    nc.vector.scalar_tensor_tensor(out=stat[:, 12:16], in0=stat[:, 8:12], scalar=-ATT_SCALE,
                                                   in1=nsink[:, 4 * g:4 * g + 4], op0=ALU.mult, op1=ALU.min).then_inc(bias_ready, 1)
                    dve.wait_ge(bias_ready, unit + 1)
                    nc.vector.tensor_tensor(stat[:, 16:20], sink[:, 4 * g:4 * g + 4], stat[:, 12:16], ALU.add).then_inc(sink_ready, 1)
                return do

            def denominator(unit):
                def do():
                    dve.wait_ge(exp_done, unit + 1)
                    nc.vector.tensor_tensor(stat[:, 28:32], stat[:, 20:24], stat[:, 24:28], ALU.add).then_inc(den_ready, 1)
                    dve.wait_ge(den_ready, unit + 1)
                    nc.vector.reciprocal(stat[:, 52:56], stat[:, 28:32]).then_inc(rden_ready, 1)
                return do

            def copy_pair(unit):
                def do():
                    dve.wait_ge(p_turned, 2 * unit + 2)
                    nc.vector.tensor_copy(pt_first[:, 2:4, :], TB[:, 0:256].rearrange("p (m q) -> p m q", m=2))
                    nc.vector.tensor_copy(pt_second[0:KEYS - P, 2:4, :],
                                          TB[0:KEYS - P, 256:512].rearrange("p (m q) -> p m q", m=2)).then_inc(pt_pair1_ready, 1)
                return do

            def attention_out(t, unit, g):
                def do():
                    dve.wait_ge(pv_done, unit + 1)
                    dve.wait_ge(rden_ready, unit + 1)
                    nc.vector.tensor_tensor(o_a[:, ds(t, 1), 256 * g:256 * g + 256].squeeze(1).rearrange("p (m d) -> p m d", m=4),
                                            TB[:, 0:256].rearrange("p (m d) -> p m d", m=4),
                                            stat[:, 52:56].unsqueeze(2).to_broadcast([P, 4, HD]), ALU.mult).then_inc(att_out, 1)
                return do

            def attention(t, unit0, g0):
                a, b = unit0, unit0 + 1
                return ({0: (stage_q(t, 0, a), stage_q(t, 1, b)), 2: (softmax_max(a, g0),), 3: (denominator(a),),
                         5: (copy_pair(a), softmax_max(b, g0 + 1)), 6: (attention_out(t, a, g0),), 7: (denominator(b),)},
                        (attention_out(t, b, g0 + 1),))

            def rope_evac(i, n0, q0):
                def evac(b):
                    e = b // 2
                    if b % 2 == 0:
                        dve.wait_ge(rope_slot_free, 2 * i + n0 + e + 1)
                        nc.vector.tensor_tensor(rope_a[:, e], M[b], cos[:, 0:SEQ], ALU.mult)
                        nc.vector.tensor_tensor(rope_c[:, e], M[b], sin[:, 0:SEQ], ALU.mult).then_inc(bank_free[b], 1)
                    if b == 2 and n0 == 4:
                        dve.wait_ge(meta_folded, i + 1)
                        mt = MB[:, 0:4 * META].rearrange("p (e two n) -> p two e n", e=2, two=2)
                        cm, sm = (c[:, SEQ:TOK].unsqueeze(1).to_broadcast([P, 2, META]) for c in (cos, sin))
                        for n, (half, w) in enumerate(((0, cm), (0, sm), (1, sm), (1, cm))):
                            ins = nc.vector.tensor_tensor(rope_m[:, n], mt[:, half], w, ALU.mult)
                        ins.then_inc(meta_free, 1)
                    if b == 3:
                        for e in range(2):
                            dve.wait_ge(bank_free[2 * e + 1], i + q0 + 1)
                            nc.vector.tensor_tensor(rope_b[:, e], rope_x[:, e], sin[:, 0:SEQ], ALU.mult)
                            nc.vector.tensor_tensor(rope_x[:, e], rope_x[:, e], cos[:, 0:SEQ], ALU.mult).then_inc(rope_parts, 1)
                        if n0 == 4:
                            dve.wait_ge(meta_free, i + 1 + 1)
                            rk_m = rk[:, ds(4 * i, 4), SEQ:TOK].rearrange("p (e two) n -> p two e n", two=2)
                            nc.vector.tensor_tensor(rk_m[:, 0], rope_m[:, 0], rope_m[:, 2], ALU.subtract)
                            nc.vector.tensor_tensor(rk_m[:, 1], rope_m[:, 1], rope_m[:, 3], ALU.add)
                return evac

            with dve.Fori(0, 2) as i:
                aux, after = attention(i, 2 * i, 0)
                quad(i + 2, aux, rope_evac(i, 0, 2), after)
            with dve.Fori(0, 2) as i:
                aux, after = attention(i + 2, 2 * i + 4, 0)
                quad(i + 4, aux, rope_evac(i, 4, 4), after)
            quad(6)
            dve.wait_ge(rope_slot_free, 2 + 8)

            def v_evac(i):
                def evac(b):
                    if b % 2 == 0:
                        nc.vector.tensor_copy(v_r[:, b, ds(i * COLS, COLS)], M[b]).then_inc(bank_free[b], 1)
                    if b == 0:
                        dve.wait_ge(meta_staged, i + 2 + 1)
                        nc.vector.tensor_tensor(v_rm[:, ds(i * COLS, COLS)], MB[0:META, :], m_rows[0:META, :], ALU.add).then_inc(meta_free, 1)
                return evac

            with dve.Fori(0, 2) as i:
                aux, after = attention(i, 2 * i + 8, 2)
                quad(i + 7, aux, v_evac(i), after)

            def silu_evac(i):
                def evac(b):
                    dve.wait_ge(th_ready, 4 * i + b + 1)
                    nc.vector.scalar_tensor_tensor(out=g2[:, b, ds(i * COLS, COLS)], in0=th[:, b % 2, :], scalar=1.0, in1=M[b],
                                                   op0=ALU.add, op1=ALU.mult).then_inc(bank_free[b], 1)
                return evac

            with dve.Fori(0, 2) as i:
                aux, after = attention(i + 2, 2 * i + 12, 2)
                quad(i + 9, aux, silu_evac(i), after)

            def stage_k(hd):
                def do():
                    dve.wait_ge(hk_hi_ready, hd + 1)
                    nc.vector.tensor_tensor(hk_lo[:], rk[:, ds(2 * hd, 2), :], f32(hk_hi[:]), ALU.subtract)
                    dve.wait_ge(hq_hi_ready, hd + 1)
                    nc.vector.tensor_tensor(hq_lo[:], rq[:, ds(2 * hd, 2), :], f32(hq_hi[:]), ALU.subtract).then_inc(hq_lo_ready, 1)
                return do

            def stage_v(hd):
                def do():
                    dve.wait_ge(hv_hi_ready, hd + 1)
                    nc.vector.tensor_tensor(hv_lo[:, 0:NT, :], v_r[:, :, ds(RD * hd, RD)], f32(hv_hi[:, 0:NT, :]), ALU.subtract)
                    nc.vector.tensor_tensor(hv_lo[0:META, NT, :], v_rm[:, ds(RD * hd, RD)], f32(hv_hi[0:META, NT, :]),
                                            ALU.subtract).then_inc(hv_lo_ready, 1)
                return do

            def decay_scores(hd, n):
                rows, cols = score_shape(n)
                first = META if n == 0 else 0

                def do():
                    dve.wait_ge(rs_done, 5 * hd + n + 1)
                    nc.vector.tensor_tensor(sc[0:rows, n % 2, 0:cols], A[n % 2][0:rows, 0:cols],
                                            decay[0:rows, ds(hd, 1), first:first + cols].squeeze(1), ALU.mult).then_inc(sc_ready, 1)
                return do

            def score_lo(hd, n):
                rows, cols = score_shape(n)

                def do():
                    dve.wait_ge(sc_hi_ready, 5 * hd + n + 1)
                    nc.vector.tensor_tensor(sc_lo[0:rows, n % 2, 0:cols], sc[0:rows, n % 2, 0:cols],
                                            f32(sc_hi[0:rows, n % 2, 0:cols]), ALU.subtract).then_inc(sc_lo_ready, 1)
                return do

            def retention_out(hd):
                def do():
                    dve.wait_ge(ro_rstd, hd + 1)
                    for j in range(NT):
                        part = g2[:, j, ds(RD * hd, RD)]
                        nc.vector.scalar_tensor_tensor(out=part, in0=A[2 + j // 2][:, (j % 2) * RD:(j % 2 + 1) * RD],
                                                       scalar=stat[:, 36 + j:37 + j], in1=part, op0=ALU.mult,
                                                       op1=ALU.mult).then_inc(ro_scaled, 1)
                return do

            def retention(hd, more=True):
                return {1: (stage_v(hd),),
                        2: (decay_scores(hd, 0), decay_scores(hd, 1), score_lo(hd, 0), score_lo(hd, 1)),
                        4: (decay_scores(hd, 2), score_lo(hd, 2)), 5: (decay_scores(hd, 3), score_lo(hd, 3)),
                        6: (decay_scores(hd, 4), score_lo(hd, 4), *((stage_k(hd + 1),) if more else ()))}

            def gate_a_evac(i):
                def evac(b):
                    dve.wait_ge(bank_free[b], i + 11 + 1)
                    part = o_a[:, b, ds(i * COLS, COLS)]
                    nc.vector.scalar_tensor_tensor(out=part, in0=th_gate[b], scalar=1.0, in1=part, op0=ALU.add,
                                                   op1=ALU.mult).then_inc(gated, 1)
                return evac

            def gate_r_evac(i):
                def evac(b):
                    dve.wait_ge(bank_free[b], i + 13 + 1)
                    cols = slice(i * COLS, (i + 1) * COLS)
                    nc.vector.scalar_tensor_tensor(out=th_gate[b], in0=th_gate[b], scalar=1.0, in1=g2[:, b, cols],
                                                   op0=ALU.add, op1=ALU.mult).then_inc(r_gated, 1)
                    dve.wait_ge(r_gated, 4 * i + b + 1)
                    nc.vector.tensor_tensor(o_a[:, b, cols], o_a[:, b, cols], th_gate[b], ALU.add).then_inc(gated, 1)
                return evac

            dve.wait_ge(decay_landed, 16)
            stage_k(0)()
            with dve.Fori(0, 2) as i:
                quad(i + 11, retention(i), gate_a_evac(i), (retention_out(i),))
            quad(13, retention(2), gate_r_evac(0), (retention_out(2),))

            def mix_part(f):
                def do():
                    dve.wait_ge(mix_hi, f + 1)
                    sub_hi(xt_lo[:, f, 0:SEQ], xt_hi[:, f, 0:SEQ], A[f % 4], 0.5).then_inc(mix_lo, 1)
                return do

            last_gate = gate_r_evac(1)

            def gate_and_mix(b):
                if b == 0:
                    dve.wait_ge(ro_scaled, 4 * RH)
                last_gate(b)
                if b == 1:
                    mix_part(2)()
                    mix_part(3)()

            aux = retention(3, more=False)
            aux[7] = (mix_part(0), retention_out(3), mix_part(1))
            quad(14, aux, gate_and_mix)

            def y_evac(cg):
                def evac(b):
                    if b == cg == 0:
                        dve.wait_ge(row_post_landed, 16)
                    dve.wait_ge(y_sq, 4 * cg + b + 1)
                    cols = slice(cg * COLS, (cg + 1) * COLS)
                    nc.vector.tensor_tensor(y[:, b, cols], M[b], row_post[:, cols], ALU.mult).then_inc(bank_free[b], 1)
                return evac

            def residual(t):
                dve.wait_ge(bank_free[t], 16 + 1)
                dve.wait_ge(y_rstd, t + 1)
                nc.vector.scalar_tensor_tensor(out=h[:, t, :], in0=y[:, t, :], scalar=stat[:, 12 + t:13 + t], in1=h[:, t, :],
                                               op0=ALU.mult, op1=ALU.add).then_inc(h_done, 1)

            def norm_h(t):
                dve.wait_ge(h_rstd, t + 1)
                nc.vector.tensor_scalar(y[:, t, :], h[:, t, :], stat[:, 20 + t:21 + t], None, ALU.mult).then_inc(f_normed, 1)

            def y_and_h(b):
                y_evac(1)(b)
                if b < 2:
                    residual(b)
                if b == 1:
                    norm_h(0)
                if b == 2:
                    norm_h(1)
                    split(17, 0)

            def turned_lo(n, f, first, cols):
                dve.wait_ge(ft_hi, n + 1)
                sub_hi(xt_lo[:, f, first:first + cols], xt_hi[:, f, first:first + cols], A[f % 4][:, 0:cols],
                       col_ffn[:, f:f + 1]).then_inc(ft_lo, 1)

            quad(15, {k: (mix_part(f), mix_part(f + 1)) for k, f in MIX_AT[1:]}, y_evac(0))
            dve.wait_ge(x_back, 16)
            quad(16, None, y_and_h, staggered=True)
            for k in (1, 2):
                split(17, k)
                turned_lo(k - 1, k - 1, 0, 2 * P)
            residual(2)
            for f in (2, 3):
                turned_lo(f, f, 0, 2 * P)
            residual(3)

            def turned_half():
                norm_h(2)
                norm_h(3)
                for f in range(4):
                    turned_lo(4 + f, f, 2 * P, 2 * P)

            def up_evac(i, half):
                def evac(b):
                    dve.wait_ge(bank_free[b], i + (17 + 6 * half) + 1)
                    nc.vector.tensor_tensor(relu2[:, b % 2, :], relu[:, b, :], relu[:, b, :], ALU.mult).then_inc(sq_full, 1)
                    dve.wait_ge(sq_full, 4 * i + 16 * half + b + 1)
                    dve.wait_ge(sq_hi_ready, 4 * i + 16 * half + b + 1)
                    nc.vector.tensor_tensor(u_lo[:, ds(4 * i + b, 1), :].squeeze(1), relu2[:, b % 2, :],
                                            f32(u_hi[:, ds(4 * i + b, 1), :].squeeze(1)), ALU.subtract).then_inc(u_done, 1)
                return evac

            def down_evac(half, cg):
                def evac(b):
                    part = y[:, b, cg * COLS:(cg + 1) * COLS]
                    if half == 0:
                        nc.vector.tensor_copy(part, M[b]).then_inc(bank_free[b], 1)
                    else:
                        nc.vector.tensor_tensor(part, M[b], part, ALU.add).then_inc(y_done if cg else bank_free[b], 1)
                        if cg:
                            dve.wait_ge(y_done, b + 1)
                            nc.vector.tensor_tensor(scaled[:, b % 2, :], part, row_ffn[:, COLS:], ALU.mult).then_inc(o_scaled, 1)
                            if b:
                                block_out(b - 1)
                return evac

            def weigh_y(b):
                def do():
                    if b == 0:
                        dve.wait_ge(row_ffn_landed, 16)
                    dve.wait_ge(o_sq, b + 1)
                    nc.vector.tensor_tensor(y[:, b, 0:COLS], y[:, b, 0:COLS], row_ffn[:, 0:COLS], ALU.mult).then_inc(o_scaled, 1)
                return do

            def block_out(t):
                dve.wait_ge(o_scaled, 4 + t + 1)
                dve.wait_ge(o_rstd, t + 1)
                for c, part in enumerate((y[:, t, 0:COLS], scaled[:, t % 2, :])):
                    cols = slice(c * COLS, (c + 1) * COLS)
                    nc.vector.scalar_tensor_tensor(out=h[:, t, cols], in0=part, scalar=stat[:, 12 + t:13 + t], in1=h[:, t, cols],
                                                   op0=ALU.mult, op1=ALU.add).then_inc(o_ready, 1)

            for half in range(2):
                q0 = 17 + 8 * half
                if half == 0:
                    quad(17, {0: (turned_half,), **{k: (lambda f=k + 3: turned_lo(4 + f, f, 0, SEQ),) for k in range(1, 5)}},
                         up_evac(0, 0))
                with dve.Fori(1 - half, 4) as i:
                    quad(i + q0, None, up_evac(i, half))
                for r in range(4):
                    quad(q0 + 4 + r, {k: (weigh_y(k),) for k in range(4)} if half == 1 and r == 2 else None,
                         down_evac(half, r // 2) if r % 2 else None, staggered=q0 + 5 + r == QUADS)
            block_out(NT - 1)

        @block.tensor
        def _(pe):
            def three(out_ap, l_hi, l_lo, r_hi, r_lo, start, stop, **kw):
                nc.tensor.matmul(out_ap, l_hi, r_hi, start=start, stop=False, **kw)
                nc.tensor.matmul(out_ap, l_hi, r_lo, start=False, stop=False, **kw)
                return nc.tensor.matmul(out_ap, l_lo, r_hi, start=False, stop=stop, **kw)

            def columns(k, b):
                return (w[:, k % W_SLOTS, b * P:(b + 1) * P] for w in (w_hi, w_lo))

            def tokens(k, first, n):
                return (t[:, k, first:first + n] for t in (xt_hi, xt_lo))

            def features_step(k, b):
                return three(M[b], *columns(k, b), *tokens(k, 0, SEQ), k == 0, k == KT - 1)

            def rows_step(k, b):
                return three(M[b], *tokens(k, b * P, P), w_hi[:, k % W_SLOTS, :], w_lo[:, k % W_SLOTS, :], k == 0, k == KT - 1)

            def quad(q, step, extra=None, aux=None, before=None, grp=None, first=True, staggered=False):
                order = [(k, b) for k in range(KT) for b in range(4)]
                if staggered:
                    order[4 * W_SLOTS:] = [(k, b) for b in range(4) for k in range(KT - W_SLOTS, KT)]
                for k, b in order:
                    if b == 0:
                        pe.wait_ge(lo_ready, 8 * q + k + 1)
                        if extra and k == KT - 1:
                            extra(k).then_inc(meta_done, 1)
                    if before:
                        before(k, b)
                    if k == 0 and first and not (isinstance(q, int) and q == 0):
                        pe.wait_ge(bank_free[b], q if grp is None else grp)
                    mm = step(k, b)
                    if b < 3 or not extra or k == KT - 1:
                        mm.then_inc(mm_done, 1)
                    for do in (aux or {}).get((k, b), ()):
                        do()
                    if b == 3:
                        if extra and k < KT - 1:
                            extra(k).then_inc(mm_done, 1)
                        for do in (aux or {}).get(k, ()):
                            do()

            pe.wait_ge(const_landed, 16 * 2)
            pe.wait_ge(normed, 1)
            for f in range(KT):
                mm = nc.tensor.transpose(A[3][:, f * META:(f + 1) * META], meta_in[:, f * P:(f + 1) * P], ident[0:META, 0:META])
            mm.then_inc(turned, 1)
            for t in range(NT):
                pe.wait_ge(normed, t + 2)
                for f in range(KT):
                    if t == 0 and f == 7:
                        pe.wait_ge(meta_scaled, 1)
                    mm = nc.tensor.transpose(ps[:, f, t * P:(t + 1) * P], x_in[:, t, f * P:(f + 1) * P], ident[:])
                    if t == NT - 1 or f == KT - 1:
                        mm.then_inc(turned, 1)

            def kv_step(k, b):
                if b < 2:
                    return features_step(k, b)
                wv = [w[:, k % W_SLOTS, 256:512] for w in (w_hi, w_lo)]
                for n in range(2):
                    first, rows = ((0, P), (CHUNK, P), (CHUNK + P, P), (CHUNK + 2 * P, P))[2 * (b - 2) + n]
                    mm = three(M[b][0:rows, n * 256:(n + 1) * 256], *tokens(k, first, rows), *wv, k == 0 and n == 0,
                               k == KT - 1, skip_group_check=True)
                return mm

            def kv_extra(k):
                if k == 0:
                    pe.wait_ge(xt_lo_ready, 6)
                wv = [w[:, k % W_SLOTS, 256:512] for w in (w_hi, w_lo)]
                rows = CHUNK + META
                three(A[0][0:rows, 0:256], *tokens(k, TOK - rows, rows), *wv, k == 0, k == KT - 1)
                for f in range(2):
                    mm = three(A[1][:, f * META:(f + 1) * META], *columns(k, f), *tokens(k, SEQ, META), k == 0 and f == 0,
                               k == KT - 1, skip_group_check=True)
                return mm

            quad(0, kv_step, kv_extra, before=lambda k, b: pe.wait_ge(xt_lo_ready, max(k, b) + 1) if k == 0 or b == 0 else None)

            quad(1, features_step)

            def scores(t, unit, u, f):
                def do():
                    pe.wait_ge(qz_lo_ready, unit + 1)
                    if u == 1:
                        pe.wait_ge(exp_done, unit)
                    for m in range(4):
                        dst = S4[:, m // 2, m % 2, :]
                        nc.tensor.matmul(dst, mask_q[:], mask_k[:, ds(KEYS * t, KEYS)], start=True, stop=False)
                        mm = three(dst, qz_hi[u][:, m, :], qz_lo[u][:, m, :], kt_hi[:, f, ds(KEYS * t, KEYS)],
                                   kt_lo[:, f, ds(KEYS * t, KEYS)], False, True)
                    mm.then_inc(qk_done, 1)
                return do

            def turn_probs(unit, u, pair):
                def do():
                    if pair == 0:
                        pe.wait_ge(exp_done, unit + 1)
                        if u == 1:
                            pe.wait_ge(att_out, unit)
                    else:
                        pe.wait_ge(pt_pair0_ready, unit + 1)
                    for n in range(2):
                        m = 2 * pair + n
                        nc.tensor.transpose(TB[:, n * P:(n + 1) * P], prob[:, m, 0:P], ident[:])
                        mm = nc.tensor.transpose(TB[0:KEYS - P, 256 + n * P:256 + (n + 1) * P], prob[:, m, P:KEYS], ident[:])
                    mm.then_inc(p_turned, 1)
                return do

            def values(t, unit, g):
                def do():
                    pe.wait_ge(pt_pair1_ready, unit + 1)
                    for m in range(4):
                        dst = TB[:, m * HD:(m + 1) * HD]
                        nc.tensor.matmul(dst, pt_first[:, m, :], v_first[:, ds(t, 1), g * HD:(g + 1) * HD].squeeze(1), start=True, stop=False)
                        mm = nc.tensor.matmul(dst, pt_second[0:KEYS - P, m, :],
                                              v_second[0:KEYS - P, ds(t, 1), g * HD:(g + 1) * HD].squeeze(1), start=False, stop=True)
                    mm.then_inc(pv_done, 1)
                return do

            def attention(t, unit0, g0):
                a, b, f = unit0, unit0 + 1, g0 // 2
                return {1: (scores(t, a, 0, f),), 3: (turn_probs(a, 0, 0),), 4: (turn_probs(a, 0, 1), scores(t, b, 1, f)),
                        5: (values(t, a, g0),), 6: (turn_probs(b, 1, 0),), (7, 0): (turn_probs(b, 1, 1),),
                        7: (values(t, b, g0 + 1),)}

            def meta_rows(k, n):
                if k == 0:
                    pe.wait_ge(meta_free, n + 1)
                nc.tensor.matmul(MB[0:M_BOTH, :], xt_hi[:, k, SEQ:SEQ + M_BOTH], w_hi[:, k % W_SLOTS, :], start=k == 0, stop=False,
                                 skip_group_check=True)
                return nc.tensor.matmul(MB[0:META, :], xt_hi[:, k, SEQ:TOK], w_lo[:, k % W_SLOTS, :], start=False, stop=k == KT - 1,
                                        skip_group_check=True)

            def turn_meta(i):
                def do():
                    pe.wait_ge(meta_staged, i + 1)
                    for b in range(4):
                        mm = nc.tensor.matmul(MB[:, b * META:(b + 1) * META], m_rows[:, b * P:(b + 1) * P], fold[:], start=True, stop=True)
                    mm.then_inc(meta_folded, 1)
                return do

            with pe.Fori(0, 2) as i:
                quad(i + 2, features_step, None, attention(i, 2 * i, 0))
            with pe.Fori(0, 2) as i:
                aux = attention(i + 2, 2 * i + 4, 0)
                aux[7] += (turn_meta(i),)
                quad(i + 4, features_step, lambda k: meta_rows(k, i), aux)
            quad(6, features_step)
            with pe.Fori(0, 2) as i:
                quad(i + 7, rows_step, lambda k: meta_rows(k, i + 2), attention(i, 2 * i + 8, 2))
            with pe.Fori(0, 2) as i:
                quad(i + 9, rows_step, None, attention(i + 2, 2 * i + 12, 2))

            def ret_scores(hd, n):
                rows, cols = score_shape(n)
                k0, q0 = (SEQ, 0) if n == 0 else (P * (n - 1), P * (n - 1))

                def do():
                    if n == 0:
                        pe.wait_ge(hq_lo_ready, hd + 1)
                    for f in range(2):
                        mm = three(A[n % 2][0:rows, 0:cols], hk_hi[:, f, k0:k0 + rows], hk_lo[:, f, k0:k0 + rows],
                                   hq_hi[:, f, q0:SEQ], hq_lo[:, f, q0:SEQ], f == 0, f == 1)
                    mm.then_inc(rs_done, 1)
                return do

            def ret_values(hd, n):
                rows, cols = score_shape(n)
                tile, j0 = (NT, 0) if n == 0 else (n - 1, n - 1)

                def do():
                    if n == 0:
                        pe.wait_ge(hv_lo_ready, hd + 1)
                    pe.wait_ge(sc_lo_ready, 5 * hd + n + 1)
                    for j in range(j0, NT):
                        c0 = (j - j0) * P
                        mm = three(A[2 + j // 2][:, (j % 2) * RD:(j % 2 + 1) * RD], sc_hi[0:rows, n % 2, c0:c0 + P],
                                   sc_lo[0:rows, n % 2, c0:c0 + P], hv_hi[0:rows, tile, :], hv_lo[0:rows, tile, :],
                                   n == 0 and j % 2 == 0, n == j + 1, skip_group_check=True)
                    if n == NT:
                        mm.then_inc(ro_done, 1)
                return do

            def retention(hd):
                s, v = (lambda n: ret_scores(hd, n)), (lambda n: ret_values(hd, n))
                return {1: (s(0), s(1)), 3: (v(0), s(2)), 4: (v(1), s(3)), 5: (v(2), s(4)), 6: (v(3), v(4))}

            with pe.Fori(0, 2) as i:
                quad(i + 11, rows_step, None, retention(i))
            quad(13, rows_step, None, retention(2))

            def turn_mixed(f):
                def do():
                    if f == 2:
                        pe.wait_ge(ro_scaled, 4 * RH)
                    if f >= 4:
                        pe.wait_ge(gated, 16)
                        pe.wait_ge(mix_lo, f - 3)
                    for t in range(NT):
                        mm = nc.tensor.transpose(A[f % 4][:, t * P:(t + 1) * P], o_a[:, t, f * P:(f + 1) * P], ident[:])
                    mm.then_inc(mix_turned, 1)
                return do

            aux = retention(3)
            aux[7, 0] = (turn_mixed(0), turn_mixed(1))
            quad(14, rows_step, None, aux)
            quad(15, rows_step, None, {k: (turn_mixed(f), turn_mixed(f + 1)) for k, f in MIX_AT}, before=lambda k, b: pe.wait_ge(mix_lo, k + 1) if b == 0 else None)
            quad(16, rows_step, staggered=True)

            def down_step(r):
                def step(k, b):
                    kk = 8 * r + k
                    return three(M[b], u_hi[:, kk, b * P:(b + 1) * P], u_lo[:, kk, b * P:(b + 1) * P],
                                 w_hi[:, k % W_SLOTS, :], w_lo[:, k % W_SLOTS, :], kk == 0, kk == 15)
                return step

            def turn_rows(f, tiles):
                for n, t in enumerate(tiles):
                    mm = nc.tensor.transpose(A[f % 4][:, n * P:(n + 1) * P], y[:, t, f * P:(f + 1) * P], ident[:])
                mm.then_inc(f_turned, 1)

            def first_up():
                pe.wait_ge(f_normed, 2)
                for f in range(4):
                    turn_rows(f, (0, 1))
                for part in range(2):
                    first = 2 * P * part
                    if part:
                        pe.wait_ge(f_normed, NT)
                        for f in range(4):
                            turn_rows(f, (2, 3))
                    for k in range(4):
                        pe.wait_ge(lo_ready, 8 * 17 + k + 1)
                        pe.wait_ge(ft_lo, 4 * part + k + 1)
                        for b in range(4):
                            if k == part == 0:
                                pe.wait_ge(bank_free[b], 17)
                            mm = three(M[b][:, first:first + 2 * P], *columns(k, b), *tokens(k, first, 2 * P), k == part == 0,
                                       False, skip_group_check=True)
                            if part:
                                mm.then_inc(mm_done, 1)
                        if part:
                            turn_rows(4 + k, range(NT))
                for k in range(4, KT):
                    pe.wait_ge(lo_ready, 8 * 17 + k + 1)
                    pe.wait_ge(ft_lo, 4 + k + 1)
                    for b in range(4):
                        three(M[b], *columns(k, b), *tokens(k, 0, SEQ), False, k == KT - 1, skip_group_check=True).then_inc(mm_done, 1)

            for half in range(2):
                q0 = 17 + 8 * half
                g0 = 17 + 6 * half
                if half == 0:
                    first_up()
                with pe.Fori(1 - half, 4) as i:
                    quad(i + q0, features_step, grp=i + g0)
                for r in range(4):
                    quad(q0 + 4 + r, down_step(r % 2), grp=g0 + 4 + r // 2, first=r % 2 == 0,
                         before=(lambda k, b: pe.wait_ge(u_done, 16 * half + 16) if k == b == 0 else None) if r % 2 else None,
                         staggered=q0 + 5 + r == QUADS)


def tables():
    import numpy as np

    f = np.float32
    half = RD // 2
    pos = np.concatenate([np.arange(CHUNK, CHUNK + SEQ), np.arange(CHUNK - META, CHUNK)]).astype(f)
    inv_freq = (f(10000.0) ** (-np.arange(half, dtype=f) / f(half))).astype(f)
    ang = (pos[None, :] * inv_freq[:, None]).astype(f)
    log_gamma = np.log(f(1.0) - f(2.0) ** (f(-5.0) - np.arange(RH, dtype=f))).astype(f)
    k, q = np.arange(P)[:, None], np.arange(TOK)[None, :]
    seen = (q // CHUNK >= k // CHUNK)
    decay = np.exp(log_gamma[None, :, None] * np.abs(q - k)[:, None, :].astype(f)) * seen[:, None, :] * f(RD ** -0.5)
    mask_q = np.zeros((2, P), f)
    mask_q[0, :CHUNK] = mask_q[1, CHUNK:] = 1
    mask_k = np.zeros((2, NT, KEYS), f)
    mask_k[0, :, P:P + CHUNK] = -1e30
    mask_k[1, :, 0:CHUNK] = -1e30
    mask_k[0, 0, 0:CHUNK] = -1e30
    return {"ident": np.eye(P, dtype=f), "cos": np.cos(ang), "sin": np.sin(ang), "decay": decay.astype(f),
            "mask_q": mask_q, "mask_k": mask_k.reshape(2, NT * KEYS)}


_INS = ["x", "meta_tokens", "norm_mix_pre", "attn_sinks", "norm_mix_post", "norm_ffn_pre", "norm_ffn_post"]
_TABLES = ["ident", "cos", "sin", "decay", "mask_q", "mask_k"]


def quads(w_in, w_out, w_up, w_down):
    import numpy as np

    def cut(w, row, col):
        return w[0, row:row + D, col:col + COLS].reshape(4, 2, P, COLS).transpose(0, 2, 1, 3)

    def q_a(half):
        q = cut(w_in, 0, COLS * half)
        return q.reshape(4, P, 2, 2, 4, HD).transpose(0, 1, 2, 4, 3, 5).reshape(q.shape)

    order = [cut(w_in, 0, 1024), q_a(0)]
    order += [cut(w_in, 0, 1536 + COLS * n) for n in range(4)] + [q_a(1)]
    order += [cut(w_in, 0, 3584 + COLS * n) for n in range(8)]
    order += [cut(w_out, 0, COLS * n) for n in range(2)]
    for half in range(2):
        order += [cut(w_up, 0, DFF // 2 * half + COLS * n) for n in range(4)]
        order += [cut(w_down, DFF // 2 * half + D * r, COLS * cg) for cg in range(2) for r in range(2)]
    return np.ascontiguousarray(np.stack(order))


def kernel(**inputs):
    import numpy as np
    import concourse.bacc as bacc
    from concourse.bass_utils import run_bass_kernel_spmd as run

    nc = bacc.Bacc("TRN2", target_bir_lowering=False, num_devices=1)
    given = {n: np.ascontiguousarray(inputs[n]) for n in _INS}
    given["weights"] = quads(*(np.asarray(inputs[n]) for n in ("w_in", "w_out", "w_up", "w_down")))
    for n in ("norm_mix_pre", "norm_ffn_pre"):
        given[n] = np.ascontiguousarray(given[n].reshape(KT, P).T)
    given.update(tables())
    arrays, args = {}, []
    for name in _INS + ["weights"] + _TABLES:
        arrays[f"in_{name}"] = given[name]
        args.append(nc.dram_tensor(f"in_{name}", given[name].shape, mybir.dt.from_np(given[name].dtype), kind="ExternalInput").ap())
    args.append(nc.dram_tensor("out_0", (1, SEQ, D), F32, kind="ExternalOutput").ap())
    hybrid_block(nc, *args)
    r = run(nc, [arrays], core_ids=[0])
    return r.results[0]["out_0"]
```

```python
from contextlib import ExitStack

import concourse.bass as bass
from concourse import mybir

F32 = mybir.dt.float32
F32R = mybir.dt.float32r
ACT = mybir.ActivationFunctionType
ALU = mybir.AluOpType
AX_X = mybir.AxisListType.X
ds = bass.ds

P = 128
D = 1024
SEQ = 512
KT = D // P
NT = SEQ // P
CHUNK = 64
META = 16
TOK = SEQ + META
M_LO = 32
M_BOTH = M_LO + META
COLS = 512
DFF = 4096
HD = 64
KEYS = CHUNK + P + META
RH = 4
RD = 256
M_ROWS = 5 * META
EPS = 1e-6
ATT_SCALE = HD ** -0.5
W_SLOTS = 4
QUADS = 33
MIX_AT = ((0, 2), (2, 4), (3, 6))
H_BACK = 17


def hybrid_block(nc, x, meta_tokens, w_pre, sinks, w_post, w_ffn_pre, w_ffn_post, weights,
                 c_ident, c_cos, c_sin, c_decay, c_mask, out):
    ctx = ExitStack()
    with ctx:
        def sem(name):
            return ctx.enter_context(nc.semaphore(name))

        def keep(name, shape, dt=F32):
            return ctx.enter_context(nc.sbuf_tensor(name, shape, dt))

        raw = keep("raw", [P, 4, 2, COLS])
        w_hi = keep("w_hi", [P, W_SLOTS, COLS], F32R)
        w_lo = keep("w_lo", [P, W_SLOTS, COLS], F32R)
        xt_hi = keep("xt_hi", [P, KT, SEQ + M_BOTH], F32R)
        xt_lo = keep("xt_lo", [P, KT, SEQ], F32R)
        ident = keep("ident", [P, P])
        col_pre = keep("col_pre", [P, KT])
        col_ffn = keep("col_ffn", [P, KT])
        stat = keep("stat", [P, 64])
        neg_half = keep("neg_half", [P, 4])

        mixer = ExitStack()

        def a_buf(name, shape, dt=F32):
            return mixer.enter_context(nc.sbuf_tensor(name, shape, dt))

        o_a = a_buf("o_a", [P, NT, D])
        with ExitStack() as early:
            kx_hi = early.enter_context(nc.sbuf_tensor("kx_hi", [P, 2, NT * KEYS], F32R))
            kx_lo = early.enter_context(nc.sbuf_tensor("kx_lo", [P, 2, NT * KEYS], F32R))
        rq = a_buf("rq", [P, KT, SEQ])
        rk = a_buf("rk", [P, KT, TOK])
        with ExitStack() as early:
            kt_early = early.enter_context(nc.sbuf_tensor("kt_early", [P, 2, 2, NT * KEYS], F32R))
        g2 = a_buf("g2", [P, NT, D])
        v_r = a_buf("v_r", [P, NT, D])
        v_rm = a_buf("v_rm", [META, D])
        cos_sin = a_buf("cos_sin", [P, 2, TOK])
        cos, sin = cos_sin[:, 0, :], cos_sin[:, 1, :]
        th = cos_sin[:, :, 0:COLS]
        rope_a, rope_c, rope_b, rope_x = (v_r[:, n, :].rearrange("p (e c) -> p e c", e=2) for n in range(4))
        x_in, meta_in = g2, v_rm

        att = ExitStack()

        def t_buf(name, shape, dt=F32):
            return att.enter_context(nc.sbuf_tensor(name, shape, dt))

        kt_late = t_buf("kt_late", [P, 2, 2, NT * KEYS], F32R)
        qt = t_buf("qt", [P, 4, SEQ])
        v_first = t_buf("v_first", [P, NT, 256])
        v_own = t_buf("v_own", [P, NT, 256])
        v_meta = t_buf("v_meta", [4 * META, 4, 256])
        qs = [t_buf(f"qs{u}", [P, 2, 4, CHUNK], F32R) for u in range(2)]
        prob = t_buf("prob", [P, 4, P])
        prob_m = t_buf("prob_m", [P, 4, META])
        pt = t_buf("pt", [P, 4, P])
        pt_m = t_buf("pt_m", [4 * META, P])
        rope_m = t_buf("rope_m", [P, 4, 2, META])
        m_rows = t_buf("m_rows", [P, COLS])
        fold = t_buf("fold", [P, META])
        mask = t_buf("mask", [P, NT, P])
        sink = t_buf("sink", [P, 16])
        nsink = t_buf("nsink", [P, 16])
        att.close()

        ret = ExitStack()

        def r_buf(name, shape, dt=F32):
            return ret.enter_context(nc.sbuf_tensor(name, shape, dt))

        decay = r_buf("decay", [P, RH, SEQ + M_ROWS])
        hk_hi = r_buf("hk_hi", [P, 2, SEQ + M_ROWS], F32R)
        hk_lo = r_buf("hk_lo", [P, 2, SEQ + M_ROWS], F32R)
        hq_hi = r_buf("hq_hi", [P, 2, SEQ], F32R)
        hq_lo = r_buf("hq_lo", [P, 2, SEQ], F32R)
        hv_hi = r_buf("hv_hi", [P, NT + 1, RD], F32R)
        hv_lo = r_buf("hv_lo", [P, NT, RD], F32R)
        sc = r_buf("sc", [P, 2, SEQ])
        sc_hi = r_buf("sc_hi", [P, 2, SEQ], F32R)
        sc_lo = r_buf("sc_lo", [P, 2, SEQ], F32R)
        th_more = r_buf("th_more", [P, 2, COLS])
        ret_junk = sc[:, 1, 0:RD]
        th_gate = [th[:, 0, :], th[:, 1, :], th_more[:, 0, :], th_more[:, 1, :]]
        ret.close()
        mixer.close()

        u_hi = keep("u_hi", [P, 16, SEQ], F32R)
        u_lo = keep("u_lo", [P, 16, SEQ], F32R)
        y = keep("y", [P, NT, D])
        h = keep("h", [P, NT, D])
        row_post = keep("row_post", [P, D])
        row_ffn = keep("row_ffn", [P, D])
        relu = keep("relu", [P, 4, COLS])
        relu2 = keep("relu2", [P, 2, COLS])
        scaled = keep("scaled", [P, 2, COLS])
        junk = keep("junk", [P, D])

        ps = ctx.enter_context(nc.psum_tensor("ps", [P, 8, COLS], F32))
        M = [ps[:, b, :] for b in range(4)]
        A = [ps[:, 4 + b, :] for b in range(4)]
        S4 = ps[:, 4:6, 0:2 * KEYS].rearrange("p b (m k) -> p b m k", m=2)
        TB = A[2]
        MB = A[3]

        raw_landed = [sem(f"raw_landed{c}") for c in range(4)]
        hi_ready, lo_ready, mm_done = sem("hi_ready"), sem("lo_ready"), sem("mm_done")
        bank_free = [sem(f"bank_free{b}") for b in range(4)]
        x_landed = [sem(f"x_landed{t}") for t in range(NT)]
        meta_landed, const_landed, table_landed = sem("meta_landed"), sem("const_landed"), sem("table_landed")
        decay_landed = sem("decay_landed")
        ms_eps = sem("ms_eps")
        zeroed, nsink_ready = sem("zeroed"), sem("nsink_ready")
        sq_ready, rstd_ready, normed, turned = sem("sq_ready"), sem("rstd_ready"), sem("normed"), sem("turned")
        meta_scaled, xt_hi_ready, xt_lo_ready = sem("meta_scaled"), sem("xt_hi_ready"), sem("xt_lo_ready")
        kx_hi_done, kx_ready, v_done = sem("kx_hi_done"), sem("kx_ready"), sem("v_done")
        kt_landed = [sem("kt_early_landed"), sem("kt_late_landed")]
        rope_parts, rope_slot_free, meta_free = sem("rope_parts"), sem("rope_slot_free"), sem("meta_free")
        meta_done, meta_staged, meta_folded = sem("meta_done"), sem("meta_staged"), sem("meta_folded")
        fold_ready, vm_ready, v_meta_landed = sem("fold_ready"), sem("vm_ready"), sem("v_meta_landed")
        qs_hi_ready, qk_done = sem("qs_hi_ready"), sem("qk_done")
        masked, max_ready, bias_ready, sink_ready, exp_done = sem("masked"), sem("max_ready"), sem("bias_ready"), sem("sink_ready"), sem("exp_done")
        den_ready, rden_ready = sem("den_ready"), sem("rden_ready")
        p_turned, pt_pair0_ready, pt_pair1_ready = sem("p_turned"), sem("pt_pair0_ready"), sem("pt_pair1_ready")
        pv_done, att_out = sem("pv_done"), sem("att_out")
        hv_zeroed = sem("hv_zeroed")
        hk_hi_ready, hq_hi_ready, hv_hi_ready = sem("hk_hi_ready"), sem("hq_hi_ready"), sem("hv_hi_ready")
        hq_lo_ready, hv_lo_ready = sem("hq_lo_ready"), sem("hv_lo_ready")
        r_gated, qs_ready = sem("r_gated"), sem("qs_ready")
        rs_done, sc_ready, sc_hi_ready, sc_lo_ready = sem("rs_done"), sem("sc_ready"), sem("sc_hi_ready"), sem("sc_lo_ready")
        ro_done, ro_sq, ro_rstd, ro_scaled = sem("ro_done"), sem("ro_sq"), sem("ro_rstd"), sem("ro_scaled")
        th_ready, gated = sem("th_ready"), sem("gated")
        mix_turned, mix_hi, mix_lo = sem("mix_turned"), sem("mix_hi"), sem("mix_lo")
        y_sq, y_sum, y_rstd, h_done = sem("y_sq"), sem("y_sum"), sem("y_rstd"), sem("h_done")
        h_sq, h_rstd, f_normed, f_turned = sem("h_sq"), sem("h_rstd"), sem("f_normed"), sem("f_turned")
        ft_hi, ft_lo = sem("ft_hi"), sem("ft_lo")
        sq_hi_ready, sq_full, u_done = sem("sq_hi_ready"), sem("sq_full"), sem("u_done")
        x_back, row_post_landed, row_ffn_landed = sem("x_back"), sem("row_post_landed"), sem("row_ffn_landed")
        y_done, o_sq, o_rstd, o_scaled = sem("y_done"), sem("o_sq"), sem("o_rstd"), sem("o_scaled")
        o_ready, stored = sem("o_ready"), sem("stored")

        start_junk = [rq[:, 2 * t:2 * t + 2, :].rearrange("p a b -> p (a b)") for t in range(NT)]
        m_scaled = o_a[:, 1, 0:KT * META].rearrange("p (k n) -> p k n", k=KT)

        def kt_views(kt, f):
            v = kt[:, f, :].rearrange("p (t k) -> p t k", k=KEYS)
            return v[:, :, CHUNK:CHUNK + P], v[:, 1:NT, 0:CHUNK], v[:, :, CHUNK + P:KEYS]

        def rk_views(hd):
            k = rk[:, ds(2 * hd, 2), :]
            return k[:, :, 0:SEQ], k[:, :, SEQ:TOK].unsqueeze(2).to_broadcast([P, 2, M_ROWS // META, META])

        def by_chunk(q):
            return q.rearrange("p c m q -> p m c q")

        def q_chunks(rows, t):
            return qt[rows, :, ds(P * t, P)].rearrange("p m (c q) -> p m c q", c=2)

        def score_shape(n):
            return (M_ROWS, SEQ) if n == 0 else (P, SEQ - P * (n - 1))

        def f32(ap):
            return ap.bitcast(F32)

        x_v = x[0].rearrange("(t p) d -> t p d", p=P)
        out_v = out[0].rearrange("(t p) d -> t p d", p=P)

        block = ctx.enter_context(nc.Block())

        @block.sync
        def _(sp):
            def load(q, c):
                sp.dma_start(raw[:, c], weights[q, c] if isinstance(q, int) else weights[ds(q, 1), c].squeeze(0)).then_inc(raw_landed[c], 16)

            def reload(q, c):
                sp.wait_ge(lo_ready, 8 * (q - 1) + 2 * c + 2)
                load(q, c)

            sp.dma_start(meta_in[:], meta_tokens).then_inc(meta_landed, 16)
            for t in range(NT):
                sp.dma_start(x_in[:, t, :], x_v[t]).then_inc(x_landed[t], 16)
                if t == 0:
                    sp.dma_start(ident[:], c_ident).then_inc(const_landed, 16)
                    sp.dma_start(col_pre[:], w_pre).then_inc(const_landed, 16)
            for c in range(4):
                load(0, c)
            with sp.Fori(1, H_BACK) as q:
                for c in range(4):
                    reload(q, c)
            sp.wait_ge(mix_lo, KT)
            sp.dma_start(row_post[:], w_post[0].partition_broadcast(P)).then_inc(row_post_landed, 16)
            sp.dma_start(h[:], x[0].rearrange("(t p) d -> p t d", p=P)).then_inc(x_back, 16)
            with sp.Fori(H_BACK, QUADS) as q:
                for c in range(4):
                    reload(q, c)
            for t in range(NT):
                for c in range(2):
                    sp.wait_ge(o_ready, 2 * t + c + 1)
                    cols = slice(c * COLS, (c + 1) * COLS)
                    sp.dma_start(out_v[t][:, cols], h[:, t, cols]).then_inc(stored, 16)
            sp.wait_ge(stored, 16 * 2 * NT)

        @block.gpsimd
        def _(pool):
            nc.gpsimd.memset(f32(xt_hi[:, :, TOK:SEQ + M_LO]), 0.0).then_inc(zeroed, 1)
            nc.gpsimd.memset(neg_half[:], -0.5).then_inc(rope_slot_free, 1)
            nc.gpsimd.memset(stat[:, 62:63], 0.0).then_inc(rope_slot_free, 1)
            nc.gpsimd.memset(stat[:, 63:64], 0.0).then_inc(meta_free, 1)

            def rsqrt(dst, src, eps, done):
                rows, cols = src.shape
                nc.gpsimd.tensor_scalar(dst, src, eps, None, ALU.add).then_inc(ms_eps, 1)
                pool.wait_ge(ms_eps, done + 1)
                return nc.gpsimd.tensor_tensor(dst, dst, neg_half[0:rows, 0:cols], ALU.pow)

            pool.wait_ge(sq_ready, 1)
            rsqrt(stat[0:META, 5:6], stat[0:META, 4:5], EPS, 0).then_inc(rstd_ready, 1)
            for t in range(NT):
                pool.wait_ge(sq_ready, t + 2)
                rsqrt(stat[:, 8 + t:9 + t], stat[:, t:t + 1], EPS, 1 + t).then_inc(rstd_ready, 1)

            pool.dma_start(mask[:], c_mask).then_inc(table_landed, 16)
            pool.dma_start(sink[:], sinks).then_inc(table_landed, 16)
            pool.dma_start(col_ffn[:], w_ffn_pre).then_inc(table_landed, 16)
            pool.dma_start(cos, c_cos).then_inc(table_landed, 16)
            pool.dma_start(sin, c_sin).then_inc(table_landed, 16)
            for kx in (kx_hi, kx_lo):
                for f in range(2):
                    nc.gpsimd.memset(f32(kx[:, f, 0:CHUNK]), 0.0)
            nc.gpsimd.memset(m_rows[:], 0.0)
            nc.gpsimd.memset(v_meta[:], 0.0)
            nc.gpsimd.memset(fold[:], 0.0)
            nc.gpsimd.memset(v_first[:, 0, :], 0.0).then_inc(zeroed, 1)

            def rotate(i, dst, n0):
                for e in range(2):
                    pool.wait_ge(rope_parts, 2 * i + n0 + e + 1)
                    lo_t = dst[:, ds(4 * i + 2 * e, 1), 0:SEQ].squeeze(1)
                    hi_t = dst[:, ds(4 * i + 2 * e + 1, 1), 0:SEQ].squeeze(1)
                    nc.gpsimd.tensor_tensor(lo_t, rope_a[:, e], rope_b[:, e], ALU.subtract)
                    nc.gpsimd.tensor_tensor(hi_t, rope_c[:, e], rope_x[:, e], ALU.add).then_inc(rope_slot_free, 1)

            pool.wait_ge(zeroed, 2)
            pool.wait_ge(vm_ready, 1)
            for c in range(4):
                pool.dma_start(v_meta[c * META:(c + 1) * META, :, c * HD:(c + 1) * HD],
                               m_rows[0:META, 0:256].rearrange("p (g d) -> p g d", g=4)).then_inc(v_meta_landed, 16)
            pool.wait_ge(kx_ready, 2)
            for f, kt in enumerate((kt_early, kt_late)):
                for part, kx in enumerate((kx_hi, kx_lo)):
                    for e in range(2):
                        for rows in (slice(0, HD), slice(HD, P)):
                            pool.dma_start(kt[rows, part, e], kx[e * HD:(e + 1) * HD, f]).then_inc(kt_landed[f], 16)
            for f in range(2):
                pool.wait_ge(kt_landed[f], 16 * 8)
            with pool.Fori(0, 2) as i:
                rotate(i, rq, 0)
            with pool.Fori(0, 2) as i:
                rotate(i, rk, 4)
            pool.wait_ge(qk_done, 16)
            pool.dma_start(decay[:], c_decay).then_inc(decay_landed, 16)
            pool.wait_ge(att_out, 16)
            nc.gpsimd.memset(f32(hv_hi[:, NT, :]), 0.0).then_inc(hv_zeroed, 1)
            for hd in range(RH):
                pool.wait_ge(ro_sq, 4 * hd + 4)
                rsqrt(stat[:, 36:40], stat[:, 32:36], 4 * EPS, hd + 5).then_inc(ro_rstd, 1)
            pool.wait_ge(x_back, 16)
            pool.dma_start(row_ffn[:], w_ffn_post[0].partition_broadcast(P)).then_inc(row_ffn_landed, 16)

            def add_eps(squares, done):
                pool.wait_ge(squares, NT)
                nc.gpsimd.tensor_scalar(stat[:, 0:NT], stat[:, 0:NT], EPS, None, ALU.add).then_inc(y_sum, 1)
                pool.wait_ge(y_sum, done + 1)

            def rsqrt_sum(t, squares, done):
                pool.wait_ge(squares, NT + t + 1)
                nc.gpsimd.tensor_tensor(stat[:, 12 + t:13 + t], stat[:, t:t + 1], stat[:, 4 + t:5 + t], ALU.add).then_inc(y_sum, 1)
                pool.wait_ge(y_sum, done + 1)
                return nc.gpsimd.tensor_tensor(stat[:, 12 + t:13 + t], stat[:, 12 + t:13 + t], neg_half[:, 0:1], ALU.pow)

            add_eps(y_sq, 0)
            for t in range(NT + 1):
                if t < NT:
                    rsqrt_sum(t, y_sq, 1 + t).then_inc(y_rstd, 1)
                if t > 0:
                    pool.wait_ge(h_sq, t)
                    rsqrt(stat[:, 19 + t:20 + t], stat[:, 15 + t:16 + t], EPS, 8 + t).then_inc(h_rstd, 1)
            add_eps(o_sq, 1 + NT)
            for t in range(NT):
                rsqrt_sum(t, o_sq, 2 + NT + t).then_inc(o_rstd, 1)

        @block.scalar
        def _(act):
            def split(q, k, staggered=False):
                if k >= KT:
                    q, k = q + 1, k - KT
                s = 8 * q + k
                if k % 2 == 0:
                    act.wait_ge(raw_landed[k // 2], 16 * q + 16)
                if staggered:
                    act.wait_ge(mm_done, 4 * (s - k - 1) + k + 1)
                elif not (isinstance(s, int) and s < W_SLOTS):
                    act.wait_ge(mm_done, 4 * (s - W_SLOTS + 1))
                nc.scalar.activation(w_hi[:, k % W_SLOTS, :], raw[:, k // 2, k % 2, :], ACT.Copy).then_inc(hi_ready, 1)

            def quad(q, aux=None, evac=None, after=None, staggered=False):
                for k in range(KT):
                    if not (staggered and k + 3 >= KT):
                        split(q, k + 3)
                    for do in (aux or {}).get(k, ()):
                        do()
                for b in range(4 if evac else 0):
                    if staggered and b == 3 and q + 1 < QUADS:
                        for k in range(3):
                            split(q + 1, k, staggered=True)
                    act.wait_ge(mm_done, 4 * (8 * q + 4 + b + 1) if staggered else 4 * (8 * q + 7) + b + 1)
                    evac(b)
                for do in after or ():
                    do()

            def bank_copy(banks, dst):
                def evac(b):
                    if b in banks:
                        nc.scalar.activation(dst(b), M[b], ACT.Copy).then_inc(bank_free[b], 1)
                return evac

            act.wait_ge(meta_landed, 16)
            nc.scalar.activation(o_a[0:META, 2, :], meta_in[:], ACT.Square, scale=1 / 32, accum_out=stat[0:META, 4:5]).then_inc(sq_ready, 1)
            for t in range(NT):
                act.wait_ge(x_landed[t], 16)
                nc.scalar.activation(start_junk[t], x_in[:, t, :], ACT.Square, scale=1 / 32,
                                     accum_out=stat[:, t:t + 1]).then_inc(sq_ready, 1)
            split(0, 0)
            act.wait_ge(meta_scaled, 1)
            nc.scalar.activation(xt_hi[:, :, SEQ:TOK], m_scaled, ACT.Copy).then_inc(xt_hi_ready, 1)
            for f in range(KT):
                act.wait_ge(turned, 1 + 3 + f + 1)
                nc.scalar.activation(xt_hi[:, f, 0:SEQ], ps[:, f, :], ACT.Copy,
                                     scale=col_pre[:, f:f + 1]).then_inc(xt_hi_ready, 1)
                if f in (4, 6):
                    split(0, f // 2 - 1)

            def negate_sinks():
                act.wait_ge(table_landed, 16 * 5)
                act.wait_ge(zeroed, 2)
                nc.scalar.mul(nsink[:], sink[:], -1.0).then_inc(nsink_ready, 1)

            def kv_evac(b):
                if b < 2:
                    own, prev, _ = kt_views(kx_hi, b)
                    nc.scalar.activation(own, M[b].rearrange("p (t n) -> p t n", t=NT), ACT.Copy)
                    nc.scalar.activation(prev, M[b][:, CHUNK:CHUNK + 3 * P].rearrange("p (t n) -> p t n", t=3)[:, :, 0:CHUNK],
                                         ACT.Copy).then_inc(kx_hi_done, 1)
                else:
                    t0 = 2 * (b - 2)
                    after = min(2, NT - 1 - t0)
                    nc.scalar.activation(v_first[CHUNK:P, t0:t0 + 2, :], M[b][0:CHUNK, :].rearrange("p (t n) -> p t n", t=2), ACT.Copy)
                    nc.scalar.activation(v_first[0:CHUNK, t0 + 1:t0 + 1 + after, :],
                                         M[b][CHUNK:P, 0:256 * after].rearrange("p (t n) -> p t n", t=after), ACT.Copy).then_inc(v_done, 1)

            def stage_meta(i, bank, rows, n):
                def do():
                    act.wait_ge(meta_done, i + 1)
                    nc.scalar.activation(m_rows[0:n, :], bank[rows, :], ACT.Copy).then_inc(meta_staged, 1)
                return do

            def meta_keys():
                act.wait_ge(meta_folded, 1)
                nc.scalar.activation(m_rows[0:META, 0:256], A[1][0:META, 2 * META:2 * META + 256], ACT.Copy).then_inc(vm_ready, 1)
                for f in range(2):
                    ins = nc.scalar.activation(kt_views(kx_hi, f)[2], A[1][:, f * META:(f + 1) * META].unsqueeze(1)
                                               .to_broadcast([P, NT, META]), ACT.Copy)
                ins.then_inc(kx_hi_done, 1)

            quad(0, {6: (negate_sinks,), 7: (stage_meta(0, A[0], slice(0, M_BOTH), M_BOTH),)}, kv_evac)

            def q_evac():
                return bank_copy((0, 1, 2, 3), lambda b: qt[:, b, :])

            quad(1, {0: (meta_keys,)}, q_evac())
            act.wait_ge(bank_free[3], 1 + 1)

            def stage_q(t, u):
                rows = slice(64 * u, 64 * u + 64)

                def do():
                    nc.scalar.activation(by_chunk(qs[u][rows]), q_chunks(rows, t), ACT.Copy).then_inc(qs_hi_ready, 1)
                return do

            def exps(unit):
                def do():
                    act.wait_ge(bias_ready, unit + 1)
                    for c in range(4):
                        src = prob[:, c, :] if c < 2 else S4[:, 1, c % 2, CHUNK:CHUNK + P]
                        nc.scalar.activation(prob[:, c, :], src, ACT.Exp, bias=stat[:, 12 + c:13 + c],
                                             scale=ATT_SCALE, accum_out=stat[:, 20 + c:21 + c])
                        nc.scalar.activation(prob_m[:, c, :], S4[:, c // 2, c % 2, CHUNK + P:KEYS], ACT.Exp, bias=stat[:, 12 + c:13 + c],
                                             scale=ATT_SCALE, accum_out=stat[:, 40 + c:41 + c])
                    act.wait_ge(sink_ready, unit + 1)
                    nc.scalar.activation(stat[:, 24:28], stat[:, 16:20], ACT.Exp).then_inc(exp_done, 1)
                return do

            def copy_pair(unit, pair, done):
                def do():
                    act.wait_ge(p_turned, 2 * unit + pair + 1)
                    if pair == 0:
                        nc.scalar.activation(pt_m[:], TB[0:4 * META, 256:256 + P], ACT.Copy)
                    nc.scalar.activation(pt[:, 2 * pair:2 * pair + 2, :], TB[:, 0:256].rearrange("p (m q) -> p m q", m=2),
                                         ACT.Copy).then_inc(done, 1)
                return do

            def attention(t, unit0):
                return {0: (stage_q(t, 0), stage_q(t, 1)), 2: (exps(unit0),), 4: (copy_pair(unit0, 0, pt_pair0_ready),),
                        5: (exps(unit0 + 1),),
                        7: (copy_pair(unit0 + 1, 0, pt_pair0_ready), copy_pair(unit0 + 1, 1, pt_pair1_ready))}

            def rope_evac(i, n0):
                def evac(b):
                    if b % 2:
                        act.wait_ge(rope_slot_free, 2 * i + n0 + b // 2 + 1)
                        nc.scalar.activation(rope_x[:, b // 2], M[b], ACT.Copy).then_inc(bank_free[b], 1)
                return evac

            with act.Fori(0, 2) as i:
                aux = attention(i, 2 * i)
                quad(i + 2, aux, rope_evac(i, 0))
            with act.Fori(0, 2) as i:
                aux = attention(i + 2, 2 * i + 4)
                aux[7] += (stage_meta(i + 1, MB, slice(0, M_BOTH), M_BOTH),)
                quad(i + 4, aux, rope_evac(i, 4))
            quad(6, evac=q_evac())
            act.wait_ge(bank_free[3], 6 + 1)

            with act.Fori(0, 2) as i:
                aux = attention(i, 2 * i + 8)
                aux[7] += (stage_meta(i + 3, MB, slice(M_LO, M_BOTH), META),)
                quad(i + 7, aux, bank_copy((1, 3), lambda b: v_r[:, b, ds(i * COLS, COLS)]))

            def tanh_evac(i):
                def evac(b):
                    if b >= 2:
                        act.wait_ge(bank_free[b - 2], i + 9 + 1)
                    nc.scalar.activation(th[:, b % 2, :], M[b], ACT.Tanh, scale=0.5).then_inc(th_ready, 1)
                return evac

            def gate_evac(b):
                nc.scalar.activation(th_gate[b], M[b], ACT.Tanh, scale=0.5).then_inc(bank_free[b], 1)

            with act.Fori(0, 2) as i:
                aux = attention(i + 2, 2 * i + 12)
                quad(i + 9, aux, tanh_evac(i))

            act.wait_ge(rope_slot_free, 2 + 8)

            def stage_kq(hd):
                def do():
                    keys, metas = rk_views(hd)
                    nc.scalar.activation(hk_hi[:, :, 0:SEQ], keys, ACT.Copy)
                    nc.scalar.activation(hk_hi[:, :, SEQ:].rearrange("p f (c n) -> p f c n", n=META), metas, ACT.Copy).then_inc(hk_hi_ready, 1)
                    nc.scalar.activation(hq_hi[:], rq[:, ds(2 * hd, 2), :], ACT.Copy).then_inc(hq_hi_ready, 1)
                return do

            def stage_v(hd):
                def do():
                    nc.scalar.activation(hv_hi[:, 0:NT, :], v_r[:, :, ds(RD * hd, RD)], ACT.Copy)
                    act.wait_ge(hv_zeroed, 1)
                    for row in (M_LO, 0):
                        ins = nc.scalar.activation(hv_hi[row:row + META, NT, :], v_rm[:, ds(RD * hd, RD)], ACT.Copy)
                    ins.then_inc(hv_hi_ready, 1)
                return do

            def score_hi(hd, n):
                rows, cols = score_shape(n)

                def do():
                    act.wait_ge(sc_ready, 5 * hd + n + 1)
                    nc.scalar.activation(sc_hi[0:rows, n % 2, 0:cols], sc[0:rows, n % 2, 0:cols], ACT.Copy).then_inc(sc_hi_ready, 1)
                return do

            def ret_squares(hd):
                def do():
                    act.wait_ge(ro_done, hd + 1)
                    for j in range(NT):
                        if j:
                            act.wait_ge(ro_sq, 4 * hd + j)
                        nc.scalar.activation(ret_junk, A[2 + j // 2][:, (j % 2) * RD:(j % 2 + 1) * RD], ACT.Square,
                                             scale=1 / 8, accum_out=stat[:, 32 + j:33 + j]).then_inc(ro_sq, 1)
                return do

            def retention(hd, more=True):
                return {1: (stage_v(hd),), 2: (score_hi(hd, 0), score_hi(hd, 1)), 4: (score_hi(hd, 2),), 5: (score_hi(hd, 3),),
                        6: (score_hi(hd, 4), *((stage_kq(hd + 1),) if more else ())), 7: (ret_squares(hd),)}

            stage_kq(0)()
            with act.Fori(0, 2) as i:
                quad(i + 11, retention(i), gate_evac)
            quad(13, retention(2), gate_evac)

            def mix_part(f):
                def do():
                    act.wait_ge(mix_turned, f + 1)
                    nc.scalar.activation(xt_hi[:, f, 0:SEQ], A[f % 4], ACT.Copy, scale=0.5).then_inc(mix_hi, 1)
                return do

            aux = retention(3, more=False)
            aux[7] += (mix_part(0), mix_part(1))
            quad(14, aux, gate_evac, (mix_part(2), mix_part(3)))

            def y_evac(cg):
                def evac(b):
                    nc.scalar.activation(relu[:, b], M[b], ACT.Square, scale=1 / 32,
                                         accum_out=stat[:, 4 * cg + b:4 * cg + b + 1]).then_inc(y_sq, 1)
                return evac

            quad(15, {k: (mix_part(f), mix_part(f + 1)) for k, f in MIX_AT[1:]}, y_evac(0))

            def h_squares(t):
                act.wait_ge(h_done, t + 1)
                if t:
                    act.wait_ge(h_sq, t)
                nc.scalar.activation(junk[:], h[:, t, :], ACT.Square, scale=1 / 32,
                                     accum_out=stat[:, 16 + t:17 + t]).then_inc(h_sq, 1)

            def turned_hi(n, f, first, cols):
                act.wait_ge(f_turned, n + 1)
                nc.scalar.activation(xt_hi[:, f, first:first + cols], A[f % 4][:, 0:cols], ACT.Copy,
                                     scale=col_ffn[:, f:f + 1]).then_inc(ft_hi, 1)

            def y_and_h(b):
                if b == 3:
                    turned_hi(0, 0, 0, 2 * P)
                y_evac(1)(b)
                if 0 < b < 3:
                    h_squares(b - 1)

            quad(16, None, y_and_h, staggered=True)
            for f in range(1, 4):
                turned_hi(f, f, 0, 2 * P)
            h_squares(2)

            def turned_half():
                h_squares(3)
                for f in range(4):
                    turned_hi(4 + f, f, 2 * P, 2 * P)

            def up_evac(i, half):
                def evac(b):
                    nc.scalar.activation(relu[:, b, :], M[b], ACT.Relu).then_inc(bank_free[b], 1)
                    if b == 3:
                        for n in range(4):
                            act.wait_ge(bank_free[n], i + (17 + 6 * half) + 1)
                            nc.scalar.activation(u_hi[:, ds(4 * i + n, 1), :].squeeze(1), relu[:, n, :],
                                                 ACT.Square).then_inc(sq_hi_ready, 1)
                return evac

            def out_squares(cg):
                def evac(b):
                    if cg:
                        act.wait_ge(y_done, b + 1)
                    else:
                        act.wait_ge(bank_free[b], 17 + 6 + 5)
                    nc.scalar.activation(relu[:, b], y[:, b, cg * COLS:(cg + 1) * COLS], ACT.Square, scale=1 / 32,
                                         accum_out=stat[:, 4 * cg + b:4 * cg + b + 1]).then_inc(o_sq, 1)
                return evac

            for half in range(2):
                q0 = 17 + 8 * half
                if half == 0:
                    quad(17, {0: (turned_half,), **{k: (lambda f=k + 3: turned_hi(4 + f, f, 0, SEQ),) for k in range(1, 5)}},
                         up_evac(0, 0))
                with act.Fori(1 - half, 4) as i:
                    quad(i + q0, None, up_evac(i, half))
                for r in range(4):
                    quad(q0 + 4 + r, None, out_squares(r // 2) if half == 1 and r % 2 else None, staggered=q0 + 5 + r == QUADS)
        @block.vector
        def _(dve):
            def split(q, k):
                if k >= KT:
                    q, k = q + 1, k - KT
                dve.wait_ge(hi_ready, 8 * q + k + 1)
                nc.vector.tensor_tensor(w_lo[:, k % W_SLOTS, :], raw[:, k // 2, k % 2, :], f32(w_hi[:, k % W_SLOTS, :]),
                                        ALU.subtract).then_inc(lo_ready, 1)

            def quad(q, aux=None, evac=None, after=None, staggered=False):
                for k in range(KT):
                    if not (staggered and k + 3 >= KT):
                        split(q, k + 3)
                    for do in (aux or {}).get(k, ()):
                        do()
                for b in range(4 if evac else 0):
                    dve.wait_ge(mm_done, 4 * (8 * q + 4 + b + 1) if staggered else 4 * (8 * q + 7) + b + 1)
                    evac(b)
                for do in after or ():
                    do()

            def sub_hi(lo, hi, src, scale):
                return nc.vector.scalar_tensor_tensor(out=lo, in0=src, scalar=scale, in1=f32(hi), op0=ALU.mult, op1=ALU.subtract)

            dve.wait_ge(rstd_ready, 1)
            nc.vector.tensor_scalar(meta_in[:], meta_in[:], stat[0:META, 5:6], None, ALU.mult).then_inc(normed, 1)
            for t in range(NT):
                dve.wait_ge(rstd_ready, t + 2)
                nc.vector.tensor_scalar(x_in[:, t, :], x_in[:, t, :], stat[:, 8 + t:9 + t], None, ALU.mult).then_inc(normed, 1)
                if t == 0:
                    dve.wait_ge(turned, 1)
                    dve.wait_ge(const_landed, 16 * 2)
                    nc.vector.tensor_tensor(m_scaled, A[3][:, 0:KT * META].rearrange("p (k n) -> p k n", k=KT),
                                            col_pre[:].unsqueeze(2).to_broadcast([P, KT, META]), ALU.mult).then_inc(meta_scaled, 1)
            split(0, 0)
            dve.wait_ge(xt_hi_ready, 1)
            dve.wait_ge(zeroed, 1)
            nc.vector.tensor_tensor(xt_hi[:, :, SEQ + M_LO:SEQ + M_BOTH], m_scaled, f32(xt_hi[:, :, SEQ:TOK]), ALU.subtract)
            for f in range(KT):
                dve.wait_ge(xt_hi_ready, f + 2)
                sub_hi(xt_lo[:, f, 0:SEQ], xt_hi[:, f, 0:SEQ], ps[:, f, :], col_pre[:, f:f + 1]).then_inc(xt_lo_ready, 1)
                if f in (4, 6):
                    split(0, f // 2 - 1)

            def make_fold():
                dve.wait_ge(nsink_ready, 1)
                nc.vector.tensor_tensor(fold[0:M_BOTH, :], ident[0:M_BOTH, 0:META], ident[0:M_BOTH, M_LO:M_BOTH],
                                        ALU.add).then_inc(fold_ready, 1)

            def kv_evac(b):
                if b < 2:
                    dve.wait_ge(kx_hi_done, b + 1)
                    own, prev, _ = kt_views(kx_lo, b)
                    own_hi, prev_hi, _ = kt_views(kx_hi, b)
                    nc.vector.tensor_tensor(own, M[b].rearrange("p (t n) -> p t n", t=NT), f32(own_hi), ALU.subtract)
                    nc.vector.tensor_tensor(prev, M[b][:, CHUNK:CHUNK + 3 * P].rearrange("p (t n) -> p t n", t=3)[:, :, 0:CHUNK],
                                            f32(prev_hi), ALU.subtract).then_inc(bank_free[b], 1)
                if b >= 2:
                    dve.wait_ge(v_done, b - 1)
                    nc.vector.tensor_copy(v_own[:, 2 * (b - 2):2 * (b - 1), :],
                                          M[b].rearrange("p (t n) -> p t n", t=2)).then_inc(bank_free[b], 1)

            def meta_keys():
                dve.wait_ge(kx_hi_done, 3)
                for f in range(2):
                    nc.vector.tensor_tensor(kt_views(kx_lo, f)[2], A[1][:, f * META:(f + 1) * META].unsqueeze(1)
                                            .to_broadcast([P, NT, META]), f32(kt_views(kx_hi, f)[2]), ALU.subtract).then_inc(kx_ready, 1)

            quad(0, {6: (make_fold,)}, kv_evac)
            quad(1, {1: (meta_keys,)})

            def stage_q(t, u, unit):
                rows = slice(64 * u, 64 * u + 64)

                def do():
                    dve.wait_ge(qs_hi_ready, unit + 1)
                    other = slice(64 - 64 * u, 128 - 64 * u)
                    nc.vector.tensor_tensor(by_chunk(qs[u][other]), q_chunks(rows, t), f32(by_chunk(qs[u][rows])),
                                            ALU.subtract).then_inc(qs_ready, 1)
                return do

            def softmax_max(t, unit, g):
                def do():
                    dve.wait_ge(qk_done, unit + 1)
                    nc.vector.tensor_tensor(prob[:, 0:2, :], S4[:, 0, :, 0:P], mask[:, ds(t, 1), :].to_broadcast([P, 2, P]),
                                            ALU.add).then_inc(masked, 1)
                    nc.vector.tensor_reduce(stat[:, 10:12], S4[:, 1, :, CHUNK:KEYS], AX_X, ALU.max)
                    nc.vector.tensor_reduce(stat[:, 44:46], S4[:, 0, :, CHUNK + P:KEYS], AX_X, ALU.max)
                    dve.wait_ge(masked, unit + 1)
                    nc.vector.tensor_reduce(stat[:, 8:10], prob[:, 0:2, :], AX_X, ALU.max).then_inc(max_ready, 1)
                    dve.wait_ge(max_ready, 2 * unit + 1)
                    nc.vector.tensor_tensor(stat[:, 8:10], stat[:, 8:10], stat[:, 44:46], ALU.max).then_inc(max_ready, 1)
                    dve.wait_ge(max_ready, 2 * unit + 2)
                    nc.vector.scalar_tensor_tensor(out=stat[:, 12:16], in0=stat[:, 8:12], scalar=-ATT_SCALE,
                                                   in1=nsink[:, 4 * g:4 * g + 4], op0=ALU.mult, op1=ALU.min).then_inc(bias_ready, 1)
                    dve.wait_ge(bias_ready, unit + 1)
                    nc.vector.tensor_tensor(stat[:, 16:20], sink[:, 4 * g:4 * g + 4], stat[:, 12:16], ALU.add).then_inc(sink_ready, 1)
                return do

            def denominator(unit):
                def do():
                    dve.wait_ge(exp_done, unit + 1)
                    nc.vector.tensor_tensor(stat[:, 28:32], stat[:, 20:24], stat[:, 24:28], ALU.add).then_inc(den_ready, 1)
                    dve.wait_ge(den_ready, 2 * unit + 1)
                    nc.vector.tensor_tensor(stat[:, 28:32], stat[:, 28:32], stat[:, 40:44], ALU.add).then_inc(den_ready, 1)
                    dve.wait_ge(den_ready, 2 * unit + 2)
                    nc.vector.reciprocal(stat[:, 52:56], stat[:, 28:32]).then_inc(rden_ready, 1)
                return do

            def copy_pair(unit):
                def do():
                    dve.wait_ge(p_turned, 2 * unit + 2)
                    nc.vector.tensor_copy(pt[:, 2:4, :], TB[:, 0:256].rearrange("p (m q) -> p m q", m=2)).then_inc(pt_pair1_ready, 1)
                return do

            def attention_out(t, unit, g):
                def do():
                    dve.wait_ge(pv_done, unit + 1)
                    dve.wait_ge(rden_ready, unit + 1)
                    for c in range(2):
                        for e in range(2):
                            rows, toks = slice(e * CHUNK, (e + 1) * CHUNK), slice(c * CHUNK, (c + 1) * CHUNK)
                            dst = o_a[toks, ds(t, 1), 256 * g:256 * g + 256].squeeze(1).rearrange("p (h e d) -> p h e d", h=2, e=2)
                            ins = nc.vector.tensor_tensor(
                                dst[:, :, e, :], TB[rows, 2 * c * HD:2 * (c + 1) * HD].rearrange("p (h d) -> p h d", h=2),
                                stat[rows, 52 + 2 * c:54 + 2 * c].unsqueeze(2).to_broadcast([CHUNK, 2, HD]), ALU.mult)
                    ins.then_inc(att_out, 1)
                return do

            def attention(t, unit0, g0):
                a, b = unit0, unit0 + 1
                return ({0: (stage_q(t, 0, a), stage_q(t, 1, b)), 2: (softmax_max(t, a, g0),), 3: (denominator(a),),
                         5: (copy_pair(a), softmax_max(t, b, g0 + 1), attention_out(t, a, g0)), 7: (denominator(b),)},
                        (attention_out(t, b, g0 + 1),))

            def rope_evac(i, n0, q0):
                def evac(b):
                    e = b // 2
                    if b % 2 == 0:
                        dve.wait_ge(rope_slot_free, 2 * i + n0 + e + 1)
                        nc.vector.tensor_tensor(rope_a[:, e], M[b], cos[:, 0:SEQ], ALU.mult)
                        nc.vector.tensor_tensor(rope_c[:, e], M[b], sin[:, 0:SEQ], ALU.mult).then_inc(bank_free[b], 1)
                    if b == 2 and n0 == 4:
                        dve.wait_ge(meta_folded, i + 1 + 1)
                        mt = MB[:, 0:4 * META].rearrange("p (e two n) -> p two e n", e=2, two=2)
                        cm, sm = (c[:, SEQ:TOK].unsqueeze(1).to_broadcast([P, 2, META]) for c in (cos, sin))
                        for n, (half, w) in enumerate(((0, cm), (0, sm), (1, sm), (1, cm))):
                            ins = nc.vector.tensor_tensor(rope_m[:, n], mt[:, half], w, ALU.mult)
                        ins.then_inc(meta_free, 1)
                    if b == 3:
                        for e in range(2):
                            dve.wait_ge(bank_free[2 * e + 1], i + q0 + 1)
                            nc.vector.tensor_tensor(rope_b[:, e], rope_x[:, e], sin[:, 0:SEQ], ALU.mult)
                            nc.vector.tensor_tensor(rope_x[:, e], rope_x[:, e], cos[:, 0:SEQ], ALU.mult).then_inc(rope_parts, 1)
                        if n0 == 4:
                            dve.wait_ge(meta_free, i + 1 + 1)
                            rk_m = rk[:, ds(4 * i, 4), SEQ:TOK].rearrange("p (e two) n -> p two e n", two=2)
                            nc.vector.tensor_tensor(rk_m[:, 0], rope_m[:, 0], rope_m[:, 2], ALU.subtract)
                            nc.vector.tensor_tensor(rk_m[:, 1], rope_m[:, 1], rope_m[:, 3], ALU.add)
                return evac

            with dve.Fori(0, 2) as i:
                aux, after = attention(i, 2 * i, 0)
                quad(i + 2, aux, rope_evac(i, 0, 2), after)
            with dve.Fori(0, 2) as i:
                aux, after = attention(i + 2, 2 * i + 4, 0)
                quad(i + 4, aux, rope_evac(i, 4, 4), after)
            quad(6)
            dve.wait_ge(rope_slot_free, 2 + 8)

            def v_evac(i):
                def evac(b):
                    if b % 2 == 0:
                        nc.vector.tensor_copy(v_r[:, b, ds(i * COLS, COLS)], M[b]).then_inc(bank_free[b], 1)
                    if b == 0:
                        dve.wait_ge(meta_staged, i + 3 + 1)
                        nc.vector.tensor_tensor(v_rm[:, ds(i * COLS, COLS)], MB[0:META, :], m_rows[0:META, :], ALU.add).then_inc(meta_free, 1)
                return evac

            with dve.Fori(0, 2) as i:
                aux, after = attention(i, 2 * i + 8, 2)
                quad(i + 7, aux, v_evac(i), after)

            def silu_evac(i):
                def evac(b):
                    dve.wait_ge(th_ready, 4 * i + b + 1)
                    nc.vector.scalar_tensor_tensor(out=g2[:, b, ds(i * COLS, COLS)], in0=th[:, b % 2, :], scalar=1.0, in1=M[b],
                                                   op0=ALU.add, op1=ALU.mult).then_inc(bank_free[b], 1)
                return evac

            with dve.Fori(0, 2) as i:
                aux, after = attention(i + 2, 2 * i + 12, 2)
                quad(i + 9, aux, silu_evac(i), after)

            def stage_k(hd):
                def do():
                    dve.wait_ge(hk_hi_ready, hd + 1)
                    keys, metas = rk_views(hd)
                    nc.vector.tensor_tensor(hk_lo[:, :, 0:SEQ], keys, f32(hk_hi[:, :, 0:SEQ]), ALU.subtract)
                    parts = [t[:, :, SEQ:].rearrange("p f (c n) -> p f c n", n=META) for t in (hk_lo, hk_hi)]
                    nc.vector.tensor_tensor(parts[0], metas, f32(parts[1]), ALU.subtract)
                    dve.wait_ge(hq_hi_ready, hd + 1)
                    nc.vector.tensor_tensor(hq_lo[:], rq[:, ds(2 * hd, 2), :], f32(hq_hi[:]), ALU.subtract).then_inc(hq_lo_ready, 1)
                return do

            def stage_v(hd):
                def do():
                    dve.wait_ge(hv_hi_ready, hd + 1)
                    nc.vector.tensor_tensor(hv_lo[:, 0:NT, :], v_r[:, :, ds(RD * hd, RD)], f32(hv_hi[:, 0:NT, :]), ALU.subtract)
                    nc.vector.tensor_tensor(hv_hi[2 * M_LO:M_ROWS, NT, :], v_rm[:, ds(RD * hd, RD)], f32(hv_hi[0:META, NT, :]),
                                            ALU.subtract).then_inc(hv_lo_ready, 1)
                return do

            def decay_scores(hd, n):
                rows, cols = score_shape(n)
                parts = ((0, M_LO), (M_LO, 2 * M_LO), (2 * M_LO, M_ROWS)) if n == 0 else ((0, rows),)

                def do():
                    dve.wait_ge(rs_done, 5 * hd + n + 1)
                    for r0, r1 in parts:
                        first = r0 + META if n == 0 else 0
                        ins = nc.vector.tensor_tensor(sc[r0:r1, n % 2, 0:cols], A[n % 2][r0:r1, 0:cols],
                                                      decay[r0:r1, ds(hd, 1), first:first + cols].squeeze(1), ALU.mult)
                    ins.then_inc(sc_ready, 1)
                return do

            def score_lo(hd, n):
                rows, cols = score_shape(n)

                def do():
                    dve.wait_ge(sc_hi_ready, 5 * hd + n + 1)
                    if n == 0:
                        lo = sc_hi[M_LO:2 * M_LO, 0, :]
                        nc.vector.tensor_tensor(lo, sc[M_LO:2 * M_LO, 0, :], f32(lo), ALU.subtract).then_inc(sc_lo_ready, 1)
                        return
                    nc.vector.tensor_tensor(sc_lo[0:rows, n % 2, 0:cols], sc[0:rows, n % 2, 0:cols],
                                            f32(sc_hi[0:rows, n % 2, 0:cols]), ALU.subtract).then_inc(sc_lo_ready, 1)
                return do

            def retention_out(hd):
                def do():
                    dve.wait_ge(ro_rstd, hd + 1)
                    for j in range(NT):
                        part = g2[:, j, ds(RD * hd, RD)]
                        nc.vector.scalar_tensor_tensor(out=part, in0=A[2 + j // 2][:, (j % 2) * RD:(j % 2 + 1) * RD],
                                                       scalar=stat[:, 36 + j:37 + j], in1=part, op0=ALU.mult,
                                                       op1=ALU.mult).then_inc(ro_scaled, 1)
                return do

            def retention(hd, more=True):
                return {1: (stage_v(hd),),
                        2: (decay_scores(hd, 0), decay_scores(hd, 1), score_lo(hd, 0), score_lo(hd, 1)),
                        4: (decay_scores(hd, 2), score_lo(hd, 2)), 5: (decay_scores(hd, 3), score_lo(hd, 3)),
                        6: (decay_scores(hd, 4), score_lo(hd, 4), *((stage_k(hd + 1),) if more else ()))}

            def gate_a_evac(i):
                def evac(b):
                    dve.wait_ge(bank_free[b], i + 11 + 1)
                    part = o_a[:, b, ds(i * COLS, COLS)]
                    nc.vector.scalar_tensor_tensor(out=part, in0=th_gate[b], scalar=1.0, in1=part, op0=ALU.add,
                                                   op1=ALU.mult).then_inc(gated, 1)
                return evac

            def gate_r_evac(i):
                def evac(b):
                    dve.wait_ge(bank_free[b], i + 13 + 1)
                    cols = slice(i * COLS, (i + 1) * COLS)
                    nc.vector.scalar_tensor_tensor(out=th_gate[b], in0=th_gate[b], scalar=1.0, in1=g2[:, b, cols],
                                                   op0=ALU.add, op1=ALU.mult).then_inc(r_gated, 1)
                    dve.wait_ge(r_gated, 4 * i + b + 1)
                    nc.vector.tensor_tensor(o_a[:, b, cols], o_a[:, b, cols], th_gate[b], ALU.add).then_inc(gated, 1)
                return evac

            dve.wait_ge(decay_landed, 16)
            stage_k(0)()
            with dve.Fori(0, 2) as i:
                quad(i + 11, retention(i), gate_a_evac(i), (retention_out(i),))
            quad(13, retention(2), gate_r_evac(0), (retention_out(2),))

            def mix_part(f):
                def do():
                    dve.wait_ge(mix_hi, f + 1)
                    sub_hi(xt_lo[:, f, 0:SEQ], xt_hi[:, f, 0:SEQ], A[f % 4], 0.5).then_inc(mix_lo, 1)
                return do

            last_gate = gate_r_evac(1)

            def gate_and_mix(b):
                if b == 0:
                    dve.wait_ge(ro_scaled, 4 * RH)
                last_gate(b)
                if b == 1:
                    mix_part(2)()
                    mix_part(3)()

            aux = retention(3, more=False)
            aux[7] = (mix_part(0), retention_out(3), mix_part(1))
            quad(14, aux, gate_and_mix)

            def y_evac(cg):
                def evac(b):
                    if b == cg == 0:
                        dve.wait_ge(row_post_landed, 16)
                    dve.wait_ge(y_sq, 4 * cg + b + 1)
                    cols = slice(cg * COLS, (cg + 1) * COLS)
                    nc.vector.tensor_tensor(y[:, b, cols], M[b], row_post[:, cols], ALU.mult).then_inc(bank_free[b], 1)
                return evac

            def residual(t):
                dve.wait_ge(bank_free[t], 16 + 1)
                dve.wait_ge(y_rstd, t + 1)
                nc.vector.scalar_tensor_tensor(out=h[:, t, :], in0=y[:, t, :], scalar=stat[:, 12 + t:13 + t], in1=h[:, t, :],
                                               op0=ALU.mult, op1=ALU.add).then_inc(h_done, 1)

            def norm_h(t):
                dve.wait_ge(h_rstd, t + 1)
                nc.vector.tensor_scalar(y[:, t, :], h[:, t, :], stat[:, 20 + t:21 + t], None, ALU.mult).then_inc(f_normed, 1)

            def turned_lo(n, f, first, cols):
                dve.wait_ge(ft_hi, n + 1)
                sub_hi(xt_lo[:, f, first:first + cols], xt_hi[:, f, first:first + cols], A[f % 4][:, 0:cols],
                       col_ffn[:, f:f + 1]).then_inc(ft_lo, 1)

            quad(15, {k: (mix_part(f), mix_part(f + 1)) for k, f in MIX_AT[1:]}, y_evac(0))
            dve.wait_ge(x_back, 16)
            def y_and_h(b):
                if b == 3:
                    turned_lo(0, 0, 0, 2 * P)
                y_evac(1)(b)
                if b < 3:
                    residual(b)
                if b == 1:
                    norm_h(0)
                if b == 2:
                    norm_h(1)
                    split(17, 0)

            quad(16, None, y_and_h, staggered=True)
            split(17, 1)
            turned_lo(1, 1, 0, 2 * P)
            residual(3)
            split(17, 2)
            for f in (2, 3):
                turned_lo(f, f, 0, 2 * P)
            norm_h(2)

            def turned_half():
                norm_h(3)
                for f in range(4):
                    turned_lo(4 + f, f, 2 * P, 2 * P)

            def up_evac(i, half):
                def evac(b):
                    dve.wait_ge(bank_free[b], i + (17 + 6 * half) + 1)
                    nc.vector.tensor_tensor(relu2[:, b % 2, :], relu[:, b, :], relu[:, b, :], ALU.mult).then_inc(sq_full, 1)
                    dve.wait_ge(sq_full, 4 * i + 16 * half + b + 1)
                    dve.wait_ge(sq_hi_ready, 4 * i + 16 * half + b + 1)
                    nc.vector.tensor_tensor(u_lo[:, ds(4 * i + b, 1), :].squeeze(1), relu2[:, b % 2, :],
                                            f32(u_hi[:, ds(4 * i + b, 1), :].squeeze(1)), ALU.subtract).then_inc(u_done, 1)
                return evac

            def down_evac(half, cg):
                def evac(b):
                    part = y[:, b, cg * COLS:(cg + 1) * COLS]
                    if half == 0:
                        nc.vector.tensor_copy(part, M[b]).then_inc(bank_free[b], 1)
                    else:
                        nc.vector.tensor_tensor(part, M[b], part, ALU.add).then_inc(y_done if cg else bank_free[b], 1)
                        if cg:
                            dve.wait_ge(y_done, b + 1)
                            nc.vector.tensor_tensor(scaled[:, b % 2, :], part, row_ffn[:, COLS:], ALU.mult).then_inc(o_scaled, 1)
                            if b:
                                block_out(b - 1)
                return evac

            def weigh_y(b):
                def do():
                    if b == 0:
                        dve.wait_ge(row_ffn_landed, 16)
                    dve.wait_ge(o_sq, b + 1)
                    nc.vector.tensor_tensor(y[:, b, 0:COLS], y[:, b, 0:COLS], row_ffn[:, 0:COLS], ALU.mult).then_inc(o_scaled, 1)
                return do

            def block_out(t):
                dve.wait_ge(o_scaled, 4 + t + 1)
                dve.wait_ge(o_rstd, t + 1)
                for c, part in enumerate((y[:, t, 0:COLS], scaled[:, t % 2, :])):
                    cols = slice(c * COLS, (c + 1) * COLS)
                    nc.vector.scalar_tensor_tensor(out=h[:, t, cols], in0=part, scalar=stat[:, 12 + t:13 + t], in1=h[:, t, cols],
                                                   op0=ALU.mult, op1=ALU.add).then_inc(o_ready, 1)

            for half in range(2):
                q0 = 17 + 8 * half
                if half == 0:
                    quad(17, {0: (turned_half,), **{k: (lambda f=k + 3: turned_lo(4 + f, f, 0, SEQ),) for k in range(1, 5)}},
                         up_evac(0, 0))
                with dve.Fori(1 - half, 4) as i:
                    quad(i + q0, None, up_evac(i, half))
                for r in range(4):
                    quad(q0 + 4 + r, {k: (weigh_y(k),) for k in range(4)} if half == 1 and r == 2 else None,
                         down_evac(half, r // 2) if r % 2 else None, staggered=q0 + 5 + r == QUADS)
            block_out(NT - 1)

        @block.tensor
        def _(pe):
            def three(out_ap, l_hi, l_lo, r_hi, r_lo, start, stop, **kw):
                nc.tensor.matmul(out_ap, l_hi, r_hi, start=start, stop=False, **kw)
                nc.tensor.matmul(out_ap, l_hi, r_lo, start=False, stop=False, **kw)
                return nc.tensor.matmul(out_ap, l_lo, r_hi, start=False, stop=stop, **kw)

            def columns(k, b):
                return (w[:, k % W_SLOTS, b * P:(b + 1) * P] for w in (w_hi, w_lo))

            def tokens(k, first, n):
                return (t[:, k, first:first + n] for t in (xt_hi, xt_lo))

            def features_step(k, b):
                return three(M[b], *columns(k, b), *tokens(k, 0, SEQ), k == 0, k == KT - 1)

            def rows_step(k, b):
                return three(M[b], *tokens(k, b * P, P), w_hi[:, k % W_SLOTS, :], w_lo[:, k % W_SLOTS, :], k == 0, k == KT - 1)

            def quad(q, step, extra=None, aux=None, before=None, grp=None, first=True, staggered=False):
                order = [(k, b) for k in range(KT) for b in range(4)]
                if staggered:
                    order[4 * W_SLOTS:] = [(k, b) for b in range(4) for k in range(KT - W_SLOTS, KT)]
                for k, b in order:
                    if b == 0:
                        pe.wait_ge(lo_ready, 8 * q + k + 1)
                        if extra and k == KT - 1:
                            extra(k).then_inc(meta_done, 1)
                    if before:
                        before(k, b)
                    if k == 0 and first and not (isinstance(q, int) and q == 0):
                        pe.wait_ge(bank_free[b], q if grp is None else grp)
                    mm = step(k, b)
                    if b < 3 or not extra or k == KT - 1:
                        mm.then_inc(mm_done, 1)
                    for do in (aux or {}).get((k, b), ()):
                        do()
                    if b == 3:
                        if extra and k < KT - 1:
                            extra(k).then_inc(mm_done, 1)
                        for do in (aux or {}).get(k, ()):
                            do()

            pe.wait_ge(const_landed, 16 * 2)
            pe.wait_ge(normed, 1)
            for f in range(KT):
                mm = nc.tensor.transpose(A[3][:, f * META:(f + 1) * META], meta_in[:, f * P:(f + 1) * P], ident[0:META, 0:META])
            mm.then_inc(turned, 1)
            for t in range(NT):
                pe.wait_ge(normed, t + 2)
                for f in range(KT):
                    if t == 0 and f == 7:
                        pe.wait_ge(meta_scaled, 1)
                    mm = nc.tensor.transpose(ps[:, f, t * P:(t + 1) * P], x_in[:, t, f * P:(f + 1) * P], ident[:])
                    if t == NT - 1 or f == KT - 1:
                        mm.then_inc(turned, 1)

            def kv_step(k, b):
                if b < 2:
                    return features_step(k, b)
                wv = [w[:, k % W_SLOTS, 256:512] for w in (w_hi, w_lo)]
                for n in range(2):
                    mm = three(M[b][:, n * 256:(n + 1) * 256], *tokens(k, (2 * (b - 2) + n) * P, P), *wv, k == 0 and n == 0,
                               k == KT - 1, skip_group_check=True)
                return mm

            def meta_rows(k, bank):
                nc.tensor.matmul(bank[0:M_BOTH, :], xt_hi[:, k, SEQ:SEQ + M_BOTH], w_hi[:, k % W_SLOTS, :], start=k == 0, stop=False,
                                 skip_group_check=True)
                return nc.tensor.matmul(bank[0:META, :], xt_hi[:, k, SEQ:TOK], w_lo[:, k % W_SLOTS, :], start=False, stop=k == KT - 1,
                                        skip_group_check=True)

            def kv_extra(k):
                if k == 0:
                    pe.wait_ge(xt_lo_ready, 5)
                return meta_rows(k, A[0])

            def fold_kv():
                pe.wait_ge(fold_ready, 1)
                pe.wait_ge(meta_staged, 1)
                for f in range(2):
                    nc.tensor.matmul(A[1][:, f * META:(f + 1) * META], m_rows[:, f * P:(f + 1) * P], fold[:], start=True, stop=True)
                nc.tensor.matmul(A[1][0:META, 2 * META:2 * META + 256], fold[:], m_rows[:, 256:512], start=True, stop=True).then_inc(meta_folded, 1)

            quad(0, kv_step, kv_extra, {7: (fold_kv,)},
                 before=lambda k, b: pe.wait_ge(xt_lo_ready, max(k, b) + 1) if k == 0 or b == 0 else None)

            quad(1, features_step)

            def scores(t, unit, u, f):
                kt = (kt_early, kt_late)[f]

                def do():
                    pe.wait_ge(qs_ready, unit + 1)
                    if u == 1:
                        pe.wait_ge(exp_done, unit)
                    for m in range(4):
                        dst = S4[:, m // 2, m % 2, :]
                        q = qs[u][:, m // 2, 2 * (m % 2):2 * (m % 2) + 2, :].rearrange("p h q -> p (h q)")
                        nc.tensor.matmul(dst, q, kt[:, 0, u, ds(KEYS * t, KEYS)], start=True, stop=False)
                        mm = nc.tensor.matmul(dst, q, kt[:, 1, u, ds(KEYS * t, KEYS)], start=False, stop=True)
                    mm.then_inc(qk_done, 1)
                return do

            def turn_probs(unit, u, pair):
                def do():
                    if pair == 0:
                        pe.wait_ge(exp_done, unit + 1)
                        if u == 1:
                            pe.wait_ge(att_out, unit)
                    else:
                        pe.wait_ge(pt_pair0_ready, unit + 1)
                    for n in range(2):
                        m = 2 * pair + n
                        mm = nc.tensor.transpose(TB[:, n * P:(n + 1) * P], prob[:, m, :], ident[:])
                    if pair == 0:
                        mm = nc.tensor.transpose(TB[0:4 * META, 256:256 + P], prob_m[:].rearrange("p m k -> p (m k)"), ident[:])
                    mm.then_inc(p_turned, 1)
                return do

            def values(t, unit, g):
                def do():
                    pe.wait_ge(pt_pair1_ready, unit + 1)
                    for m in range(4):
                        dst = TB[:, m * HD:(m + 1) * HD]
                        v = (v_first, v_own)[m // 2]
                        nc.tensor.matmul(dst, pt[:, m, :], v[:, ds(t, 1), g * HD:(g + 1) * HD].squeeze(1), start=m == 0, stop=False,
                                         skip_group_check=True)
                    mm = nc.tensor.matmul(TB[:, 0:256], pt_m[:], v_meta[:, g, :], start=False, stop=True, skip_group_check=True)
                    mm.then_inc(pv_done, 1)
                return do

            def attention(t, unit0, g0):
                a, b, f = unit0, unit0 + 1, g0 // 2
                return {1: (scores(t, a, 0, f),), 3: (turn_probs(a, 0, 0),), 4: (turn_probs(a, 0, 1), scores(t, b, 1, f)),
                        5: (values(t, a, g0),), 6: (turn_probs(b, 1, 0),), (7, 1): (turn_probs(b, 1, 1),),
                        7: (values(t, b, g0 + 1),)}

            def meta_extra(k, n):
                if k == 0:
                    pe.wait_ge(meta_free, n + 1)
                return meta_rows(k, MB)

            def turn_meta(i):
                def do():
                    pe.wait_ge(meta_staged, i + 1 + 1)
                    for b in range(4):
                        mm = nc.tensor.matmul(MB[:, b * META:(b + 1) * META], m_rows[:, b * P:(b + 1) * P], fold[:], start=True, stop=True)
                    mm.then_inc(meta_folded, 1)
                return do

            pe.wait_ge(v_meta_landed, 16 * 4)
            pe.wait_ge(kt_landed[0], 16 * 8)
            with pe.Fori(0, 2) as i:
                quad(i + 2, features_step, None, attention(i, 2 * i, 0))
            with pe.Fori(0, 2) as i:
                aux = attention(i + 2, 2 * i + 4, 0)
                aux[7] += (turn_meta(i),)
                quad(i + 4, features_step, lambda k: meta_extra(k, i), aux)
            quad(6, features_step)
            pe.wait_ge(kt_landed[1], 16 * 8)
            with pe.Fori(0, 2) as i:
                quad(i + 7, rows_step, lambda k: meta_extra(k, i + 2), attention(i, 2 * i + 8, 2))
            with pe.Fori(0, 2) as i:
                quad(i + 9, rows_step, None, attention(i + 2, 2 * i + 12, 2))

            def ret_scores(hd, n):
                rows, cols = score_shape(n)
                k0, q0 = (SEQ, 0) if n == 0 else (P * (n - 1), P * (n - 1))

                def do():
                    if n == 0:
                        pe.wait_ge(hq_lo_ready, hd + 1)
                    for f in range(2):
                        mm = three(A[n % 2][0:rows, 0:cols], hk_hi[:, f, k0:k0 + rows], hk_lo[:, f, k0:k0 + rows],
                                   hq_hi[:, f, q0:SEQ], hq_lo[:, f, q0:SEQ], f == 0, f == 1)
                    mm.then_inc(rs_done, 1)
                return do

            def ret_values(hd, n):
                rows, cols = score_shape(n)
                tile = j0 = n - 1

                def do():
                    if n == 0:
                        pe.wait_ge(hv_lo_ready, hd + 1)
                    pe.wait_ge(sc_lo_ready, 5 * hd + n + 1)
                    if n == 0:
                        for j in range(NT):
                            nc.tensor.matmul(A[2 + j // 2][:, (j % 2) * RD:(j % 2 + 1) * RD], sc_hi[0:M_ROWS, 0, j * P:(j + 1) * P],
                                             hv_hi[0:M_ROWS, NT, :], start=j % 2 == 0, stop=False, skip_group_check=True)
                        return
                    for j in range(j0, NT):
                        c0 = (j - j0) * P
                        mm = three(A[2 + j // 2][:, (j % 2) * RD:(j % 2 + 1) * RD], sc_hi[0:rows, n % 2, c0:c0 + P],
                                   sc_lo[0:rows, n % 2, c0:c0 + P], hv_hi[0:rows, tile, :], hv_lo[0:rows, tile, :],
                                   False, n == j + 1, skip_group_check=True)
                    if n == NT:
                        mm.then_inc(ro_done, 1)
                return do

            def retention(hd):
                s, v = (lambda n: ret_scores(hd, n)), (lambda n: ret_values(hd, n))
                return {1: (s(0), s(1)), 3: (v(0), s(2)), 4: (v(1), s(3)), 5: (v(2), s(4)), 6: (v(3), v(4))}

            with pe.Fori(0, 2) as i:
                quad(i + 11, rows_step, None, retention(i))
            quad(13, rows_step, None, retention(2))

            def turn_mixed(f):
                def do():
                    if f == 2:
                        pe.wait_ge(ro_scaled, 4 * RH)
                    if f >= 4:
                        pe.wait_ge(gated, 16)
                        pe.wait_ge(mix_lo, f - 3)
                    for t in range(NT):
                        mm = nc.tensor.transpose(A[f % 4][:, t * P:(t + 1) * P], o_a[:, t, f * P:(f + 1) * P], ident[:])
                    mm.then_inc(mix_turned, 1)
                return do

            aux = retention(3)
            aux[7, 0] = (turn_mixed(0), turn_mixed(1))
            quad(14, rows_step, None, aux)
            quad(15, rows_step, None, {k: (turn_mixed(f), turn_mixed(f + 1)) for k, f in MIX_AT},
                 before=lambda k, b: pe.wait_ge(mix_lo, k + 1) if b == 0 else None)
            quad(16, rows_step, staggered=True)

            def down_step(r):
                def step(k, b):
                    kk = 8 * r + k
                    return three(M[b], u_hi[:, kk, b * P:(b + 1) * P], u_lo[:, kk, b * P:(b + 1) * P],
                                 w_hi[:, k % W_SLOTS, :], w_lo[:, k % W_SLOTS, :], kk == 0, kk == 15)
                return step

            def turn_row(f, t, n):
                return nc.tensor.transpose(A[f % 4][:, n * P:(n + 1) * P], y[:, t, f * P:(f + 1) * P], ident[:])

            def turn_pair(t0):
                for n in range(2):
                    pe.wait_ge(f_normed, t0 + n + 1)
                    for f in range(4):
                        mm = turn_row(f, t0 + n, n)
                        if n:
                            mm.then_inc(f_turned, 1)

            def first_up():
                turn_pair(0)
                for part in range(2):
                    first = 2 * P * part
                    for k in range(4):
                        pe.wait_ge(lo_ready, 8 * 17 + k + 1)
                        pe.wait_ge(ft_lo, 4 * part + k + 1)
                        for b in range(4):
                            if k == part == 0:
                                pe.wait_ge(bank_free[b], 17)
                            mm = three(M[b][:, first:first + 2 * P], *columns(k, b), *tokens(k, first, 2 * P), k == part == 0,
                                       False, skip_group_check=True)
                            if part:
                                mm.then_inc(mm_done, 1)
                            elif k == 3 and b == 1:
                                turn_pair(2)
                        if part:
                            for t in range(NT):
                                mm = turn_row(4 + k, t, t)
                            mm.then_inc(f_turned, 1)
                for k in range(4, KT):
                    pe.wait_ge(lo_ready, 8 * 17 + k + 1)
                    pe.wait_ge(ft_lo, 4 + k + 1)
                    for b in range(4):
                        three(M[b], *columns(k, b), *tokens(k, 0, SEQ), False, k == KT - 1, skip_group_check=True).then_inc(mm_done, 1)

            for half in range(2):
                q0 = 17 + 8 * half
                g0 = 17 + 6 * half
                if half == 0:
                    first_up()
                with pe.Fori(1 - half, 4) as i:
                    quad(i + q0, features_step, grp=i + g0)
                for r in range(4):
                    quad(q0 + 4 + r, down_step(r % 2), grp=g0 + 4 + r // 2, first=r % 2 == 0,
                         before=(lambda k, b: pe.wait_ge(u_done, 16 * half + 16) if k == b == 0 else None) if r % 2 else None,
                         staggered=q0 + 5 + r == QUADS)


def tables():
    import numpy as np

    f = np.float32
    half = RD // 2
    pos = np.concatenate([np.arange(CHUNK, CHUNK + SEQ), np.arange(CHUNK - META, CHUNK)]).astype(f)
    inv_freq = (f(10000.0) ** (-np.arange(half, dtype=f) / f(half))).astype(f)
    ang = (pos[None, :] * inv_freq[:, None]).astype(f)
    log_gamma = np.log(f(1.0) - f(2.0) ** (f(-5.0) - np.arange(RH, dtype=f))).astype(f)
    k, q = np.arange(P)[:, None], np.arange(SEQ + M_ROWS)[None, :]
    seen = (q // CHUNK >= k // CHUNK)
    decay = np.exp(log_gamma[None, :, None] * np.abs(q - k)[:, None, :].astype(f)) * seen[:, None, :] * f(RD ** -0.5)
    mask = np.zeros((P, NT, P), f)
    mask[:, 0, 0:CHUNK] = -1e30
    return {"ident": np.eye(P, dtype=f), "cos": np.cos(ang), "sin": np.sin(ang), "decay": decay.astype(f),
            "mask": mask}


_INS = ["x", "meta_tokens", "norm_mix_pre", "attn_sinks", "norm_mix_post", "norm_ffn_pre", "norm_ffn_post"]
_TABLES = ["ident", "cos", "sin", "decay", "mask"]


def quads(w_in, w_out, w_up, w_down):
    import numpy as np

    def cut(w, row, col):
        return w[0, row:row + D, col:col + COLS].reshape(4, 2, P, COLS).transpose(0, 2, 1, 3)

    def q_a(half):
        q = cut(w_in, 0, COLS * half)
        return q.reshape(4, P, 2, 2, 4, HD).transpose(0, 1, 2, 4, 3, 5).reshape(q.shape)

    order = [cut(w_in, 0, 1024), q_a(0)]
    order += [cut(w_in, 0, 1536 + COLS * n) for n in range(4)] + [q_a(1)]
    order += [cut(w_in, 0, 3584 + COLS * n) for n in range(8)]
    order += [cut(w_out, 0, COLS * n) for n in range(2)]
    for half in range(2):
        order += [cut(w_up, 0, DFF // 2 * half + COLS * n) for n in range(4)]
        order += [cut(w_down, DFF // 2 * half + D * r, COLS * cg) for cg in range(2) for r in range(2)]
    return np.ascontiguousarray(np.stack(order))


def kernel(**inputs):
    import numpy as np
    import concourse.bacc as bacc
    from concourse.bass_utils import run_bass_kernel_spmd as run

    nc = bacc.Bacc("TRN2", target_bir_lowering=False, num_devices=1)
    given = {n: np.ascontiguousarray(inputs[n]) for n in _INS}
    given["weights"] = quads(*(np.asarray(inputs[n]) for n in ("w_in", "w_out", "w_up", "w_down")))
    for n in ("norm_mix_pre", "norm_ffn_pre"):
        given[n] = np.ascontiguousarray(given[n].reshape(KT, P).T)
    pairs = given["attn_sinks"].reshape(4, 1, 2, 2)
    given["attn_sinks"] = np.ascontiguousarray(np.repeat(np.broadcast_to(pairs, (4, 2, 2, 2)).reshape(16, 2).T, CHUNK, axis=0))
    given.update(tables())
    arrays, args = {}, []
    for name in _INS + ["weights"] + _TABLES:
        arrays[f"in_{name}"] = given[name]
        args.append(nc.dram_tensor(f"in_{name}", given[name].shape, mybir.dt.from_np(given[name].dtype), kind="ExternalInput").ap())
    args.append(nc.dram_tensor("out_0", (1, SEQ, D), F32, kind="ExternalOutput").ap())
    hybrid_block(nc, *args)
    r = run(nc, [arrays], core_ids=[0])
    return r.results[0]["out_0"]
```
